# Optimizing a Trainium2 kernel written in Bass

```python
import math
import jax, jax.numpy as jnp
from jax import lax
import numpy as np

D_MODEL = 2048
BATCH = 1
SEQ = 256
DEPTH = 1

BRANCH_WIDTH = 1024
N_BRANCHES = 3
BLOCK_Q = 128
NORM_EPS = 1e-6
DA_HEADS = 8
DA_HEAD_DIM = 64
DA_V_DIM = 2 * DA_HEAD_DIM
ML_HEADS = 4
ML_QK_DIM = 128
ML_V_DIM = 256
ML_CONV = 4
ML_CHUNK = 64
ML_QK_WIDTH = 2 * ML_HEADS * ML_QK_DIM
DSA_HEADS = 8
DSA_LATENT = 256
DSA_V_DIM = 128
IDX_HEADS = 16
IDX_DIM = 64
IDX_TOPK_MAX = 256

IN_SPLITS = (
    DA_HEADS * 2 * DA_HEAD_DIM,
    DA_HEADS * 2 * DA_HEAD_DIM,
    DA_HEADS * DA_V_DIM,
    BRANCH_WIDTH,
    ML_QK_WIDTH,
    ML_HEADS * ML_V_DIM,
    2 * ML_HEADS,
    BRANCH_WIDTH,
    BRANCH_WIDTH,
    DSA_HEADS * DSA_LATENT,
    DSA_LATENT,
    IDX_HEADS * IDX_DIM,
    IDX_DIM,
    IDX_HEADS,
    BRANCH_WIDTH,
    N_BRANCHES * D_MODEL,
)
N_IN = sum(IN_SPLITS)

kernel_name = "hybrid_diffattn_mlstm_dsa_gated"

def rmsnorm(x, g):
    x32 = x.astype(jnp.float32)
    y = x32 * lax.rsqrt(jnp.mean(x32 * x32, axis=-1, keepdims=True) + NORM_EPS)
    return (y * g.astype(jnp.float32)).astype(x.dtype)

def to_blocks(a, n):
    b, s = a.shape[:2]
    a = a.reshape((b, s // n, n) + a.shape[2:])
    return jnp.moveaxis(a, 1, 0)

def from_blocks(a):
    a = jnp.moveaxis(a, 0, 1)
    return a.reshape((a.shape[0], a.shape[1] * a.shape[2]) + a.shape[3:])

def diff_attention(q, k, v, lam_params, norm_g, lam_init):
    b, s, _ = q.shape
    q = q.reshape(b, s, DA_HEADS, 2, DA_HEAD_DIM)
    k = k.reshape(b, s, DA_HEADS, 2, DA_HEAD_DIM)
    v = v.reshape(b, s, DA_HEADS, DA_V_DIM)
    k1, k2 = k[:, :, :, 0], k[:, :, :, 1]
    lp = lam_params.astype(jnp.float32)
    lam = jnp.exp(jnp.sum(lp[0] * lp[1])) - jnp.exp(jnp.sum(lp[2] * lp[3])) + lam_init
    scale = DA_HEAD_DIM ** -0.5
    kpos = jnp.arange(s)

    def block(args):
        i, qb = args
        qpos = i * BLOCK_Q + jnp.arange(BLOCK_Q)
        mask = kpos[None, :] <= qpos[:, None]
        s1 = jnp.einsum('bqhd,bkhd->bhqk', qb[:, :, :, 0], k1).astype(jnp.float32) * scale
        s2 = jnp.einsum('bqhd,bkhd->bhqk', qb[:, :, :, 1], k2).astype(jnp.float32) * scale
        a = (jax.nn.softmax(jnp.where(mask, s1, -jnp.inf), axis=-1)
             - lam * jax.nn.softmax(jnp.where(mask, s2, -jnp.inf), axis=-1))
        return jnp.einsum('bhqk,bkhv->bqhv', a.astype(v.dtype), v)

    nb = s // BLOCK_Q
    o = from_blocks(lax.map(block, (jnp.arange(nb), to_blocks(q, BLOCK_Q))))
    o = rmsnorm(o, norm_g) * (1.0 - lam_init)
    return o.reshape(b, s, DA_HEADS * DA_V_DIM)

def causal_conv(x, w, bias):
    kw, s = w.shape[0], x.shape[1]
    xp = jnp.pad(x, ((0, 0), (kw - 1, 0), (0, 0)))
    y = xp[:, 0:s] * w[0]
    for j in range(1, kw):
        y = y + xp[:, j:j + s] * w[j]
    return y + bias

def mlstm_chunk(carry, xs):
    C, n, m = carry
    q, k, v, logf, ig = xs
    L = q.shape[2]
    bcum = jnp.cumsum(logf, axis=-1)
    causal = jnp.tril(jnp.ones((L, L), dtype=bool))
    dmat = jnp.where(causal, bcum[..., :, None] - bcum[..., None, :] + ig[..., None, :], -jnp.inf)
    inter = bcum + m[..., None]
    m_t = jnp.maximum(jnp.max(dmat, axis=-1), inter)
    w = jnp.exp(dmat - m_t[..., None]) * jnp.einsum('bhtd,bhsd->bhts', q, k)
    decay = jnp.exp(inter - m_t)
    num = jnp.einsum('bhts,bhsv->bhtv', w, v) + decay[..., None] * jnp.einsum('bhtd,bhdv->bhtv', q, C)
    den = jnp.sum(w, axis=-1) + decay * jnp.einsum('bhtd,bhd->bht', q, n)
    h = num / jnp.maximum(jnp.abs(den), jnp.exp(-m_t))[..., None]
    b_last = bcum[..., -1]
    g = b_last[..., None] - bcum + ig
    m_new = jnp.maximum(b_last + m, jnp.max(g, axis=-1))
    wk = jnp.exp(g - m_new[..., None])
    cd = jnp.exp(b_last + m - m_new)
    C_new = cd[..., None, None] * C + jnp.einsum('bhs,bhsd,bhsv->bhdv', wk, k, v)
    n_new = cd[..., None] * n + jnp.einsum('bhs,bhsd->bhd', wk, k)
    return (C_new, n_new, m_new), h

def mlstm(qk, v, gif, o, conv_w, conv_b, gate_b, norm_g):
    b, s, _ = v.shape
    out_dtype = v.dtype
    nc = s // ML_CHUNK
    qk = jax.nn.silu(causal_conv(qk, conv_w, conv_b))
    q, k = jnp.split(qk, 2, axis=-1)

    def heads(a, d):
        a = a.reshape(b, nc, ML_CHUNK, ML_HEADS, d)
        return jnp.transpose(a, (1, 0, 3, 2, 4)).astype(jnp.float32)

    qh = heads(q, ML_QK_DIM)
    kh = heads(k, ML_QK_DIM) * (ML_QK_DIM ** -0.5)
    vh = heads(v, ML_V_DIM)
    gates = gif.reshape(b, s, 2, ML_HEADS).astype(jnp.float32) + gate_b.astype(jnp.float32)
    ig = gates[:, :, 0]
    logf = jax.nn.log_sigmoid(gates[:, :, 1])

    def gheads(a):
        return jnp.transpose(a.reshape(b, nc, ML_CHUNK, ML_HEADS), (1, 0, 3, 2))

    init = (jnp.zeros((b, ML_HEADS, ML_QK_DIM, ML_V_DIM), jnp.float32),
            jnp.zeros((b, ML_HEADS, ML_QK_DIM), jnp.float32),
            jnp.zeros((b, ML_HEADS), jnp.float32))
    _, h = lax.scan(mlstm_chunk, init, (qh, kh, vh, gheads(logf), gheads(ig)))
    h = jnp.transpose(h, (1, 0, 3, 2, 4)).reshape(b, s, ML_HEADS, ML_V_DIM)
    h = rmsnorm(h, norm_g).reshape(b, s, ML_HEADS * ML_V_DIM)
    return (h * jax.nn.sigmoid(o.astype(jnp.float32))).astype(out_dtype)

def dsa_attention(q, ckv, iq, ik, iw, kv_norm_g, ik_norm_g, w_uv):
    b, s, _ = q.shape
    topk = min(IDX_TOPK_MAX, s // 4)
    q = q.reshape(b, s, DSA_HEADS, DSA_LATENT)
    c = rmsnorm(ckv, kv_norm_g)
    iq = iq.reshape(b, s, IDX_HEADS, IDX_DIM)
    ik = rmsnorm(ik, ik_norm_g)
    iw = iw.astype(jnp.float32) * (IDX_HEADS ** -0.5)
    kpos = jnp.arange(s)

    def block(args):
        i, qb, iqb, iwb = args
        qpos = i * BLOCK_Q + jnp.arange(BLOCK_Q)
        mask = kpos[None, :] <= qpos[:, None]
        isc = jnp.einsum('bqhd,bsd->bqhs', iqb, ik).astype(jnp.float32) * (IDX_DIM ** -0.5)
        isc = jnp.einsum('bqhs,bqh->bqs', jax.nn.relu(isc), iwb)
        isc = jnp.where(mask[None], isc, -jnp.inf)
        vals, idx = lax.top_k(isc, topk)
        valid = jnp.isfinite(vals)
        c_sel = jax.vmap(lambda cb, ib: cb[ib])(c, idx)
        logits = jnp.einsum('bqhc,bqkc->bqhk', qb, c_sel).astype(jnp.float32) * (DSA_LATENT ** -0.5)
        p = jax.nn.softmax(jnp.where(valid[:, :, None, :], logits, -jnp.inf), axis=-1)
        ob = jnp.einsum('bqhk,bqkc->bqhc', p.astype(c.dtype), c_sel)
        return jnp.einsum('bqhc,hcv->bqhv', ob, w_uv)

    nb = s // BLOCK_Q
    o = lax.map(block, (jnp.arange(nb), to_blocks(q, BLOCK_Q), to_blocks(iq, BLOCK_Q), to_blocks(iw, BLOCK_Q)))
    return from_blocks(o).reshape(b, s, DSA_HEADS * DSA_V_DIM)

def setup_inputs(seed: int = 0) -> dict:
    key = jax.random.key(seed)
    ks = jax.random.split(key, 16)
    nrm = jax.random.normal
    f32 = jnp.float32
    x = nrm(ks[0], (BATCH, SEQ, D_MODEL), f32)
    pre_norm_g = 1.0 + 0.02 * nrm(ks[1], (DEPTH, D_MODEL), f32)
    w_in = nrm(ks[2], (DEPTH, D_MODEL, N_IN), f32) * (D_MODEL ** -0.5)
    da_lambda = 0.1 * nrm(ks[3], (DEPTH, 4, DA_HEAD_DIM), f32)
    da_norm_g = 1.0 + 0.02 * nrm(ks[4], (DEPTH, DA_V_DIM), f32)
    ml_conv_w = nrm(ks[5], (DEPTH, ML_CONV, ML_QK_WIDTH), f32) * (ML_CONV ** -0.5)
    ml_conv_b = 0.02 * nrm(ks[6], (DEPTH, ML_QK_WIDTH), f32)
    base = jnp.stack([jnp.zeros((ML_HEADS,), f32), jnp.linspace(3.0, 6.0, ML_HEADS, dtype=f32)])
    ml_gate_b = base[None] + 0.1 * nrm(ks[7], (DEPTH, 2, ML_HEADS), f32)
    ml_norm_g = 1.0 + 0.02 * nrm(ks[8], (DEPTH, ML_V_DIM), f32)
    dsa_kv_norm_g = 1.0 + 0.02 * nrm(ks[9], (DEPTH, DSA_LATENT), f32)
    dsa_ik_norm_g = 1.0 + 0.02 * nrm(ks[10], (DEPTH, IDX_DIM), f32)
    dsa_w_uv = nrm(ks[11], (DEPTH, DSA_HEADS, DSA_LATENT, DSA_V_DIM), f32) * (DSA_LATENT ** -0.5)
    w_branch = nrm(ks[12], (DEPTH, N_BRANCHES, BRANCH_WIDTH, D_MODEL), f32) * (BRANCH_WIDTH ** -0.5)
    w_out = nrm(ks[13], (DEPTH, D_MODEL, D_MODEL), f32) * (D_MODEL ** -0.5)
    post_norm_g = 1.0 + 0.02 * nrm(ks[14], (DEPTH, D_MODEL), f32)
    return {"x": x, "pre_norm_g": pre_norm_g, "w_in": w_in, "da_lambda": da_lambda,
            "da_norm_g": da_norm_g, "ml_conv_w": ml_conv_w, "ml_conv_b": ml_conv_b,
            "ml_gate_b": ml_gate_b, "ml_norm_g": ml_norm_g, "dsa_kv_norm_g": dsa_kv_norm_g,
            "dsa_ik_norm_g": dsa_ik_norm_g, "dsa_w_uv": dsa_w_uv, "w_branch": w_branch,
            "w_out": w_out, "post_norm_g": post_norm_g}

def reference(x, pre_norm_g, w_in, da_lambda, da_norm_g, ml_conv_w, ml_conv_b, ml_gate_b,
              ml_norm_g, dsa_kv_norm_g, dsa_ik_norm_g, dsa_w_uv, w_branch, w_out, post_norm_g):
    b, s, _ = x.shape
    split_points = [int(p) for p in np.cumsum(IN_SPLITS)[:-1]]
    for l in range(DEPTH):
        h = rmsnorm(x, pre_norm_g[l])
        proj = jnp.einsum('bsd,dn->bsn', h, w_in[l])
        (da_q, da_k, da_v, da_z, ml_qk, ml_v, ml_if, ml_o, ml_z,
         dsa_q, dsa_kv, idx_q, idx_k, idx_w, dsa_z, gates) = jnp.split(proj, split_points, axis=-1)
        lam_init = 0.8 - 0.6 * math.exp(-0.3 * l)
        y_a = diff_attention(da_q, da_k, da_v, da_lambda[l], da_norm_g[l], lam_init) * jax.nn.silu(da_z)
        y_b = mlstm(ml_qk, ml_v, ml_if, ml_o, ml_conv_w[l], ml_conv_b[l], ml_gate_b[l], ml_norm_g[l]) * jax.nn.silu(ml_z)
        y_c = dsa_attention(dsa_q, dsa_kv, idx_q, idx_k, idx_w, dsa_kv_norm_g[l], dsa_ik_norm_g[l], dsa_w_uv[l]) * jax.nn.silu(dsa_z)
        g = jax.nn.sigmoid(gates.reshape(b, s, N_BRANCHES, D_MODEL))
        mixed = (g[:, :, 0] * jnp.einsum('bsw,wd->bsd', y_a, w_branch[l, 0])
                 + g[:, :, 1] * jnp.einsum('bsw,wd->bsd', y_b, w_branch[l, 1])
                 + g[:, :, 2] * jnp.einsum('bsw,wd->bsd', y_c, w_branch[l, 2]))
        out = jnp.einsum('bsd,de->bse', mixed, w_out[l])
        x = x + rmsnorm(out, post_norm_g[l])
    return x


_drawn_inputs = setup_inputs


def setup_inputs(seed=0):
    import zlib

    import numpy as np

    out = dict(_drawn_inputs(seed))
    spreads = {}
    factors = {'da_lambda': 8.0,
     'da_norm_g': 4.81,
     'ml_conv_b': 8.0,
     'ml_norm_g': 7.666,
     'dsa_kv_norm_g': 8.0,
     'dsa_ik_norm_g': 3.815,
     'post_norm_g': 3.942}
    for name, (base, spread) in spreads.items():
        noise = np.random.default_rng([zlib.crc32(name.encode()), seed]).standard_normal(out[name].shape)
        drawn = base * np.exp(spread * noise) if base else spread * noise
        out[name] = __import__('jax').numpy.asarray(drawn.astype(out[name].dtype))
    for name, factor in factors.items():
        out[name] = (out[name] * factor).astype(out[name].dtype)
    return out
```

```python
import math
from contextlib import ExitStack

import concourse.bass as bass
from concourse import mybir

F32 = mybir.dt.float32
F32R = mybir.dt.float32r
ALU = mybir.AluOpType
ACT = mybir.ActivationFunctionType
AX = mybir.AxisListType

P = 128
D_MODEL = 2048
SEQ = 256
TILES = SEQ // P
KT = D_MODEL // P
WIDTH = 1024
YT = WIDTH // P
BRANCHES = 3
EPS = 1e-6
LAM_INIT = 0.8 - 0.6 * math.exp(0.0)

DA_HEADS, DA_DIM, DA_V = 8, 64, 128
ML_HEADS, ML_QK, ML_V, ML_CONV = 4, 128, 256, 4
DSA_HEADS, DSA_LATENT, DSA_V = 8, 256, 128
IDX_HEADS, IDX_DIM, TOPK = 16, 64, SEQ // 4

COL_A = 0
COL_ML_QKV = 4096
COL_ML_IF = 6144
COL_ML_OZ = 6152
COL_DSA_Q = 8200
COL_DSA_KV = 10248
COL_IQ = 10504
COL_IK = 11528
COL_DSA_Z = 11608
COL_GATES = 12632

KV0, IK0, IW0, IF0, SMALL = 0, 256, 320, 336, 344

GROUP = 512
UNIT_KT = 2
RING = 4
AHEAD = 4
FULL_UNITS = KT // UNIT_KT
HALF_UNITS = YT // UNIT_KT

MASKED = -1e38
TAKEN = -3e38


class Part:

    def __init__(self, unit0, group0, turns, units, groups):
        self.unit0, self.group0, self.turns, self.units, self.groups = unit0, group0, turns, units, groups

    def unit(self, i, k):
        return i * self.units + (self.unit0 + k)

    def group(self, i, k):
        return i * self.groups + (self.group0 + k)

    def next(self, turns, units, groups):
        return Part(self.unit0 + self.turns * self.units, self.group0 + self.turns * self.groups,
                    turns, units, groups)


PS = Part(0, 0, 1, FULL_UNITS, 1)
PA = PS.next(4, 2 * FULL_UNITS, 2)
PB = PA.next(4, 2 * FULL_UNITS, 2)
PC = PB.next(4, 2 * FULL_UNITS, 2)
PAIR_UNITS = FULL_UNITS + HALF_UNITS
PP = [PC.next(4, PAIR_UNITS, 2)]
PP.append(PP[0].next(4, PAIR_UNITS, 2))
PP.append(PP[1].next(4, PAIR_UNITS, 2))
PO = PP[2].next(1, 4 * FULL_UNITS, 4)
ALL_UNITS = PO.unit0 + PO.units


def landed_count(part, i, k):
    use = (part.unit0 + k) // RING
    if part is PS and use < 2:
        return 48 * (use + 1)
    return i * (16 * part.units // RING) + (16 * (use - 2) + 96 + 16)


def split_span(part, k):
    n = k + AHEAD
    return SMALL if part is PS and n < FULL_UNITS else GROUP


class Steps:

    def __init__(self, engine, sem):
        self.engine, self.sem, self.base, self.k, self.per, self.i = engine, sem, 0, 0, 0, 0

    def enter(self, i, per):
        self.base, self.i, self.per, self.k = self.base + self.k, i, per, 0

    def leave(self, turns):
        assert self.k == self.per, (self.k, self.per)
        self.base, self.k, self.per, self.i = self.base + turns * self.per, 0, 0, 0

    def step(self, instruction):
        self.k += 1
        instruction.then_inc(self.sem, 1)
        self.engine.wait_ge(self.sem, self.i * self.per + (self.base + self.k))


def build(nc, x, pre_norm_g, w_in, da_lambda, da_norm_g, ml_conv_w, ml_conv_b, ml_gate_b, ml_norm_g,
          dsa_kv_norm_g, dsa_ik_norm_g, dsa_w_uv, w_branch, w_out, post_norm_g, out):
    with ExitStack() as ctx:
        def sb(name, shape, dt=F32):
            return ctx.enter_context(nc.sbuf_tensor(name, shape, dt))

        def sem(name):
            return ctx.enter_context(nc.semaphore(name))

        xhi = sb("xhi", [P, KT, SEQ], F32R)
        xlo = sb("xlo", [P, KT, SEQ], F32R)
        raw = sb("raw", [P, RING, UNIT_KT, GROUP])
        whi = sb("whi", [P, RING, UNIT_KT, GROUP], F32R)
        wlo = sb("wlo", [P, RING, UNIT_KT, GROUP], F32R)
        area0 = sb("area0", [P, TILES, 4096])
        area1 = sb("area1", [P, TILES, 4096])
        yhi = sb("yhi", [P, YT, SEQ], F32R)
        ylo = sb("ylo", [P, YT, SEQ], F32R)
        mixed = sb("mixed", [P, TILES, D_MODEL])
        scratch = sb("scratch", [P, 3842])
        small = sb("small", [P, TILES, SMALL])
        ident = sb("ident", [P, P])
        causal = sb("causal", [P, 3 * P])
        upper = sb("upper", [P, P])
        selrow = sb("selrow", [ML_HEADS, ML_HEADS, P])
        rows = sb("rows", [56, P])
        cols = sb("cols", [P, 56])
        lam_in = sb("lam_in", [P, 4, DA_DIM])
        da_g = sb("da_g", [P, DA_V])
        ml_g = sb("ml_g", [P, ML_V])
        kv_g = sb("kv_g", [P, DSA_LATENT])
        ik_g = sb("ik_g", [P, IDX_DIM])
        gate_b = sb("gate_b", [P, 2 * ML_HEADS])
        tiny = sb("tiny", [P, 160])

        ssx, rstdx = tiny[:, 0:2], tiny[:, 2:4]
        sskv, rstdkv = tiny[:, 4:8], tiny[:, 8:12]
        neglam, lam2 = tiny[:, 12:13], tiny[:, 14:16]
        da_negmax_c = tiny[:, 16:20]
        da_sum_c = tiny[:, 20:24]
        da_rsum_c = tiny[:, 24:28]
        acol_h, guard_h = tiny[:, 28:30], tiny[:, 30:32]
        den, rden = tiny[:, 32:34], tiny[:, 34:36]
        dsa_negmax_c, dsa_sum_c, dsa_rsum_c = tiny[:, 36:38], tiny[:, 38:40], tiny[:, 40:42]
        da_ss = tiny[:, 44:60].rearrange("p (h t) -> p h t", t=TILES)
        ml_ss = tiny[:, 60:68].rearrange("p (h t) -> p h t", t=TILES)
        sso, rstdo = tiny[:, 68:76].rearrange("p (t g) -> p t g", t=TILES), tiny[:, 76:78]
        acol = tiny[:, 80:88].rearrange("p (t h) -> p t h", t=TILES)
        guard = tiny[:, 88:96].rearrange("p (t h) -> p t h", t=TILES)
        iw_pair = tiny[:, 96:100].rearrange("p (t e) -> p t e", t=TILES)
        top8 = tiny[:, 100:116].rearrange("p (t e) -> p t e", t=TILES)
        gate_in = tiny[:, 116:132].rearrange("p (t e) -> p t e", t=TILES)
        conv_h = tiny[:, 132:142].rearrange("p (a j) -> p a j", a=2)
        one = tiny[:, 142:143]
        spare = [tiny[:, 143 + n:144 + n] for n in range(10)]

        def view(base, at, *shape):
            n = 1
            for s in shape:
                n *= s
            flat = base[:, at:at + n]
            if len(shape) == 2:
                return flat.rearrange("p (a b) -> p a b", a=shape[0])
            if len(shape) == 3:
                return flat.rearrange("p (a b c) -> p a b c", a=shape[0], b=shape[1])
            return flat

        early = mixed[:, :, :].rearrange("p t n -> p (t n)")
        x_sb = mixed
        turned = area0[:, :, :].rearrange("p t n -> p (t n)")[:, 0:KT * SEQ].rearrange("p (k s) -> p k s", k=KT)
        da_q, da_k, da_v = (view(early, 256 * n, TILES, P) for n in range(3))
        da_qkT = view(early, 768, 2, SEQ)
        da_s = view(early, 1280, 2, 3 * P)
        da_a = view(early, 2048, 3 * P)
        da_aT = view(early, 2432, 3 * P)
        da_sig = view(early, 2816, TILES, P)
        da_o = view(early, 3072, TILES, P)
        da_sq = view(early, 3328, TILES, P)
        ml_qk = view(early, 0, 2, TILES, P)
        ml_xT = view(early, 512, 2, ML_CONV - 1 + SEQ)
        ml_cT = view(early, 1030, 2, SEQ)
        ml_sT = view(early, 1542, 2, SEQ)
        ml_E = view(early, 2054, 3 * P)
        ml_w = view(early, 2438, 3 * P)
        ml_h = view(early, 2822, TILES, ML_V)
        ml_sq = view(early, 3334, TILES, ML_V)
        c_sb = view(scratch, 0, TILES, DSA_LATENT)
        cT = view(scratch, 512, 2, SEQ)
        ikT = view(scratch, 1024, SEQ)
        ml_v = view(scratch, 1280, TILES, ML_V + 1)
        ml_eo = view(scratch, 1794, TILES, ML_V)
        ml_ez = view(scratch, 2306, TILES, ML_V)
        ml_negM = view(scratch, 2818, ML_HEADS, SEQ)
        row_a, row_b, row_c, row_negM = (scratch[0:ML_HEADS, 1794 + SEQ * n:1794 + SEQ * (n + 1)] for n in range(4))
        row_one = scratch[0:ML_HEADS, 1280:1280 + SEQ]
        ik2 = view(scratch, 2818, TILES, 2 * IDX_DIM)
        ya_blk = sb("ya_blk", [P, TILES, 256])
        w_uv = area1[:, 0, 0:2048].rearrange("p (h c v) -> p h c v", h=DSA_HEADS, c=2)
        sig = view(area1[:, 1, :], 0, TILES, GROUP)
        prod = view(area1[:, 1, :], 1024, TILES, GROUP)
        room0, room1 = area1[:, 0, 2048:3072], area1[:, 1, 2048:3072]
        iq_sb = view(room0, 0, TILES, P)
        iqT = view(room0, 256, SEQ)
        idx_acc = view(scratch, 2560, 3 * P)
        select = view(scratch, 1280, 3 * P)
        idx_relu = view(room1, 0, 2, 3 * P)
        dsa_q = view(room0, 0, TILES, DSA_LATENT)
        dsa_qT = view(room0, 512, 2, SEQ)
        dsa_obT = view(room1, 0, 2, SEQ)
        dsa_pT = view(room1, 512, 3 * P)
        dsa_s = view(scratch, 1664, 3 * P)
        dsa_sig = view(scratch, 2048, TILES, P)
        out_sb = area0[:, :, 0:D_MODEL]
        x_again = area0[:, :, D_MODEL:2 * D_MODEL]
        post_g = area1[:, 0, D_MODEL:2 * D_MODEL]

        stream = [[ctx.enter_context(nc.psum_tensor(f"stream{g}{t}", [P, GROUP], F32)) for t in range(TILES)]
                  for g in range(2)]
        M = [ctx.enter_context(nc.psum_tensor(f"mixer{n}", [P, GROUP], F32)) for n in range(4)]
        banks = [stream[0][0], stream[0][1], stream[1][0], stream[1][1], *M]

        x_landed = sem("x_landed")
        consts_landed = sem("consts_landed")
        raw_landed = [sem(f"raw_landed{n}") for n in range(RING)]
        uv_landed = sem("uv_landed")
        end_landed = sem("end_landed")
        stored = sem("stored")
        whi_ready = sem("whi_ready")
        wlo_ready = sem("wlo_ready")
        units_done = sem("units_done")
        banks_free = sem("banks_free")
        masks_ready = sem("masks_ready")
        dve_step, act_step, pool_step = sem("dve_step"), sem("act_step"), sem("pool_step")
        ssx_ready, msx_ready, stdx_ready = sem("ssx_ready"), sem("msx_ready"), sem("stdx_ready")
        cols_turned, cols_ready = sem("cols_turned"), sem("cols_ready")
        xn_ready, x_turned, h_ready = sem("xn_ready"), sem("x_turned"), sem("h_ready")
        xhi_ready, xlo_ready = sem("xhi_ready"), sem("xlo_ready")
        lam_sum_ready, lam_exp_ready = sem("lam_sum_ready"), sem("lam_exp_ready")
        kv_ms_ready, kv_std_ready, kv_normed = sem("kv_ms_ready"), sem("kv_std_ready"), sem("kv_normed")
        prep_turned, prep_copied = sem("prep_turned"), sem("prep_copied")
        row_ready, row_act = sem("row_ready"), sem("row_act")
        da_fetched, da_qkT_psum, da_qkT_ready = sem("da_fetched"), sem("da_qkT_psum"), sem("da_qkT_ready")
        da_scores, da_negmax, da_exp, da_attn = sem("da_scores"), sem("da_negmax"), sem("da_exp"), sem("da_attn")
        da_aT_psum, da_aT_ready, da_av, da_o_out = sem("da_aT_psum"), sem("da_aT_ready"), sem("da_av"), sem("da_o_out")
        da_ez, da_pool = sem("da_ez"), sem("da_pool")
        da_ms, da_std, ya_ready = sem("da_ms"), sem("da_std"), sem("ya_ready")
        rows_turned, rows_copied = sem("rows_turned"), sem("rows_copied")
        ml_fetched, ml_T_psum, ml_xT_ready = sem("ml_fetched"), sem("ml_T_psum"), sem("ml_xT_ready")
        ml_conv, ml_es, ml_cT_ready = sem("ml_conv"), sem("ml_es"), sem("ml_cT_ready")
        ml_arg, ml_exp, ml_E_ready, ml_scores = sem("ml_arg"), sem("ml_exp"), sem("ml_E_ready"), sem("ml_scores")
        ml_w_ready, ml_num, ml_h_ready, ml_pool = sem("ml_w_ready"), sem("ml_num"), sem("ml_h_ready"), sem("ml_pool")
        ml_eoz, ml_gated = sem("ml_eoz"), sem("ml_gated")
        ml_ms, ml_std, yb_ready = sem("ml_ms"), sem("ml_std"), sem("yb_ready")
        ya_fetched, ya_psum = sem("ya_fetched"), sem("ya_psum")
        y_psum, yhi_ready, ylo_ready = sem("y_psum"), sem("yhi_ready"), sem("ylo_ready")
        mixed_zero, gate_exp, prod_ready, merged = sem("mixed_zero"), sem("gate_exp"), sem("prod_ready"), sem("merged")
        idx_fetched, idx_T_psum, iqT_ready = sem("idx_fetched"), sem("idx_T_psum"), sem("iqT_ready")
        idx_scores, idx_relu_ready, idx_added = sem("idx_scores"), sem("idx_relu_ready"), sem("idx_added")
        dsa_fetched, dsa_T_psum, dsa_qT_ready = sem("dsa_fetched"), sem("dsa_T_psum"), sem("dsa_qT_ready")
        dsa_logits, dsa_negmax, dsa_exp = sem("dsa_logits"), sem("dsa_negmax"), sem("dsa_exp")
        dsa_pT_psum, dsa_pT_ready, dsa_ob, dsa_ob_ready = (sem("dsa_pT_psum"), sem("dsa_pT_ready"), sem("dsa_ob"),
                                                          sem("dsa_ob_ready"))
        dsa_out, dsa_y, dsa_ez = sem("dsa_out"), sem("dsa_y"), sem("dsa_ez")
        merged_psum, merged_hi, merged_lo = sem("merged_psum"), sem("merged_hi"), sem("merged_lo")
        out_copied = sem("out_copied")
        out_ss, out_ms, out_std, y_scaled, y_final = (sem("out_ss"), sem("out_ms"), sem("out_std"), sem("y_scaled"),
                                                     sem("y_final"))
        ROW_OUT = D_MODEL // GROUP

        x_d = x[0].rearrange("(t p) d -> p t d", p=P)
        out_d = out[0].rearrange("(t p) d -> p t d", p=P)
        w_in_d = w_in[0].rearrange("(k p) n -> p k n", p=P)
        w_branch_d = [w_branch[0, b].rearrange("(k p) n -> p k n", p=P) for b in range(BRANCHES)]
        w_out_d = w_out[0].rearrange("(k p) n -> p k n", p=P)

        block = ctx.enter_context(nc.Block())

        @block.sync
        def _(sp):
            def load_group(units, part, i, k0, source, col, ahead=False, waited=False):
                for u in range(units):
                    k = k0 + u
                    slot = (part.unit0 + k) % RING
                    if not (waited and u == 0):
                        sp.wait_ge(wlo_ready, part.unit(i, k) - RING + 1 + (ahead and u == units - 1))
                    sp.dma_start(raw[:, slot, :, :],
                                 source[:, UNIT_KT * u:UNIT_KT * (u + 1), bass.ds(col, GROUP)]
                                 ).then_inc(raw_landed[slot], 16)

            def load_small(u):
                slot = u % RING
                if u >= RING:
                    sp.wait_ge(wlo_ready, u - RING + 1)
                for at, col, n in ((KV0, COL_DSA_KV, DSA_LATENT), (IK0, COL_IK, IDX_DIM + IDX_HEADS),
                                   (IF0, COL_ML_IF, 2 * ML_HEADS)):
                    sp.dma_start(raw[:, slot, :, at:at + n],
                                 w_in_d[:, UNIT_KT * u:UNIT_KT * (u + 1), col:col + n]
                                 ).then_inc(raw_landed[slot], 16)

            for t in range(TILES):
                sp.dma_start(x_sb[:, t, :], x_d[:, t, :]).then_inc(x_landed, 16)
            sp.dma_start(rows[0:32, :], ml_conv_w[0].rearrange("j (b d) -> (j b) d", d=P)).then_inc(consts_landed, 16)
            sp.dma_start(rows[32:40, :], ml_conv_b[0].rearrange("(b d) -> b d", d=P)).then_inc(consts_landed, 16)
            sp.dma_start(rows[40:56, :], pre_norm_g[0].rearrange("(b d) -> b d", d=P)).then_inc(consts_landed, 16)
            for u in range(RING):
                load_small(u)
            for to, of in ((lam_in[:, :, :].rearrange("p a b -> p (a b)"), da_lambda[0].rearrange("a b -> (a b)")),
                           (da_g[:, :], da_norm_g[0]), (ml_g[:, :], ml_norm_g[0]), (kv_g[:, :], dsa_kv_norm_g[0]),
                           (ik_g[:, :], dsa_ik_norm_g[0]), (gate_b[:, :], ml_gate_b[0].rearrange("a b -> (a b)"))):
                sp.dma_start(to, of.partition_broadcast(P)).then_inc(consts_landed, 16)
            for u in range(RING, FULL_UNITS):
                load_small(u)

            with sp.Fori(0, PA.turns) as i:
                for g in range(2):
                    load_group(FULL_UNITS, PA, i, g * FULL_UNITS, w_in_d, i * 2 * GROUP + (COL_A + g * GROUP))
            for turn0, col in ((0, COL_ML_QKV), (2, COL_ML_OZ)):
                with sp.Fori(0, 2) as i:
                    for g in range(2):
                        load_group(FULL_UNITS, PB, i, (2 * turn0 + g) * FULL_UNITS, w_in_d,
                                   i * 2 * GROUP + (col + g * GROUP))
            with sp.Fori(0, 2) as i:
                for g in range(2):
                    load_group(FULL_UNITS, PC, i, g * FULL_UNITS, w_in_d, i * 2 * GROUP + (COL_DSA_Q + g * GROUP))
            for turn, col in ((2, COL_IQ), (3, COL_DSA_Z)):
                for g in range(2):
                    load_group(FULL_UNITS, PC, 0, (2 * turn + g) * FULL_UNITS, w_in_d, col + g * GROUP)
            for b in range(BRANCHES):
                if b == 1:
                    sp.wait_ge(yb_ready, ML_HEADS * TILES)
                    sp.dma_start(w_uv, dsa_w_uv[0].rearrange("h (c p) v -> p h c v", p=P)).then_inc(uv_landed, 16)
                with sp.Fori(0, PP[b].turns) as i:
                    load_group(FULL_UNITS, PP[b], i, 0, w_in_d, i * GROUP + (COL_GATES + b * D_MODEL), ahead=True)
                    load_group(HALF_UNITS, PP[b], i, FULL_UNITS, w_branch_d[b], i * GROUP, waited=True)
            sp.wait_ge(y_psum, 8)
            for t in range(TILES):
                sp.dma_start(x_again[:, t, :], x_d[:, t, :]).then_inc(end_landed, 16)
            sp.dma_start(post_g, post_norm_g[0].partition_broadcast(P)).then_inc(end_landed, 16)
            for g in range(ROW_OUT):
                load_group(FULL_UNITS, PO, 0, g * FULL_UNITS, w_out_d, g * GROUP)
            for n in range(TILES * ROW_OUT):
                t, g = n // ROW_OUT, n % ROW_OUT
                sp.wait_ge(y_final, n + 1)
                sp.dma_start(out_d[:, t, g * GROUP:(g + 1) * GROUP],
                             out_sb[:, t, g * GROUP:(g + 1) * GROUP]).then_inc(stored, 16)
            sp.wait_ge(stored, 16 * TILES * ROW_OUT)

        @block.gpsimd
        def _(pool):
            steps = Steps(pool, pool_step)
            steps.step(nc.gpsimd.memset(ident[:, :], 0.0))
            nc.gpsimd.affine_select(out=ident[:, :], in_=ident[:, :], compare_op=ALU.not_equal, fill=1.0, base=0,
                                    pattern=[[-1, P]], channel_multiplier=1).then_inc(masks_ready, 1)
            steps.step(nc.gpsimd.memset(upper[:, :], 1.0))
            nc.gpsimd.affine_select(out=upper[:, :], in_=upper[:, :], compare_op=ALU.is_ge, fill=0.0, base=0,
                                    pattern=[[1, P]], channel_multiplier=-1).then_inc(masks_ready, 1)
            steps.step(nc.gpsimd.memset(causal[:, :], 0.0))
            for at, n, base in ((0, P, 0), (P, 2 * P, P)):
                nc.gpsimd.affine_select(out=causal[:, at:at + n], in_=causal[:, at:at + n], compare_op=ALU.is_ge,
                                        fill=MASKED, base=base, pattern=[[-1, n]], channel_multiplier=1
                                        ).then_inc(masks_ready, 1)
            steps.step(nc.gpsimd.memset(selrow[:, :, :], 0.0))
            nc.gpsimd.affine_select(out=selrow[:, :, :], in_=selrow[:, :, :], compare_op=ALU.not_equal, fill=1.0,
                                    base=0, pattern=[[-1, ML_HEADS], [0, P]], channel_multiplier=1
                                    ).then_inc(masks_ready, 1)

            pool.wait_ge(banks_free, 4 + 2 * PB.group0)
            pool.wait_ge(consts_landed, 9 * 16)
            with pool.Fori(0, PB.turns) as i:
                for s in range(2):
                    h = i * 2 + s
                    pool.wait_ge(units_done, PB.unit(i, s * FULL_UNITS))
                    for n, to in enumerate((da_q, da_k, da_v)):
                        nc.gpsimd.tensor_copy(to, area0[:, :, bass.ds(h * P + n * WIDTH, P)]).then_inc(da_fetched, 1)
                    pool.wait_ge(da_o_out, h + 2)
                    nc.gpsimd.tensor_tensor(da_sq, da_o, da_o, ALU.mult).then_inc(da_pool, 1)
                    nc.gpsimd.tensor_copy(area0[:, :, bass.ds(h * P, P)], da_o).then_inc(da_pool, 1)

            pool.wait_ge(banks_free, 4 + 2 * PC.group0)
            pool.wait_ge(rows_copied, 4)
            pool.wait_ge(ya_ready, TILES * DA_HEADS)
            conv_cols = cols[:, 0:40].rearrange("p (j a h) -> p a h j", a=2, h=ML_HEADS)
            with pool.Fori(0, PC.turns) as i:
                pool.wait_ge(units_done, PC.unit(i, 0))
                for a in range(2):
                    nc.gpsimd.tensor_copy(ml_qk[:, a, :, :], area1[:, :, bass.ds(i * P + a * 512, P)]
                                          ).then_inc(ml_fetched, 1)
                nc.gpsimd.tensor_copy(ml_v[:, :, 0:ML_V], area1[:, :, bass.ds(i * ML_V + WIDTH, ML_V)]
                                      ).then_inc(ml_fetched, 1)
                nc.gpsimd.tensor_copy(conv_h[:, :, :],
                                      conv_cols[:, :, bass.ds(i, 1), :].rearrange("p a h j -> p a (h j)")
                                      ).then_inc(ml_fetched, 1)
                nc.gpsimd.tensor_copy(acol_h, acol[:, :, bass.ds(i, 1)].rearrange("p t h -> p (t h)")
                                      ).then_inc(ml_fetched, 1)
                nc.gpsimd.tensor_copy(guard_h, guard[:, :, bass.ds(i, 1)].rearrange("p t h -> p (t h)")
                                      ).then_inc(ml_fetched, 1)
                nc.gpsimd.tensor_copy(ya_blk[:, :, :], area0[:, :, bass.ds(i * 256 + 3 * WIDTH, 256)]
                                      ).then_inc(ya_fetched, 1)
                pool.wait_ge(ml_exp, i + 1)
                diagonals = ml_E.rearrange("p (c n) -> p c n", n=P)[:, 0:3:2, :]
                nc.gpsimd.tensor_tensor(diagonals, diagonals, upper[:, :].unsqueeze(1).broadcast_to([P, 2, P]),
                                        ALU.mult).then_inc(ml_E_ready, 1)
                pool.wait_ge(ml_h_ready, i * 2 + 4)
                nc.gpsimd.tensor_tensor(ml_sq, ml_h, ml_h, ALU.mult).then_inc(ml_pool, 1)
                nc.gpsimd.tensor_copy(area1[:, :, bass.ds(i * ML_V + WIDTH, ML_V)], ml_h).then_inc(ml_pool, 1)

            pool.wait_ge(yb_ready, ML_HEADS * TILES)
            nc.gpsimd.memset(mixed[:, :, :], 0.0).then_inc(mixed_zero, 1)

            pool.wait_ge(banks_free, 4 + 2 * PP[0].group0)
            with pool.Fori(0, PP[0].turns) as i:
                for s in range(2):
                    pool.wait_ge(units_done, PP[0].unit(i, 6 * s))
                    pool.wait_ge(idx_added, i * 8 + (4 * s + 1))
                    nc.gpsimd.tensor_copy(iq_sb, area0[:, :, bass.ds(i * 256 + (2048 + P * s), P)]
                                          ).then_inc(idx_fetched, 1)
                    nc.gpsimd.tensor_copy(iw_pair, small[:, :, bass.ds(i * 4 + (IW0 + 2 * s), 2)]
                                          ).then_inc(idx_fetched, 1)

            with pool.Fori(0, PP[1].turns) as i:
                for s in range(2):
                    h = i * 2 + s
                    pool.wait_ge(units_done, PP[1].unit(i, 6 * s))
                    nc.gpsimd.tensor_copy(dsa_q, area0[:, :, bass.ds(h * DSA_LATENT, DSA_LATENT)]
                                          ).then_inc(dsa_fetched, 1)

            pool.wait_ge(end_landed, 48)
            for n in range(TILES * ROW_OUT):
                t, g = n // ROW_OUT, n % ROW_OUT
                pool.wait_ge(y_scaled, n + 1)
                to = out_sb[:, t, g * GROUP:(g + 1) * GROUP]
                nc.gpsimd.tensor_tensor(to, to, x_again[:, t, g * GROUP:(g + 1) * GROUP], ALU.add).then_inc(y_final, 1)

        @block.scalar
        def _(act):
            def round_unit(part, i, k):
                n = k + AHEAD
                slot = (part.unit0 + n) % RING
                width = SMALL if part is PS and n < FULL_UNITS else GROUP
                act.wait_ge(raw_landed[slot], landed_count(part, i, n))
                if part.unit0 + n >= RING:
                    act.wait_ge(units_done, part.unit(i, n) - RING + 1)
                nc.scalar.activation(whi[:, slot, :, 0:width], raw[:, slot, :, 0:width], ACT.Copy
                                     ).then_inc(whi_ready, 1)

            def take_group(part, i, k_end, bank_pair, to, width=GROUP):
                act.wait_ge(units_done, part.unit(i, k_end))
                for t in range(TILES):
                    nc.scalar.activation(to[t], stream[bank_pair][t][:, 0:width], ACT.Copy).then_inc(banks_free, 1)

            for t in range(TILES):
                if t == 0:
                    act.wait_ge(x_landed, 32)
                nc.scalar.activation(area1[:, t, 0:D_MODEL], x_sb[:, t, :], ACT.Square,
                                     accum_out=ssx[:, t:t + 1]).then_inc(ssx_ready, 1)
            for k in range(-AHEAD, 0):
                round_unit(PS, 0, k)
            act.wait_ge(msx_ready, 1)
            nc.scalar.activation(rstdx, rstdx, ACT.Sqrt).then_inc(stdx_ready, 1)
            act.wait_ge(cols_turned, 1)
            nc.scalar.activation(cols[:, :], M[0][:, 0:56], ACT.Copy).then_inc(cols_ready, 1)
            for b in range(8):
                act.wait_ge(h_ready, 2 * b + 2)
                nc.scalar.activation(xhi[:, 2 * b:2 * b + 2, :], turned[:, 2 * b:2 * b + 2, :], ACT.Copy
                                     ).then_inc(xhi_ready, 1)

            for u in range(FULL_UNITS):
                round_unit(PS, 0, u)
            take_group(PS, 0, FULL_UNITS, 0, [small[:, t, :] for t in range(TILES)], SMALL)
            act.wait_ge(lam_sum_ready, 2)
            nc.scalar.activation(lam2, lam2, ACT.Exp).then_inc(lam_exp_ready, 1)
            act.wait_ge(kv_ms_ready, 1)
            nc.scalar.activation(rstdkv[:, 0:4], rstdkv[:, 0:4], ACT.Sqrt).then_inc(kv_std_ready, 1)

            with act.Fori(0, PA.turns) as i:
                for g in range(2):
                    for u in range(FULL_UNITS):
                        round_unit(PA, i, g * FULL_UNITS + u)
                    take_group(PA, i, (g + 1) * FULL_UNITS, (PA.group0 + g) % 2,
                               [area0[:, t, bass.ds(i * 2 * GROUP + g * GROUP, GROUP)] for t in range(TILES)])

            act.wait_ge(prep_turned, 1)
            nc.scalar.activation(cT, M[0][:, :].rearrange("p (c s) -> p c s", c=2), ACT.Copy).then_inc(prep_copied, 1)
            act.wait_ge(prep_turned, 2)
            nc.scalar.activation(ikT, M[1][:, 0:SEQ], ACT.Copy).then_inc(prep_copied, 1)
            act.wait_ge(row_ready, 1)
            nc.scalar.activation(row_c, row_c, ACT.Exp).then_inc(row_act, 1)
            act.wait_ge(row_act, 1)
            nc.scalar.activation(row_c, row_c, ACT.Ln, bias=one[0:ML_HEADS, :]).then_inc(row_act, 1)
            act.wait_ge(row_ready, 2)
            nc.scalar.activation(row_c, row_c, ACT.Exp, scale=-1.0).then_inc(row_act, 1)

            with act.Fori(0, PB.turns) as i:
                for s in range(2):
                    h = i * 2 + s
                    for u in range(FULL_UNITS):
                        round_unit(PB, i, s * FULL_UNITS + u)
                        if u == 0:
                            act.wait_ge(da_qkT_psum, h + 1)
                            nc.scalar.activation(da_qkT, M[0][:, :].rearrange("p (a s) -> p a s", a=2), ACT.Copy
                                                 ).then_inc(da_qkT_ready, 1)
                            nc.scalar.activation(da_sig, area0[:, :, bass.ds(h * P + 3 * WIDTH, P)], ACT.Exp,
                                                 scale=-1.0).then_inc(da_ez, 1)
                        if u == 2:
                            act.wait_ge(da_negmax, h * 2 + 2)
                            for t, a, n in ((0, 0, P), (1, P, 2 * P)):
                                for c in range(2):
                                    nc.scalar.activation(da_s[:, c, a:a + n], da_s[:, c, a:a + n], ACT.Exp,
                                                         bias=da_negmax_c[:, 2 * t + c:2 * t + c + 1],
                                                         accum_out=da_sum_c[:, 2 * t + c:2 * t + c + 1]
                                                         ).then_inc(da_exp, 1)
                        if u == 4:
                            act.wait_ge(da_aT_psum, h + 1)
                            nc.scalar.activation(da_aT, M[3][:, 0:3 * P], ACT.Copy).then_inc(da_aT_ready, 1)
                    take_group(PB, i, (s + 1) * FULL_UNITS, (PB.group0 + s) % 2,
                               [area1[:, t, bass.ds(i * 2 * GROUP + s * GROUP, GROUP)] for t in range(TILES)])

            for n in range(2):
                act.wait_ge(rows_turned, n + 1)
                nc.scalar.activation(ml_negM[:, 2 * n:2 * n + 2, :],
                                     M[n + 1][:, :].rearrange("p (h s) -> p h s", h=2), ACT.Copy
                                     ).then_inc(rows_copied, 1)
            act.wait_ge(rows_turned, 3)
            nc.scalar.activation(acol, M[3][:, 0:8].rearrange("p (t h) -> p t h", t=TILES), ACT.Copy
                                 ).then_inc(rows_copied, 1)
            nc.scalar.activation(guard, M[3][:, 8:16].rearrange("p (t h) -> p t h", t=TILES), ACT.Copy
                                 ).then_inc(rows_copied, 1)
            act.wait_ge(da_ms, 1)
            nc.scalar.activation(da_ss, da_ss, ACT.Sqrt).then_inc(da_std, 1)

            with act.Fori(0, PC.turns) as i:
                for v in range(2 * FULL_UNITS):
                    round_unit(PC, i, v)
                    if v == 0:
                        act.wait_ge(ml_T_psum, i + 1)
                        nc.scalar.activation(ml_xT[:, :, ML_CONV - 1:], M[0][:, :].rearrange("p (a s) -> p a s", a=2),
                                             ACT.Copy).then_inc(ml_xT_ready, 1)
                    if v == 3:
                        act.wait_ge(ml_conv, i + 1)
                        nc.scalar.activation(ml_sT, ml_cT, ACT.Exp, scale=-1.0).then_inc(ml_es, 1)
                        act.wait_ge(ml_arg, i * 2 + 2)
                        nc.scalar.activation(ml_E, ml_E, ACT.Exp).then_inc(ml_exp, 1)
                    if v == 9:
                        act.wait_ge(ml_gated, i + 1)
                        nc.scalar.activation(ml_eo, area1[:, :, bass.ds(i * ML_V + 2 * WIDTH, ML_V)], ACT.Exp,
                                             scale=-1.0).then_inc(ml_eoz, 1)
                        nc.scalar.activation(ml_ez, area1[:, :, bass.ds(i * ML_V + 3 * WIDTH, ML_V)], ACT.Exp,
                                             scale=-1.0).then_inc(ml_eoz, 1)
                    if v == 2:
                        act.wait_ge(ya_psum, i + 1)
                        nc.scalar.activation(yhi[:, bass.ds(i * 2, 2), :],
                                             M[2][:, :].rearrange("p (k s) -> p k s", k=2), ACT.Copy
                                             ).then_inc(yhi_ready, 1)
                    if v in (FULL_UNITS - 1, 2 * FULL_UNITS - 1):
                        g = v // FULL_UNITS
                        take_group(PC, i, (g + 1) * FULL_UNITS, (PC.group0 + g) % 2,
                                   [area0[:, t, bass.ds(i * 2 * GROUP + g * GROUP, GROUP)] for t in range(TILES)])
            act.wait_ge(ml_ms, 1)
            nc.scalar.activation(ml_ss, ml_ss, ACT.Sqrt).then_inc(ml_std, 1)

            def gates(part, i, n0):
                act.wait_ge(units_done, part.unit(i, FULL_UNITS))
                act.wait_ge(prod_ready, i * 2 + (2 * n0 + 2))
                for t in range(TILES):
                    nc.scalar.activation(sig[:, t, :], stream[part.group0 % 2][t][:, :], ACT.Exp, scale=-1.0
                                         ).then_inc(gate_exp, 1)

            act.wait_ge(yb_ready, ML_HEADS * TILES)
            with act.Fori(0, PP[0].turns) as i:
                for v in range(PAIR_UNITS):
                    round_unit(PP[0], i, v)
                    s, u = v // 6, v % 6
                    p = i * 2 + s
                    if u == 1:
                        act.wait_ge(idx_T_psum, p + 1)
                        nc.scalar.activation(iqT, M[0][:, 0:SEQ], ACT.Copy).then_inc(iqT_ready, 1)
                    if u == 3:
                        act.wait_ge(idx_scores, p + 1)
                        for e in range(2):
                            nc.scalar.activation(idx_relu[:, e, :], M[1 + e][:, 0:3 * P], ACT.Relu
                                                 ).then_inc(idx_relu_ready, 1)
                    if v == FULL_UNITS - 1:
                        gates(PP[0], i, 0)

            def turn_y(n):
                for b in range(4):
                    act.wait_ge(y_psum, 4 * n + b + 1)
                    nc.scalar.activation(yhi[:, 2 * b:2 * b + 2, :], M[b][:, :].rearrange("p (k s) -> p k s", k=2),
                                         ACT.Copy).then_inc(yhi_ready, 1)

            act.wait_ge(units_done, PP[1].unit0)
            turn_y(0)

            with act.Fori(0, PP[1].turns) as i:
                for v in range(PAIR_UNITS):
                    round_unit(PP[1], i, v)
                    s, u = v // 6, v % 6
                    h = i * 2 + s
                    if u == 0:
                        act.wait_ge(dsa_T_psum, h + 1)
                        nc.scalar.activation(dsa_qT, M[0][:, :].rearrange("p (c s) -> p c s", c=2), ACT.Copy
                                             ).then_inc(dsa_qT_ready, 1)
                    if u == 2:
                        act.wait_ge(dsa_negmax, h * 2 + 2)
                        for t, a, n in ((0, 0, P), (1, P, 2 * P)):
                            nc.scalar.activation(dsa_s[:, a:a + n], dsa_s[:, a:a + n], ACT.Exp,
                                                 bias=dsa_negmax_c[:, t:t + 1], accum_out=dsa_sum_c[:, t:t + 1]
                                                 ).then_inc(dsa_exp, 1)
                        act.wait_ge(dsa_y, h * 2 + 1)
                        nc.scalar.activation(dsa_sig, area0[:, :, bass.ds(h * P + 3 * WIDTH, P)], ACT.Exp,
                                             scale=-1.0).then_inc(dsa_ez, 1)
                    if u == 3:
                        act.wait_ge(dsa_pT_psum, h + 1)
                        nc.scalar.activation(dsa_pT, M[2][:, 0:3 * P], ACT.Copy).then_inc(dsa_pT_ready, 1)
                    if u == 4:
                        act.wait_ge(dsa_ob, h + 1)
                        nc.scalar.activation(dsa_obT, M[3][:, :].rearrange("p (c s) -> p c s", c=2), ACT.Copy
                                             ).then_inc(dsa_ob_ready, 1)
                    if v == FULL_UNITS - 1:
                        gates(PP[1], i, 4)
            act.wait_ge(units_done, PP[2].unit0)
            turn_y(1)

            with act.Fori(0, PP[2].turns) as i:
                for v in range(PAIR_UNITS):
                    round_unit(PP[2], i, v)
                    if v == FULL_UNITS - 1:
                        gates(PP[2], i, 8)

            for b in range(8):
                act.wait_ge(merged_psum, b + 1)
                nc.scalar.activation(xhi[:, 2 * b:2 * b + 2, :], banks[4 + b % 4][:, :].rearrange("p (k s) -> p k s", k=2),
                                     ACT.Copy).then_inc(merged_hi, 1)

            for g in range(ROW_OUT):
                for u in range(FULL_UNITS):
                    if PO.unit0 + g * FULL_UNITS + u + AHEAD < ALL_UNITS:
                        round_unit(PO, 0, g * FULL_UNITS + u)
                act.wait_ge(units_done, PO.unit0 + (g + 1) * FULL_UNITS)
                pair = stream[(PO.group0 + g) % 2]
                for t in range(TILES):
                    nc.scalar.activation(mixed[:, t, 0:GROUP], pair[t][:, :], ACT.Square,
                                         accum_out=sso[:, t, g:g + 1]).then_inc(out_ss, 1)
                    nc.scalar.activation(out_sb[:, t, g * GROUP:(g + 1) * GROUP], pair[t][:, :], ACT.Copy
                                         ).then_inc(out_copied, 1)
            act.wait_ge(out_ms, 1)
            nc.scalar.activation(rstdo, rstdo, ACT.Sqrt).then_inc(out_std, 1)

        @block.vector
        def _(dve):
            steps = Steps(dve, dve_step)

            def split_unit(part, i, k):
                n = k + AHEAD
                slot = (part.unit0 + n) % RING
                width = SMALL if part is PS and n < FULL_UNITS else GROUP
                dve.wait_ge(whi_ready, part.unit(i, n) + 1)
                nc.vector.tensor_tensor(wlo[:, slot, :, 0:width], raw[:, slot, :, 0:width],
                                        whi[:, slot, :, 0:width].bitcast(F32), ALU.subtract).then_inc(wlo_ready, 1)

            nc.vector.memset(spare[0], 0.0).then_inc(banks_free, 4)
            nc.vector.memset(spare[1], 0.0).then_inc(da_o_out, 1)
            nc.vector.memset(spare[2], 0.0).then_inc(ml_h_ready, 2)
            nc.vector.memset(spare[3], 0.0).then_inc(ml_gated, 1)
            nc.vector.memset(spare[4], 0.0).then_inc(ylo_ready, 1)
            nc.vector.memset(spare[5], 0.0).then_inc(idx_added, 1)
            nc.vector.memset(spare[6], 0.0).then_inc(dsa_y, 1)
            nc.vector.memset(spare[7], 0.0).then_inc(gate_exp, 2)
            nc.vector.memset(spare[8], 0.0).then_inc(prod_ready, 2)
            steps.step(nc.vector.memset(one, 1.0))

            dve.wait_ge(ssx_ready, 2)
            nc.vector.tensor_scalar(rstdx, ssx, 1.0 / D_MODEL, EPS, ALU.mult, ALU.add).then_inc(msx_ready, 1)
            for k in range(-AHEAD, 0):
                split_unit(PS, 0, k)
            dve.wait_ge(stdx_ready, 1)
            steps.step(nc.vector.reciprocal(rstdx, rstdx))
            for t in range(TILES):
                nc.vector.tensor_scalar(x_sb[:, t, :], x_sb[:, t, :], rstdx[:, t:t + 1], None, ALU.mult
                                        ).then_inc(xn_ready, 1)
            dve.wait_ge(cols_ready, 1)
            for k in range(KT):
                if k % 2 == 0:
                    dve.wait_ge(x_turned, k // 2 + 1)
                nc.vector.tensor_scalar(turned[:, k, :], banks[(k // 2 + 1) % 8][:, (k % 2) * SEQ:(k % 2 + 1) * SEQ],
                                        cols[:, 40 + k:41 + k], None, ALU.mult).then_inc(h_ready, 1)
                if k % 2 == 1:
                    dve.wait_ge(xhi_ready, k // 2 + 1)
                    nc.vector.tensor_tensor(xlo[:, k - 1:k + 1, :], turned[:, k - 1:k + 1, :],
                                            xhi[:, k - 1:k + 1, :].bitcast(F32), ALU.subtract).then_inc(xlo_ready, 1)

            for u in range(FULL_UNITS):
                split_unit(PS, 0, u)
            dve.wait_ge(consts_landed, 9 * 16)
            steps.step(nc.vector.tensor_tensor(lam_in[:, 0:4:2, :], lam_in[:, 0:4:2, :], lam_in[:, 1:4:2, :],
                                               ALU.mult))
            for n in range(2):
                nc.vector.tensor_reduce(lam2[:, n:n + 1], lam_in[:, 2 * n, :], AX.X, ALU.add).then_inc(lam_sum_ready, 1)
            dve.wait_ge(lam_exp_ready, 1)
            steps.step(nc.vector.tensor_tensor(neglam, lam2[:, 1:2], lam2[:, 0:1], ALU.subtract))
            steps.step(nc.vector.tensor_scalar(neglam, neglam, LAM_INIT, None, ALU.subtract))
            dve.wait_ge(banks_free, 4 + 2 * PA.group0)
            junk = view(scratch, 0, TILES, DSA_LATENT)
            junk2 = view(scratch, 512, TILES, IDX_DIM)
            steps.step(nc.vector.tensor_tensor(junk, small[:, :, KV0:KV0 + DSA_LATENT],
                                               small[:, :, KV0:KV0 + DSA_LATENT], ALU.mult))
            steps.step(nc.vector.tensor_tensor(junk2, small[:, :, IK0:IK0 + IDX_DIM],
                                               small[:, :, IK0:IK0 + IDX_DIM], ALU.mult))
            steps.step(nc.vector.tensor_reduce(sskv[:, 0:2], junk, AX.X, ALU.add))
            steps.step(nc.vector.tensor_reduce(sskv[:, 2:4], junk2, AX.X, ALU.add))
            steps.step(nc.vector.tensor_scalar(rstdkv[:, 0:2], sskv[:, 0:2], 1.0 / DSA_LATENT, EPS, ALU.mult, ALU.add))
            nc.vector.tensor_scalar(rstdkv[:, 2:4], sskv[:, 2:4], 1.0 / IDX_DIM, EPS, ALU.mult, ALU.add
                                    ).then_inc(kv_ms_ready, 1)
            dve.wait_ge(kv_std_ready, 1)
            steps.step(nc.vector.reciprocal(rstdkv, rstdkv))
            for t in range(TILES):
                nc.vector.scalar_tensor_tensor(c_sb[:, t, :], small[:, t, KV0:KV0 + DSA_LATENT], rstdkv[:, t:t + 1],
                                               kv_g[:, :], ALU.mult, ALU.mult).then_inc(kv_normed, 1)
                for n in range(2):
                    nc.vector.scalar_tensor_tensor(ik2[:, t, n * IDX_DIM:(n + 1) * IDX_DIM],
                                                   small[:, t, IK0:IK0 + IDX_DIM], rstdkv[:, 2 + t:3 + t],
                                                   ik_g[:, :], ALU.mult, ALU.mult).then_inc(kv_normed, 1)
            steps.step(nc.vector.tensor_scalar(small[:, :, IW0:IW0 + IDX_HEADS], small[:, :, IW0:IW0 + IDX_HEADS],
                                               IDX_HEADS ** -0.5 * IDX_DIM ** -0.5, None, ALU.mult))
            for t in range(TILES):
                nc.vector.tensor_tensor(gate_in[:, t, :], small[:, t, IF0:IF0 + 2 * ML_HEADS], gate_b[:, :],
                                        ALU.add).then_inc(kv_normed, 1)

            with dve.Fori(0, PA.turns) as i:
                for k in range(2 * FULL_UNITS):
                    split_unit(PA, i, k)

            dve.wait_ge(prep_turned, 3)
            steps.step(nc.vector.memset(row_one, 1.0))
            steps.step(nc.vector.tensor_scalar(row_c, M[2][0:ML_HEADS, SEQ:2 * SEQ], -1.0, None, ALU.mult))
            nc.vector.tensor_tensor(row_c, M[2][0:ML_HEADS, SEQ:2 * SEQ], row_c, ALU.min).then_inc(row_ready, 1)
            dve.wait_ge(row_act, 2)
            steps.step(nc.vector.scalar_tensor_tensor(row_b, M[2][0:ML_HEADS, SEQ:2 * SEQ], 0.0, row_c,
                                                      ALU.min, ALU.subtract))
            steps.step(nc.vector.tensor_tensor_scan(row_c, row_one, row_b, 0.0, ALU.mult, ALU.add))
            steps.step(nc.vector.tensor_tensor(row_a, M[2][0:ML_HEADS, 0:SEQ], row_c, ALU.subtract))
            steps.step(nc.vector.tensor_tensor_scan(row_b, row_a, row_a, 0.0, ALU.max, ALU.max))
            steps.step(nc.vector.tensor_scalar(row_negM, row_b, -1.0, None, ALU.mult))
            nc.vector.tensor_tensor(row_c, row_c, row_b, ALU.add).then_inc(row_ready, 1)

            dve.wait_ge(masks_ready, 5)
            with dve.Fori(0, PB.turns) as i:
                steps.enter(i, 2 * 10)
                for s in range(2):
                    h = i * 2 + s
                    for u in range(FULL_UNITS):
                        split_unit(PB, i, s * FULL_UNITS + u)
                        if u == 0:
                            dve.wait_ge(da_ez, h + 1)
                            steps.step(nc.vector.tensor_scalar(da_sig, da_sig, 1.0, None, ALU.add))
                            steps.step(nc.vector.reciprocal(da_sig, da_sig))
                            z = area0[:, :, bass.ds(h * P + 3 * WIDTH, P)]
                            steps.step(nc.vector.tensor_tensor(da_sig, z, da_sig, ALU.mult))
                            nc.vector.tensor_tensor(z, da_sig, da_g[:, :].unsqueeze(1).broadcast_to([P, TILES, P]),
                                                    ALU.mult)
                        if u == 1:
                            dve.wait_ge(da_scores, h + 1)
                            for c in range(2):
                                steps.step(nc.vector.scalar_tensor_tensor(da_s[:, c, :], M[1 + c][:, 0:3 * P],
                                                                          DA_DIM ** -0.5, causal[:, :], ALU.mult,
                                                                          ALU.add))
                            for t, a, n in ((0, 0, P), (1, P, 2 * P)):
                                nc.vector.tensor_reduce(da_negmax_c[:, 2 * t:2 * t + 2], da_s[:, :, a:a + n], AX.X,
                                                        ALU.max, negate=True).then_inc(da_negmax, 1)
                        if u == 3:
                            dve.wait_ge(da_exp, h * 4 + 4)
                            steps.step(nc.vector.reciprocal(da_rsum_c, da_sum_c))
                            steps.step(nc.vector.tensor_scalar(da_rsum_c[:, 1:4:2], da_rsum_c[:, 1:4:2], neglam, None,
                                                               ALU.mult))
                            for t, a, n in ((0, 0, P), (1, P, 2 * P)):
                                steps.step(nc.vector.tensor_scalar(da_a[:, a:a + n], da_s[:, 0, a:a + n],
                                                                   da_rsum_c[:, 2 * t:2 * t + 1], None, ALU.mult))
                                nc.vector.scalar_tensor_tensor(da_a[:, a:a + n], da_s[:, 1, a:a + n],
                                                               da_rsum_c[:, 2 * t + 1:2 * t + 2], da_a[:, a:a + n],
                                                               ALU.mult, ALU.add).then_inc(da_attn, 1)
                        if u == 5:
                            dve.wait_ge(da_av, h + 1)
                            nc.vector.tensor_copy(da_o, M[0][:, 0:SEQ].rearrange("p (t v) -> p t v", t=TILES)
                                                  ).then_inc(da_o_out, 1)
                        if u == 7:
                            dve.wait_ge(da_pool, h * 2 + 2)
                            steps.step(nc.vector.tensor_reduce(da_ss[:, bass.ds(h, 1), :].rearrange("p h t -> p (h t)"),
                                                               da_sq, AX.X, ALU.add))
                steps.leave(PB.turns)
            nc.vector.tensor_scalar(da_ss, da_ss, 1.0 / DA_V, EPS, ALU.mult, ALU.add).then_inc(da_ms, 1)
            dve.wait_ge(da_std, 1)
            steps.step(nc.vector.reciprocal(da_ss, da_ss))
            steps.step(nc.vector.tensor_scalar(da_ss, da_ss, 1.0 - LAM_INIT, None, ALU.mult))
            for h in range(DA_HEADS):
                for t in range(TILES):
                    z = area0[:, t, 3 * WIDTH + h * P:3 * WIDTH + (h + 1) * P]
                    nc.vector.scalar_tensor_tensor(z, area0[:, t, h * P:(h + 1) * P], da_ss[:, h, t:t + 1], z,
                                                   ALU.mult, ALU.mult).then_inc(ya_ready, 1)
            dve.wait_ge(ya_ready, TILES * DA_HEADS)
            nc.vector.memset(ml_xT[:, :, 0:ML_CONV - 1], 0.0)
            steps.step(nc.vector.memset(ml_v[:, :, ML_V:ML_V + 1], 1.0))

            dve.wait_ge(rows_copied, 4)
            with dve.Fori(0, PC.turns) as i:
                steps.enter(i, 16)
                for v in range(2 * FULL_UNITS):
                    split_unit(PC, i, v)
                    if v == 1:
                        dve.wait_ge(ml_xT_ready, i + 1)
                        dve.wait_ge(ml_fetched, i * 6 + 6)
                        for j in range(ML_CONV):
                            for a in range(2):
                                x_j = ml_xT[:, a, j:j + SEQ]
                                if j == 0:
                                    last = nc.vector.tensor_scalar(ml_cT[:, a, :], x_j, conv_h[:, a, 0:1],
                                                                   conv_h[:, a, 4:5], ALU.mult, ALU.add)
                                else:
                                    last = nc.vector.scalar_tensor_tensor(ml_cT[:, a, :], x_j, conv_h[:, a, j:j + 1],
                                                                          ml_cT[:, a, :], ALU.mult, ALU.add)
                            if j < ML_CONV - 1:
                                steps.step(last)
                        last.then_inc(ml_conv, 1)
                    if v == 2:
                        nc.vector.tensor_scalar(ml_E[:, 0:SEQ], ml_negM[:, bass.ds(i, 1), :].rearrange("p h s -> p (h s)"),
                                                acol_h[:, 0:1], 0.0, ALU.add, ALU.min).then_inc(ml_arg, 1)
                        nc.vector.tensor_scalar(ml_E[:, SEQ:], ml_negM[:, bass.ds(i, 1), P:].rearrange("p h s -> p (h s)"),
                                                acol_h[:, 1:2], 0.0, ALU.add, ALU.min).then_inc(ml_arg, 1)
                        dve.wait_ge(ya_psum, i + 1)
                        dve.wait_ge(yhi_ready, i + 1)
                        nc.vector.tensor_tensor(ylo[:, bass.ds(i * 2, 2), :],
                                                M[2][:, :].rearrange("p (k s) -> p k s", k=2),
                                                yhi[:, bass.ds(i * 2, 2), :].bitcast(F32), ALU.subtract
                                                ).then_inc(ylo_ready, 1)
                    if v == 4:
                        dve.wait_ge(ml_es, i + 1)
                        steps.step(nc.vector.tensor_scalar(ml_sT, ml_sT, 1.0, None, ALU.add))
                        steps.step(nc.vector.reciprocal(ml_sT, ml_sT))
                        nc.vector.tensor_tensor(ml_cT, ml_cT, ml_sT, ALU.mult).then_inc(ml_cT_ready, 1)
                    if v == 6:
                        dve.wait_ge(ml_scores, i + 1)
                        dve.wait_ge(ml_E_ready, i + 1)
                        nc.vector.scalar_tensor_tensor(ml_w, M[1][:, 0:3 * P], ML_QK ** -0.5, ml_E, ALU.mult, ALU.mult
                                                       ).then_inc(ml_w_ready, 1)
                    if v == 8:
                        dve.wait_ge(ml_num, i + 1)
                        for t in range(TILES):
                            total = M[2 + t][:, ML_V:ML_V + 1]
                            steps.step(nc.vector.tensor_scalar(den[:, t:t + 1], total, -1.0, guard_h[:, t:t + 1],
                                                               ALU.mult, ALU.max))
                            steps.step(nc.vector.tensor_scalar(den[:, t:t + 1], total, den[:, t:t + 1], None,
                                                               ALU.max))
                        steps.step(nc.vector.reciprocal(rden, den))
                        for t in range(TILES):
                            nc.vector.tensor_scalar(ml_h[:, t, :], M[2 + t][:, 0:ML_V], rden[:, t:t + 1], None,
                                                    ALU.mult).then_inc(ml_h_ready, 1)
                    if v == 10:
                        dve.wait_ge(ml_eoz, i * 2 + 2)
                        steps.step(nc.vector.tensor_scalar(ml_ez, ml_ez, 1.0, None, ALU.add))
                        steps.step(nc.vector.tensor_scalar(ml_eo, ml_eo, 1.0, None, ALU.add))
                        steps.step(nc.vector.tensor_tensor(ml_ez, ml_eo, ml_ez, ALU.mult))
                        steps.step(nc.vector.reciprocal(ml_ez, ml_ez))
                        z = area1[:, :, bass.ds(i * ML_V + 3 * WIDTH, ML_V)]
                        steps.step(nc.vector.tensor_tensor(ml_ez, z, ml_ez, ALU.mult))
                        nc.vector.tensor_tensor(z, ml_ez, ml_g[:, :].unsqueeze(1).broadcast_to([P, TILES, ML_V]),
                                                ALU.mult).then_inc(ml_gated, 1)
                    if v == 15:
                        dve.wait_ge(ml_pool, i * 2 + 2)
                        steps.step(nc.vector.tensor_reduce(ml_ss[:, bass.ds(i, 1), :].rearrange("p h t -> p (h t)"),
                                                           ml_sq, AX.X, ALU.add))
                steps.leave(PC.turns)
            nc.vector.tensor_scalar(ml_ss, ml_ss, 1.0 / ML_V, EPS, ALU.mult, ALU.add).then_inc(ml_ms, 1)
            dve.wait_ge(ml_std, 1)
            steps.step(nc.vector.reciprocal(ml_ss, ml_ss))
            for h in range(ML_HEADS):
                for t in range(TILES):
                    z = area1[:, t, 3 * WIDTH + h * ML_V:3 * WIDTH + (h + 1) * ML_V]
                    nc.vector.scalar_tensor_tensor(z, area1[:, t, WIDTH + h * ML_V:WIDTH + (h + 1) * ML_V],
                                                   ml_ss[:, h, t:t + 1], z, ALU.mult, ALU.mult).then_inc(yb_ready, 1)
            dve.wait_ge(yb_ready, ML_HEADS * TILES)

            def open_gates(part, i, n0):
                dve.wait_ge(gate_exp, i * 2 + (2 * n0 + 4))
                steps.step(nc.vector.tensor_scalar(sig, sig, 1.0, None, ALU.add))
                steps.step(nc.vector.reciprocal(sig, sig))

            def gate_branch(part, i, n0):
                dve.wait_ge(units_done, part.unit(i, PAIR_UNITS))
                for t in range(TILES):
                    nc.vector.tensor_tensor(prod[:, t, :], stream[(part.group0 + 1) % 2][t][:, :], sig[:, t, :],
                                            ALU.mult).then_inc(prod_ready, 1)
                for t in range(TILES):
                    dve.wait_ge(prod_ready, i * 2 + (2 * n0 + t + 3))
                    to = mixed[:, t, bass.ds(i * GROUP, GROUP)]
                    steps.step(nc.vector.tensor_tensor(to, to, prod[:, t, :], ALU.add))

            dve.wait_ge(mixed_zero, 1)
            nc.vector.tensor_copy(idx_acc, causal[:, :])
            with dve.Fori(0, PP[0].turns) as i:
                steps.enter(i, 4)
                for v in range(PAIR_UNITS):
                    split_unit(PP[0], i, v)
                    s, u = v // 6, v % 6
                    p = i * 2 + s
                    if u == 4:
                        dve.wait_ge(idx_relu_ready, p * 2 + 2)
                        dve.wait_ge(idx_fetched, p * 2 + 2)
                        for e in range(2):
                            dve.wait_ge(idx_added, p * 4 + (2 * e + 1))
                            for t, a, n in ((0, 0, P), (1, P, 2 * P)):
                                nc.vector.scalar_tensor_tensor(idx_acc[:, a:a + n], idx_relu[:, e, a:a + n],
                                                               iw_pair[:, t, e:e + 1], idx_acc[:, a:a + n],
                                                               ALU.mult, ALU.add).then_inc(idx_added, 1)
                    if v == FULL_UNITS:
                        open_gates(PP[0], i, 0)
                gate_branch(PP[0], i, 0)
                steps.leave(PP[0].turns)

            def turn_y(n):
                for b in range(4):
                    dve.wait_ge(yhi_ready, 4 + 4 * n + b + 1)
                    nc.vector.tensor_tensor(ylo[:, 2 * b:2 * b + 2, :], M[b][:, :].rearrange("p (k s) -> p k s", k=2),
                                            yhi[:, 2 * b:2 * b + 2, :].bitcast(F32), ALU.subtract
                                            ).then_inc(ylo_ready, 1)

            turn_y(0)
            dve.wait_ge(idx_added, 1 + 4 * IDX_HEADS // 2)
            steps.step(nc.vector.tensor_copy(select, idx_acc))
            for r in range(TOPK // 8):
                for t, a, n in ((0, 0, P), (1, P, 2 * P)):
                    last = nc.vector.max(top8[:, t, :], select[:, a:a + n])
                steps.step(last)
                for t, a, n in ((0, 0, P), (1, P, 2 * P)):
                    last = nc.vector.match_replace(select[:, a:a + n], top8[:, t, :], select[:, a:a + n], TAKEN)
                steps.step(last)
            steps.step(nc.vector.tensor_scalar(select, select, 0.5 * (MASKED + TAKEN), MASKED, ALU.is_gt, ALU.mult))
            steps.step(nc.vector.tensor_tensor(select, select, causal[:, :], ALU.min))

            with dve.Fori(0, PP[1].turns) as i:
                steps.enter(i, 2 * 5 + 4)
                for v in range(PAIR_UNITS):
                    split_unit(PP[1], i, v)
                    s, u = v // 6, v % 6
                    h = i * 2 + s
                    if u == 1:
                        dve.wait_ge(dsa_logits, h + 1)
                        steps.step(nc.vector.scalar_tensor_tensor(dsa_s, M[1][:, 0:3 * P], DSA_LATENT ** -0.5, select,
                                                                  ALU.mult, ALU.add))
                        for t, a, n in ((0, 0, P), (1, P, 2 * P)):
                            nc.vector.tensor_reduce(dsa_negmax_c[:, t:t + 1], dsa_s[:, a:a + n], AX.X, ALU.max,
                                                    negate=True).then_inc(dsa_negmax, 1)
                    if u == 2:
                        dve.wait_ge(dsa_exp, h * 2 + 2)
                        steps.step(nc.vector.reciprocal(dsa_rsum_c, dsa_sum_c))
                        dve.wait_ge(dsa_ez, h + 1)
                        steps.step(nc.vector.tensor_scalar(dsa_sig, dsa_sig, 1.0, None, ALU.add))
                        steps.step(nc.vector.reciprocal(dsa_sig, dsa_sig))
                        steps.step(nc.vector.tensor_tensor(dsa_sig, area0[:, :, bass.ds(h * P + 3 * WIDTH, P)], dsa_sig,
                                                           ALU.mult))
                    if u == 5:
                        dve.wait_ge(dsa_out, h + 1)
                        for t in range(TILES):
                            nc.vector.scalar_tensor_tensor(area0[:, t, bass.ds(h * P + 3 * WIDTH, P)],
                                                           M[0][:, t * P:(t + 1) * P], dsa_rsum_c[:, t:t + 1],
                                                           dsa_sig[:, t, :], ALU.mult, ALU.mult).then_inc(dsa_y, 1)
                    if v == FULL_UNITS:
                        open_gates(PP[1], i, 4)
                gate_branch(PP[1], i, 4)
                steps.leave(PP[1].turns)
            turn_y(1)

            with dve.Fori(0, PP[2].turns) as i:
                steps.enter(i, 4)
                for v in range(PAIR_UNITS):
                    split_unit(PP[2], i, v)
                    if v == FULL_UNITS:
                        open_gates(PP[2], i, 8)
                gate_branch(PP[2], i, 8)
                steps.leave(PP[2].turns)
            nc.vector.memset(spare[9], 0.0).then_inc(merged, 1)

            for b in range(8):
                dve.wait_ge(merged_hi, b + 1)
                nc.vector.tensor_tensor(xlo[:, 2 * b:2 * b + 2, :],
                                        banks[4 + b % 4][:, :].rearrange("p (k s) -> p k s", k=2),
                                        xhi[:, 2 * b:2 * b + 2, :].bitcast(F32), ALU.subtract).then_inc(merged_lo, 1)
            for k in range(PO.units - AHEAD):
                split_unit(PO, 0, k)
            dve.wait_ge(out_ss, TILES * ROW_OUT)
            steps.step(nc.vector.tensor_reduce(rstdo, sso, AX.X, ALU.add))
            nc.vector.tensor_scalar(rstdo, rstdo, 1.0 / D_MODEL, EPS, ALU.mult, ALU.add).then_inc(out_ms, 1)
            dve.wait_ge(out_std, 1)
            dve.wait_ge(end_landed, 48)
            dve.wait_ge(out_copied, TILES * ROW_OUT)
            steps.step(nc.vector.reciprocal(rstdo, rstdo))
            for n in range(TILES * ROW_OUT):
                t, g = n // ROW_OUT, n % ROW_OUT
                to = out_sb[:, t, g * GROUP:(g + 1) * GROUP]
                nc.vector.scalar_tensor_tensor(to, to, rstdo[:, t:t + 1], post_g[:, g * GROUP:(g + 1) * GROUP],
                                               ALU.mult, ALU.mult).then_inc(y_scaled, 1)

        @block.tensor
        def _(pe):
            def multiply(part, i, k, u, units, bank_pair, left_hi, left_lo, width=GROUP):
                slot = (part.unit0 + k) % RING
                pe.wait_ge(wlo_ready, part.unit(i, k) + 1)
                for j in range(UNIT_KT):
                    kt = UNIT_KT * u + j
                    first, final = kt == 0, kt == UNIT_KT * units - 1
                    for t in range(TILES):
                        to = stream[bank_pair][t][:, 0:width]
                        tokens = slice(t * P, (t + 1) * P)
                        high, low = whi[:, slot, j, 0:width], wlo[:, slot, j, 0:width]
                        nc.tensor.matmul(to, left_hi[:, kt, tokens], high, start=first, stop=False)
                        nc.tensor.matmul(to, left_hi[:, kt, tokens], low, start=False, stop=False)
                        last = nc.tensor.matmul(to, left_lo[:, kt, tokens], high, start=False, stop=final)
                last.then_inc(units_done, 1)

            def open_banks(part, i, k):
                pe.wait_ge(banks_free, i * (2 * part.groups) + (2 * (part.group0 + k) + 2))

            pe.wait_ge(masks_ready, 1)
            pe.wait_ge(consts_landed, 9 * 16)
            nc.tensor.transpose(M[0][:, 0:56], rows[:, :], ident[0:56, 0:56]).then_inc(cols_turned, 1)
            pe.wait_ge(xn_ready, 2)
            for b in range(8):
                if b == 3:
                    pe.wait_ge(cols_ready, 1)
                for j in range(2):
                    for t in range(TILES):
                        kt = 2 * b + j
                        last = nc.tensor.transpose(banks[(b + 1) % 8][:, j * SEQ + t * P:j * SEQ + (t + 1) * P],
                                                   x_sb[:, t, kt * P:(kt + 1) * P], ident[:, :])
                last.then_inc(x_turned, 1)
            pe.wait_ge(xlo_ready, 8)

            for u in range(FULL_UNITS):
                multiply(PS, 0, u, u, FULL_UNITS, 0, xhi, xlo, SMALL)
            with pe.Fori(0, PA.turns) as i:
                for g in range(2):
                    open_banks(PA, i, g)
                    for u in range(FULL_UNITS):
                        multiply(PA, i, g * FULL_UNITS + u, u, FULL_UNITS, (PA.group0 + g) % 2, xhi, xlo)

            pe.wait_ge(kv_normed, 6 + TILES)
            for c in range(2):
                for t in range(TILES):
                    last = nc.tensor.transpose(M[0][:, c * SEQ + t * P:c * SEQ + (t + 1) * P],
                                               c_sb[:, t, c * P:(c + 1) * P], ident[:, :])
            last.then_inc(prep_turned, 1)
            for t in range(TILES):
                last = nc.tensor.transpose(M[1][:, t * P:(t + 1) * P], ik2[:, t, :], ident[:, :])
            last.then_inc(prep_turned, 1)
            for e in range(2):
                for t in range(TILES):
                    last = nc.tensor.transpose(M[2][0:ML_HEADS, e * SEQ + t * P:e * SEQ + (t + 1) * P],
                                               gate_in[:, t, e * ML_HEADS:(e + 1) * ML_HEADS], ident[:, :])
            last.then_inc(prep_turned, 1)

            pe.wait_ge(prep_copied, 2)
            with pe.Fori(0, PB.turns) as i:
                for s in range(2):
                    h = i * 2 + s
                    open_banks(PB, i, s)
                    for u in range(FULL_UNITS):
                        multiply(PB, i, s * FULL_UNITS + u, u, FULL_UNITS, (PB.group0 + s) % 2, xhi, xlo)
                        if u == 0:
                            pe.wait_ge(da_fetched, h * 3 + 3)
                            pe.wait_ge(da_o_out, h + 1)
                            for n, of in enumerate((da_q, da_k)):
                                for t in range(TILES):
                                    last = nc.tensor.transpose(M[0][:, n * SEQ + t * P:n * SEQ + (t + 1) * P],
                                                               of[:, t, :], ident[:, :])
                            last.then_inc(da_qkT_psum, 1)
                        if u == 1:
                            pe.wait_ge(da_qkT_ready, h + 1)
                            pe.wait_ge(row_act, 3)
                            for c in range(2):
                                d = slice(c * DA_DIM, (c + 1) * DA_DIM)
                                nc.tensor.matmul(M[1 + c][:, 0:P], da_qkT[d, 0, 0:P], da_qkT[d, 1, 0:P],
                                                 start=True, stop=True)
                                last = nc.tensor.matmul(M[1 + c][:, P:3 * P], da_qkT[d, 0, P:], da_qkT[d, 1, :],
                                                        start=True, stop=True)
                            last.then_inc(da_scores, 1)
                        if u == 4:
                            pe.wait_ge(da_attn, h * 2 + 2)
                            for b in range(3):
                                last = nc.tensor.transpose(M[3][:, b * P:(b + 1) * P], da_a[:, b * P:(b + 1) * P],
                                                           ident[:, :])
                            last.then_inc(da_aT_psum, 1)
                        if u == 5:
                            pe.wait_ge(da_aT_ready, h + 1)
                            nc.tensor.matmul(M[0][:, 0:P], da_aT[:, 0:P], da_v[:, 0, :], start=True, stop=True)
                            for t in range(TILES):
                                last = nc.tensor.matmul(M[0][:, P:2 * P], da_aT[:, (1 + t) * P:(2 + t) * P],
                                                        da_v[:, t, :], start=(t == 0), stop=(t == 1))
                            last.then_inc(da_av, 1)

            for n in range(2):
                for e in range(2):
                    last = nc.tensor.matmul(M[n + 1][:, e * SEQ:(e + 1) * SEQ], selrow[:, 2 * n + e, :], row_negM,
                                            start=True, stop=True)
                last.then_inc(rows_turned, 1)
            for n, row in enumerate((row_a, row_c)):
                for t in range(TILES):
                    last = nc.tensor.transpose(M[3][:, 8 * n + ML_HEADS * t:8 * n + ML_HEADS * (t + 1)],
                                               row[:, t * P:(t + 1) * P], ident[0:ML_HEADS, 0:ML_HEADS])
            last.then_inc(rows_turned, 1)

            with pe.Fori(0, PC.turns) as i:
                for v in range(2 * FULL_UNITS):
                    g, u = v // FULL_UNITS, v % FULL_UNITS
                    if u == 0:
                        open_banks(PC, i, g)
                    multiply(PC, i, v, u, FULL_UNITS, (PC.group0 + g) % 2, xhi, xlo)
                    if v == 0:
                        pe.wait_ge(ml_fetched, i * 6 + 6)
                        for a in range(2):
                            for t in range(TILES):
                                last = nc.tensor.transpose(M[0][:, a * SEQ + t * P:a * SEQ + (t + 1) * P],
                                                           ml_qk[:, a, t, :], ident[:, :])
                        last.then_inc(ml_T_psum, 1)
                    if v == 1:
                        pe.wait_ge(ya_fetched, i + 1)
                        pe.wait_ge(rows_copied, 4)
                        pe.wait_ge(ml_h_ready, i * 2 + 2)
                        for j in range(2):
                            for t in range(TILES):
                                last = nc.tensor.transpose(M[2][:, j * SEQ + t * P:j * SEQ + (t + 1) * P],
                                                           ya_blk[:, t, j * P:(j + 1) * P], ident[:, :])
                        last.then_inc(ya_psum, 1)
                    if v == 5:
                        pe.wait_ge(ml_cT_ready, i + 1)
                        nc.tensor.matmul(M[1][:, 0:SEQ], ml_cT[:, 1, 0:P], ml_cT[:, 0, :], start=True, stop=True)
                        nc.tensor.matmul(M[1][:, SEQ:3 * P], ml_cT[:, 1, P:], ml_cT[:, 0, P:], start=True, stop=True
                                         ).then_inc(ml_scores, 1)
                    if v == 7:
                        pe.wait_ge(ml_w_ready, i + 1)
                        pe.wait_ge(ylo_ready, i + 2)
                        n = ML_V + 1
                        nc.tensor.matmul(M[2][:, 0:n], ml_w[:, 0:P], ml_v[:, 0, :], start=True, stop=True)
                        nc.tensor.matmul(M[3][:, 0:n], ml_w[:, P:2 * P], ml_v[:, 0, :], start=True, stop=False)
                        nc.tensor.matmul(M[3][:, 0:n], ml_w[:, 2 * P:], ml_v[:, 1, :], start=False, stop=True
                                         ).then_inc(ml_num, 1)

            def gate_units(part, i, v, n0):
                if v == 0:
                    pe.wait_ge(gate_exp, i * 2 + (2 * n0 + 2))
                multiply(part, i, v, v, FULL_UNITS, part.group0 % 2, xhi, xlo)

            def branch_units(part, i, v, n0, ylo_count):
                if v == FULL_UNITS:
                    pe.wait_ge(prod_ready, i * 2 + (2 * n0 + 2))
                    pe.wait_ge(banks_free, 4 + 2 * PP[0].group0)
                    pe.wait_ge(ylo_ready, ylo_count)
                multiply(part, i, v, v - FULL_UNITS, HALF_UNITS, (part.group0 + 1) % 2, yhi, ylo)

            def turn_y(area):
                for b in range(4):
                    for j in range(2):
                        for t in range(TILES):
                            kt = 2 * b + j
                            last = nc.tensor.transpose(M[b][:, j * SEQ + t * P:j * SEQ + (t + 1) * P],
                                                       area[:, t, 3 * WIDTH + kt * P:3 * WIDTH + (kt + 1) * P],
                                                       ident[:, :])
                    last.then_inc(y_psum, 1)

            pe.wait_ge(banks_free, 4 + 2 * (PP[0].group0 - 1))
            with pe.Fori(0, PP[0].turns) as i:
                for v in range(PAIR_UNITS):
                    s, u = v // 6, v % 6
                    p = i * 2 + s
                    if v < FULL_UNITS:
                        gate_units(PP[0], i, v, 0)
                    else:
                        branch_units(PP[0], i, v, 0, 5)
                    if u == 0:
                        pe.wait_ge(idx_fetched, p * 2 + 2)
                        for t in range(TILES):
                            last = nc.tensor.transpose(M[0][:, t * P:(t + 1) * P], iq_sb[:, t, :], ident[:, :])
                        last.then_inc(idx_T_psum, 1)
                    if u == 2:
                        pe.wait_ge(iqT_ready, p + 1)
                        for e in range(2):
                            d = slice(e * IDX_DIM, (e + 1) * IDX_DIM)
                            nc.tensor.matmul(M[1 + e][:, 0:P], iqT[d, 0:P], ikT[d, 0:P], start=True, stop=True)
                            last = nc.tensor.matmul(M[1 + e][:, P:3 * P], iqT[d, P:], ikT[d, :], start=True, stop=True)
                        last.then_inc(idx_scores, 1)
            pe.wait_ge(idx_relu_ready, IDX_HEADS)
            turn_y(area1)

            with pe.Fori(0, PP[1].turns) as i:
                for v in range(PAIR_UNITS):
                    s, u = v // 6, v % 6
                    h = i * 2 + s
                    if v < FULL_UNITS:
                        gate_units(PP[1], i, v, 4)
                    else:
                        branch_units(PP[1], i, v, 4, 9)
                    if u == 0:
                        pe.wait_ge(dsa_fetched, h + 1)
                        pe.wait_ge(dsa_y, h * 2 + 1)
                        pe.wait_ge(ylo_ready, 9)
                        for c in range(2):
                            for t in range(TILES):
                                last = nc.tensor.transpose(M[0][:, c * SEQ + t * P:c * SEQ + (t + 1) * P],
                                                           dsa_q[:, t, c * P:(c + 1) * P], ident[:, :])
                        last.then_inc(dsa_T_psum, 1)
                    if u == 1:
                        pe.wait_ge(dsa_qT_ready, h + 1)
                        for t, a, n in ((0, 0, P), (1, P, 2 * P)):
                            for c in range(2):
                                last = nc.tensor.matmul(M[1][:, a:a + n], dsa_qT[:, c, t * P:(t + 1) * P],
                                                        cT[:, c, 0:n], start=(c == 0), stop=(c == 1))
                        last.then_inc(dsa_logits, 1)
                    if u == 3:
                        pe.wait_ge(dsa_exp, h * 2 + 2)
                        for b in range(3):
                            last = nc.tensor.transpose(M[2][:, b * P:(b + 1) * P], dsa_s[:, b * P:(b + 1) * P],
                                                       ident[:, :])
                        last.then_inc(dsa_pT_psum, 1)
                    if u == 4:
                        pe.wait_ge(dsa_pT_ready, h + 1)
                        for c in range(2):
                            latent = slice(c * P, (c + 1) * P)
                            nc.tensor.matmul(M[3][:, c * SEQ:c * SEQ + P], c_sb[:, 0, latent], dsa_pT[:, 0:P],
                                             start=True, stop=True)
                            for t in range(TILES):
                                last = nc.tensor.matmul(M[3][:, c * SEQ + P:(c + 1) * SEQ], c_sb[:, t, latent],
                                                        dsa_pT[:, (1 + t) * P:(2 + t) * P],
                                                        start=(t == 0), stop=(t == 1))
                        last.then_inc(dsa_ob, 1)
                    if u == 5:
                        pe.wait_ge(dsa_ob_ready, h + 1)
                        pe.wait_ge(uv_landed, 16)
                        for t in range(TILES):
                            for c in range(2):
                                last = nc.tensor.matmul(M[0][:, t * P:(t + 1) * P], dsa_obT[:, c, t * P:(t + 1) * P],
                                                        w_uv[:, bass.ds(h, 1), c, :].rearrange("p h v -> p (h v)"),
                                                        start=(c == 0), stop=(c == 1))
                        last.then_inc(dsa_out, 1)
            pe.wait_ge(dsa_y, 1 + TILES * DSA_HEADS)
            turn_y(area0)

            with pe.Fori(0, PP[2].turns) as i:
                for v in range(PAIR_UNITS):
                    if v < FULL_UNITS:
                        gate_units(PP[2], i, v, 8)
                    else:
                        branch_units(PP[2], i, v, 8, 13)

            pe.wait_ge(merged, 1)
            for b in range(8):
                if b >= 4:
                    pe.wait_ge(merged_lo, b - 3)
                for j in range(2):
                    for t in range(TILES):
                        kt = 2 * b + j
                        last = nc.tensor.transpose(banks[4 + b % 4][:, j * SEQ + t * P:j * SEQ + (t + 1) * P],
                                                   mixed[:, t, kt * P:(kt + 1) * P], ident[:, :])
                last.then_inc(merged_psum, 1)
            pe.wait_ge(merged_lo, 8)

            for g in range(ROW_OUT):
                if g == 0:
                    pe.wait_ge(gate_exp, 2 + 2 * 4 * BRANCHES)
                elif g == 1:
                    pe.wait_ge(prod_ready, 2 + 2 * 4 * BRANCHES)
                else:
                    pe.wait_ge(out_copied, TILES * (g - 1))
                for u in range(FULL_UNITS):
                    multiply(PO, 0, g * FULL_UNITS + u, u, FULL_UNITS, (PO.group0 + g) % 2, xhi, xlo)


_INS = ["x", "pre_norm_g", "w_in", "da_lambda", "da_norm_g", "ml_conv_w", "ml_conv_b", "ml_gate_b", "ml_norm_g",
        "dsa_kv_norm_g", "dsa_ik_norm_g", "dsa_w_uv", "w_branch", "w_out", "post_norm_g"]


def kernel(**inputs):
    import numpy as np
    import concourse.bacc as bacc
    from concourse.bass_utils import run_bass_kernel_spmd

    nc = bacc.Bacc("TRN2", target_bir_lowering=False, num_devices=1)
    arrays, args = {}, []
    for name in _INS:
        a = np.ascontiguousarray(inputs[name])
        arrays[f"in_{name}"] = a
        args.append(nc.dram_tensor(f"in_{name}", a.shape, mybir.dt.from_np(a.dtype), kind="ExternalInput").ap())
    out = nc.dram_tensor("out_0", (1, SEQ, D_MODEL), F32, kind="ExternalOutput").ap()
    build(nc, *args, out)
    result = run_bass_kernel_spmd(nc, [arrays], core_ids=[0])
    return result.results[0]["out_0"]
```

```python
import math
from contextlib import ExitStack

import concourse.bass as bass
from concourse import mybir

F32 = mybir.dt.float32
F32R = mybir.dt.float32r
ALU = mybir.AluOpType
ACT = mybir.ActivationFunctionType
AX = mybir.AxisListType

P = 128
D_MODEL = 2048
SEQ = 256
TILES = SEQ // P
KT = D_MODEL // P
WIDTH = 1024
YT = WIDTH // P
BRANCHES = 3
EPS = 1e-6
LAM_INIT = 0.8 - 0.6 * math.exp(0.0)

DA_HEADS, DA_DIM, DA_V = 8, 64, 128
ML_HEADS, ML_QK, ML_V, ML_CONV = 4, 128, 256, 4
DSA_HEADS, DSA_LATENT, DSA_V = 8, 256, 128
IDX_HEADS, IDX_DIM, TOPK = 16, 64, SEQ // 4

COL_A = 0
COL_ML_QKV = 4096
COL_ML_IF = 6144
COL_ML_OZ = 6152
COL_DSA_Q = 8200
COL_DSA_KV = 10248
COL_IQ = 10504
COL_IK = 11528
COL_DSA_Z = 11608
COL_GATES = 12632

KV0, IK0, IW0, IF0, SMALL = 0, 256, 320, 336, 344

X_LOADS = 4
GROUP = 512
UNIT_KT = 2
RING = 4
AHEAD = 4
FULL_UNITS = KT // UNIT_KT
HALF_UNITS = YT // UNIT_KT
IDX_TURNS = 2

MASKED = -1e38
TAKEN = -3e38


class Part:

    def __init__(self, unit0, group0, turns, units, groups):
        self.unit0, self.group0, self.turns, self.units, self.groups = unit0, group0, turns, units, groups

    def unit(self, i, k):
        return i * self.units + (self.unit0 + k)

    def group(self, i, k):
        return i * self.groups + (self.group0 + k)

    def next(self, turns, units, groups):
        return Part(self.unit0 + self.turns * self.units, self.group0 + self.turns * self.groups,
                    turns, units, groups)


EARLY_UNITS = {6: (0,), 7: (1, 2, 3)}
PS = Part(0, 0, 1, FULL_UNITS, 1)
PA = PS.next(4, 2 * FULL_UNITS, 2)
PB = PA.next(4, 2 * FULL_UNITS, 2)
PC = PB.next(4, 2 * FULL_UNITS, 2)
PAIR_UNITS = FULL_UNITS + HALF_UNITS
PP = [PC.next(4, PAIR_UNITS, 2)]
PP.append(PP[0].next(4, PAIR_UNITS, 2))
PP.append(PP[1].next(4, PAIR_UNITS, 2))
PO = PP[2].next(1, 4 * FULL_UNITS, 4)
ALL_UNITS = PO.unit0 + PO.units


def landed_count(part, i, k):
    use = (part.unit0 + k) // RING
    if part is PS and use < 2:
        return 48 * (use + 1)
    return i * (16 * part.units // RING) + (16 * (use - 2) + 96 + 16)


def split_span(part, k):
    n = k + AHEAD
    return SMALL if part is PS and n < FULL_UNITS else GROUP


class Steps:

    def __init__(self, engine, sem):
        self.engine, self.sem, self.base, self.k, self.per, self.i = engine, sem, 0, 0, 0, 0

    def enter(self, i, per):
        self.base, self.i, self.per, self.k = self.base + self.k, i, per, 0

    def leave(self, turns):
        assert self.k == self.per, (self.k, self.per)
        self.base, self.k, self.per, self.i = self.base + turns * self.per, 0, 0, 0

    def step(self, instruction):
        self.k += 1
        instruction.then_inc(self.sem, 1)
        self.engine.wait_ge(self.sem, self.i * self.per + (self.base + self.k))


def build(nc, x, pre_norm_g, w_in, da_lambda, da_norm_g, ml_conv_w, ml_conv_b, ml_gate_b, ml_norm_g,
          dsa_kv_norm_g, dsa_ik_norm_g, dsa_w_uv, w_branch, w_out, post_norm_g, out):
    with ExitStack() as ctx:
        def sb(name, shape, dt=F32):
            return ctx.enter_context(nc.sbuf_tensor(name, shape, dt))

        def sem(name):
            return ctx.enter_context(nc.semaphore(name))

        xhi = sb("xhi", [P, KT, SEQ], F32R)
        xlo = sb("xlo", [P, KT, SEQ], F32R)
        raw = sb("raw", [P, RING, UNIT_KT, GROUP])
        whi = sb("whi", [P, RING, UNIT_KT, GROUP], F32R)
        wlo = sb("wlo", [P, RING, UNIT_KT, GROUP], F32R)
        area0 = sb("area0", [P, TILES, 4096])
        area1 = sb("area1", [P, TILES, 4096])
        yhi = sb("yhi", [P, YT, SEQ], F32R)
        ylo = sb("ylo", [P, YT, SEQ], F32R)
        mixed = sb("mixed", [P, TILES, D_MODEL])
        scratch = sb("scratch", [P, 3842])
        small = sb("small", [P, TILES, SMALL])
        ident = sb("ident", [P, P])
        causal = sb("causal", [P, 3 * P])
        upper = sb("upper", [P, P])
        selrow = sb("selrow", [ML_HEADS, ML_HEADS, P])
        rows = sb("rows", [56, P])
        cols = sb("cols", [P, 56])
        lam_in = sb("lam_in", [P, 4, DA_DIM])
        da_g = sb("da_g", [P, DA_V])
        ml_g = sb("ml_g", [P, ML_V])
        kv_g = sb("kv_g", [P, DSA_LATENT])
        ik_g = sb("ik_g", [P, IDX_DIM])
        gate_b = sb("gate_b", [P, 2 * ML_HEADS])
        tiny = sb("tiny", [P, 168])

        ssx, rstdx, half_rstdx = tiny[:, 0:2], tiny[:, 2:4], tiny[:, 154:156]
        sskv, rstdkv = tiny[:, 4:8], tiny[:, 8:12]
        neglam, lam2 = tiny[:, 12:13], tiny[:, 14:16]
        da_negmax_c = tiny[:, 16:20]
        da_sum_c = tiny[:, 20:24]
        da_rsum_c = tiny[:, 24:28]
        acol_h, guard_h = tiny[:, 28:30], tiny[:, 30:32]
        den, rden = tiny[:, 32:34], tiny[:, 34:36]
        dsa_negmax_c, dsa_sum_c, dsa_rsum_c = tiny[:, 36:38], tiny[:, 38:40], tiny[:, 40:42]
        da_ss = tiny[:, 44:60].rearrange("p (h t) -> p h t", t=TILES)
        ml_ss = tiny[:, 60:68].rearrange("p (h t) -> p h t", t=TILES)
        sso, rstdo = tiny[:, 68:76].rearrange("p (t g) -> p t g", t=TILES), tiny[:, 76:78]
        acol = tiny[:, 80:88].rearrange("p (t h) -> p t h", t=TILES)
        guard = tiny[:, 88:96].rearrange("p (t h) -> p t h", t=TILES)
        iw_pair = tiny[:, 96:100].rearrange("p (t e) -> p t e", t=TILES)
        top8 = tiny[:, 100:116].rearrange("p (t e) -> p t e", t=TILES)
        gate_in = tiny[:, 116:132].rearrange("p (t e) -> p t e", t=TILES)
        forget_t = tiny[:, 156:164].rearrange("p (t h) -> p t h", t=TILES)
        conv_h = tiny[:, 132:142].rearrange("p (a j) -> p a j", a=2)
        wait_carrier = tiny[:, 166:167]
        one = tiny[:, 142:143]
        spare = [tiny[:, 143 + n:144 + n] for n in range(10)]

        def view(base, at, *shape):
            n = 1
            for s in shape:
                n *= s
            flat = base[:, at:at + n]
            if len(shape) == 2:
                return flat.rearrange("p (a b) -> p a b", a=shape[0])
            if len(shape) == 3:
                return flat.rearrange("p (a b c) -> p a b c", a=shape[0], b=shape[1])
            return flat

        early = mixed[:, :, :].rearrange("p t n -> p (t n)")
        x_sb = mixed
        turned = area0[:, :, :].rearrange("p t n -> p (t n)")[:, 0:KT * SEQ].rearrange("p (k s) -> p k s", k=KT)
        da_q, da_k, da_v = (view(early, 256 * n, TILES, P) for n in range(3))
        da_qkT = view(early, 768, 2, SEQ)
        da_s = view(early, 1280, 2, 3 * P)
        da_a = view(early, 2048, 3 * P)
        da_aT = view(early, 2432, 3 * P)
        da_sig = view(early, 2816, TILES, P)
        da_o = view(early, 3072, TILES, P)
        da_sq = view(early, 3328, TILES, P)
        ml_qk = view(early, 0, 2, TILES, P)
        ml_xT = view(early, 512, 2, ML_CONV - 1 + SEQ)
        ml_cT = view(early, 1030, 2, SEQ)
        ml_sT = view(early, 1542, 2, SEQ)
        ml_E = view(early, 2054, 3 * P)
        ml_w = view(early, 2438, 3 * P)
        ml_h = view(early, 2822, TILES, ML_V)
        ml_sq = view(early, 3334, TILES, ML_V)
        c_sb = view(scratch, 0, TILES, DSA_LATENT)
        cT = view(scratch, 512, 2, SEQ)
        ikT = view(scratch, 1024, SEQ)
        ml_v = view(scratch, 1280, TILES, ML_V + 1)
        ml_to = view(scratch, 1794, TILES, ML_V)
        ml_tz = view(scratch, 2306, TILES, ML_V)
        ml_negM = view(scratch, 2818, ML_HEADS, SEQ)
        row_a, row_b, row_c, row_negM = (scratch[0:ML_HEADS, 1794 + SEQ * n:1794 + SEQ * (n + 1)] for n in range(4))
        row_one = scratch[0:ML_HEADS, 1280:1280 + SEQ]
        ik2 = view(scratch, 2818, TILES, 2 * IDX_DIM)
        ya_blk = sb("ya_blk", [P, TILES, 256])
        w_uv = area1[:, 0, 0:2048].rearrange("p (h c v) -> p h c v", h=DSA_HEADS, c=2)
        sig = view(area1[:, 1, :], 0, TILES, GROUP)
        prod = view(area1[:, 1, :], 1024, TILES, GROUP)
        room0, room1 = area1[:, 0, 2048:3072], area1[:, 1, 2048:3072]
        iq_sb = ya_blk[:, :, 0:P]
        iqT = view(room0, 256, SEQ)
        idx_acc = view(scratch, 2560, 3 * P)
        select = view(scratch, 1280, 3 * P)
        idx_relu = view(room1, 0, 2, 3 * P)
        dsa_q = ya_blk[:, :, :]
        dsa_qT = view(room0, 512, 2, SEQ)
        dsa_obT = view(room1, 0, 2, SEQ)
        dsa_pT = view(room1, 512, 3 * P)
        dsa_s = view(scratch, 1664, 3 * P)
        dsa_sig = view(scratch, 2048, TILES, P)
        out_sb = area0[:, :, 0:D_MODEL]
        x_again = area0[:, :, D_MODEL:2 * D_MODEL]
        post_g = area1[:, 0, D_MODEL:2 * D_MODEL]

        stream = [[ctx.enter_context(nc.psum_tensor(f"stream{g}{t}", [P, GROUP], F32)) for t in range(TILES)]
                  for g in range(2)]
        M = [ctx.enter_context(nc.psum_tensor(f"mixer{n}", [P, GROUP], F32)) for n in range(4)]
        banks = [stream[0][0], stream[0][1], stream[1][0], stream[1][1], *M]

        merge_banks = M + stream[PP[2].group0 % 2] + M[0:2]

        def out_pair(g):
            return (PO.group0 + 1 + g) % 2

        x_landed = [sem(f"x_landed{n}") for n in range(X_LOADS)]
        rows_landed = sem("rows_landed")
        consts_landed = sem("consts_landed")
        raw_landed = [sem(f"raw_landed{n}") for n in range(RING)]
        uv_landed = sem("uv_landed")
        end_landed = sem("end_landed")
        stored = sem("stored")
        whi_ready = sem("whi_ready")
        wlo_ready = sem("wlo_ready")
        units_done = sem("units_done")
        banks_free = sem("banks_free")
        masks_ready = sem("masks_ready")
        dve_step, act_step, pool_step = sem("dve_step"), sem("act_step"), sem("pool_step")
        ssx_ready, msx_ready, stdx_ready = sem("ssx_ready"), sem("msx_ready"), sem("stdx_ready")
        cols_turned, cols_ready = sem("cols_turned"), sem("cols_ready")
        rstdx_ready, x_turned, h_ready = sem("rstdx_ready"), sem("x_turned"), sem("h_ready")
        xhi_ready, xlo_ready = sem("xhi_ready"), sem("xlo_ready")
        lam_sum_ready, lam_exp_ready = sem("lam_sum_ready"), sem("lam_exp_ready")
        kv_ms_ready, kv_std_ready, kv_normed = sem("kv_ms_ready"), sem("kv_std_ready"), sem("kv_normed")
        prep_turned, prep_copied = sem("prep_turned"), sem("prep_copied")
        row_ready, row_act = sem("row_ready"), sem("row_act")
        da_v_fetched = sem("da_v_fetched")
        da_fetched, da_qkT_psum, da_qkT_ready = sem("da_fetched"), sem("da_qkT_psum"), sem("da_qkT_ready")
        da_scores, da_negmax, da_exp, da_attn = sem("da_scores"), sem("da_negmax"), sem("da_exp"), sem("da_attn")
        da_aT_psum, da_aT_ready, da_av, da_o_out = sem("da_aT_psum"), sem("da_aT_ready"), sem("da_av"), sem("da_o_out")
        da_tz, da_pool = sem("da_tz"), sem("da_pool")
        da_ms, da_std, ya_ready = sem("da_ms"), sem("da_std"), sem("ya_ready")
        rows_turned, rows_copied = sem("rows_turned"), sem("rows_copied")
        ml_fetched, ml_T_psum, ml_xT_ready = sem("ml_fetched"), sem("ml_T_psum"), sem("ml_xT_ready")
        ml_conv, ml_ts, ml_cT_ready = sem("ml_conv"), sem("ml_ts"), sem("ml_cT_ready")
        ml_arg, ml_exp, ml_E_ready, ml_scores = sem("ml_arg"), sem("ml_exp"), sem("ml_E_ready"), sem("ml_scores")
        ml_w_ready, ml_num, ml_h_ready, ml_pool = sem("ml_w_ready"), sem("ml_num"), sem("ml_h_ready"), sem("ml_pool")
        ml_toz, ml_gated = sem("ml_toz"), sem("ml_gated")
        ml_ms, ml_std, yb_ready = sem("ml_ms"), sem("ml_std"), sem("yb_ready")
        ya_fetched, ya_psum = sem("ya_fetched"), sem("ya_psum")
        y_psum, yhi_ready, ylo_ready = sem("y_psum"), sem("yhi_ready"), sem("ylo_ready")
        gate_tanh, prod_ready, mixed_added, iw_fetched = (sem("gate_tanh"), sem("prod_ready"), sem("mixed_added"),
                                                          sem("iw_fetched"))
        idx_fetched, idx_T_psum, iqT_ready = sem("idx_fetched"), sem("idx_T_psum"), sem("iqT_ready")
        idx_scores, idx_relu_ready, idx_added = sem("idx_scores"), sem("idx_relu_ready"), sem("idx_added")
        dsa_fetched, dsa_T_psum, dsa_qT_ready = sem("dsa_fetched"), sem("dsa_T_psum"), sem("dsa_qT_ready")
        dsa_logits, dsa_negmax, dsa_exp = sem("dsa_logits"), sem("dsa_negmax"), sem("dsa_exp")
        dsa_pT_psum, dsa_pT_ready, dsa_ob, dsa_ob_ready = (sem("dsa_pT_psum"), sem("dsa_pT_ready"), sem("dsa_ob"),
                                                          sem("dsa_ob_ready"))
        dsa_out, dsa_y, dsa_tz = sem("dsa_out"), sem("dsa_y"), sem("dsa_tz")
        merged_psum, merged_hi, merged_lo = sem("merged_psum"), sem("merged_hi"), sem("merged_lo")
        out_copied = sem("out_copied")
        out_ss, out_ms, out_std, y_scaled, y_final = (sem("out_ss"), sem("out_ms"), sem("out_std"), sem("y_scaled"),
                                                     sem("y_final"))
        ROW_OUT = D_MODEL // GROUP

        x_d = x[0].rearrange("(t p) d -> p t d", p=P)
        out_d = out[0].rearrange("(t p) d -> p t d", p=P)
        w_in_d = w_in[0].rearrange("(k p) n -> p k n", p=P)
        w_branch_d = [w_branch[0, b].rearrange("(k p) n -> p k n", p=P) for b in range(BRANCHES)]
        w_out_d = w_out[0].rearrange("(k p) n -> p k n", p=P)

        block = ctx.enter_context(nc.Block())

        @block.sync
        def _(sp):
            def load_group(units, part, i, k0, source, col, ahead=False, waited=False):
                for u in range(units):
                    k = k0 + u
                    slot = (part.unit0 + k) % RING
                    if not (waited and u == 0):
                        sp.wait_ge(wlo_ready, part.unit(i, k) - RING + 1 + (ahead and u == units - 1))
                    sp.dma_start(raw[:, slot, :, :],
                                 source[:, UNIT_KT * u:UNIT_KT * (u + 1), bass.ds(col, GROUP)]
                                 ).then_inc(raw_landed[slot], 16)

            def load_small(u):
                slot = u % RING
                if u >= RING:
                    sp.wait_ge(wlo_ready, u - RING + 1)
                for at, col, n in ((KV0, COL_DSA_KV, DSA_LATENT), (IK0, COL_IK, IDX_DIM + IDX_HEADS),
                                   (IF0, COL_ML_IF, 2 * ML_HEADS)):
                    sp.dma_start(raw[:, slot, :, at:at + n],
                                 w_in_d[:, UNIT_KT * u:UNIT_KT * (u + 1), col:col + n]
                                 ).then_inc(raw_landed[slot], 16)

            for n in range(X_LOADS):
                part_of_x = slice(n * D_MODEL // X_LOADS, (n + 1) * D_MODEL // X_LOADS)
                sp.dma_start(x_sb[:, :, part_of_x], x_d[:, :, part_of_x]).then_inc(x_landed[n], 16)
                if n == 0:
                    sp.dma_start(rows[40:56, :], pre_norm_g[0].rearrange("(b d) -> b d", d=P)).then_inc(rows_landed, 16)
                    sp.dma_start(rows[0:32, :], ml_conv_w[0].rearrange("j (b d) -> (j b) d", d=P)
                                 ).then_inc(rows_landed, 16)
                    sp.dma_start(rows[32:40, :], ml_conv_b[0].rearrange("(b d) -> b d", d=P)).then_inc(rows_landed, 16)
                if n >= 2:
                    load_small(n - 2)
            load_small(2)
            load_small(3)
            for to, of in ((lam_in[:, :, :].rearrange("p a b -> p (a b)"), da_lambda[0].rearrange("a b -> (a b)")),
                           (da_g[:, :], da_norm_g[0]), (ml_g[:, :], ml_norm_g[0]), (kv_g[:, :], dsa_kv_norm_g[0]),
                           (ik_g[:, :], dsa_ik_norm_g[0]), (gate_b[:, :], ml_gate_b[0].rearrange("a b -> (a b)"))):
                sp.dma_start(to, of.partition_broadcast(P)).then_inc(consts_landed, 16)
            for u in range(RING, FULL_UNITS):
                load_small(u)

            with sp.Fori(0, PA.turns) as i:
                for g in range(2):
                    load_group(FULL_UNITS, PA, i, g * FULL_UNITS, w_in_d, i * 2 * GROUP + (COL_A + g * GROUP))
            for turn0, col in ((0, COL_ML_QKV), (2, COL_ML_OZ)):
                with sp.Fori(0, 2) as i:
                    for g in range(2):
                        load_group(FULL_UNITS, PB, i, (2 * turn0 + g) * FULL_UNITS, w_in_d,
                                   i * 2 * GROUP + (col + g * GROUP))
            with sp.Fori(0, 2) as i:
                for g in range(2):
                    load_group(FULL_UNITS, PC, i, g * FULL_UNITS, w_in_d, i * 2 * GROUP + (COL_DSA_Q + g * GROUP))
            for turn, col in ((2, COL_IQ), (3, COL_DSA_Z)):
                for g in range(2):
                    load_group(FULL_UNITS, PC, 0, (2 * turn + g) * FULL_UNITS, w_in_d, col + g * GROUP)
            for b in range(BRANCHES):
                if b == 1:
                    sp.wait_ge(yb_ready, ML_HEADS * TILES)
                    sp.dma_start(w_uv, dsa_w_uv[0].rearrange("h (c p) v -> p h c v", p=P)).then_inc(uv_landed, 16)
                with sp.Fori(0, PP[b].turns) as i:
                    load_group(FULL_UNITS, PP[b], i, 0, w_in_d, i * GROUP + (COL_GATES + b * D_MODEL), ahead=True)
                    load_group(HALF_UNITS, PP[b], i, FULL_UNITS, w_branch_d[b], i * GROUP, waited=True)
            sp.wait_ge(y_psum, 8)
            for t in range(TILES):
                sp.dma_start(x_again[:, t, :], x_d[:, t, :]).then_inc(end_landed, 16)
            sp.dma_start(post_g, post_norm_g[0].partition_broadcast(P)).then_inc(end_landed, 16)
            for g in range(ROW_OUT):
                load_group(FULL_UNITS, PO, 0, g * FULL_UNITS, w_out_d, g * GROUP)
            for n in range(TILES * ROW_OUT):
                t, g = n // ROW_OUT, n % ROW_OUT
                sp.wait_ge(y_final, n + 1)
                sp.dma_start(out_d[:, t, g * GROUP:(g + 1) * GROUP],
                             out_sb[:, t, g * GROUP:(g + 1) * GROUP]).then_inc(stored, 16)
            sp.wait_ge(stored, 16 * TILES * ROW_OUT)

        @block.gpsimd
        def _(pool):
            steps = Steps(pool, pool_step)
            steps.step(nc.gpsimd.memset(ident[:, :], 0.0))
            nc.gpsimd.affine_select(out=ident[:, :], in_=ident[:, :], compare_op=ALU.not_equal, fill=1.0, base=0,
                                    pattern=[[-1, P]], channel_multiplier=1).then_inc(masks_ready, 1)
            steps.step(nc.gpsimd.memset(upper[:, :], 1.0))
            nc.gpsimd.affine_select(out=upper[:, :], in_=upper[:, :], compare_op=ALU.is_ge, fill=0.0, base=0,
                                    pattern=[[1, P]], channel_multiplier=-1).then_inc(masks_ready, 1)
            steps.step(nc.gpsimd.memset(causal[:, :], 0.0))
            for at, n, base in ((0, P, 0), (P, 2 * P, P)):
                nc.gpsimd.affine_select(out=causal[:, at:at + n], in_=causal[:, at:at + n], compare_op=ALU.is_ge,
                                        fill=MASKED, base=base, pattern=[[-1, n]], channel_multiplier=1
                                        ).then_inc(masks_ready, 1)
            steps.step(nc.gpsimd.memset(selrow[:, :, :], 0.0))
            nc.gpsimd.affine_select(out=selrow[:, :, :], in_=selrow[:, :, :], compare_op=ALU.not_equal, fill=1.0,
                                    base=0, pattern=[[-1, ML_HEADS], [0, P]], channel_multiplier=1
                                    ).then_inc(masks_ready, 1)

            for b in range(8):
                pool.wait_ge(xhi_ready, b + 1)
                nc.gpsimd.tensor_tensor(xlo[:, 2 * b:2 * b + 2, :], turned[:, 2 * b:2 * b + 2, :],
                                        xhi[:, 2 * b:2 * b + 2, :].bitcast(F32), ALU.subtract).then_inc(xlo_ready, 1)

            pool.wait_ge(banks_free, 4 + 2 * PB.group0)
            pool.wait_ge(consts_landed, 6 * 16)

            def fetch_da(head, parts):
                for n in parts:
                    nc.gpsimd.tensor_copy((da_q, da_k, da_v)[n], area0[:, :, bass.ds(head * P + n * WIDTH, P)]
                                          ).then_inc(da_v_fetched if n == 2 else da_fetched, 1)

            for n, to in enumerate((da_q, da_k)):
                nc.gpsimd.tensor_copy(to, area0[:, :, n * WIDTH:n * WIDTH + P]).then_inc(da_fetched, 1)
            with pool.Fori(0, PB.turns) as i:
                for s in range(2):
                    h = i * 2 + s
                    pool.wait_ge(da_o_out, h + 1)
                    fetch_da(h, (2,))
                    pool.wait_ge(da_qkT_psum, h + 1)
                    fetch_da(h + 1, (0, 1))
                    pool.wait_ge(da_o_out, h + 2)
                    nc.gpsimd.tensor_tensor(da_sq, da_o, da_o, ALU.mult).then_inc(da_pool, 1)
                    nc.gpsimd.tensor_copy(area0[:, :, bass.ds(h * P, P)], da_o).then_inc(da_pool, 1)

            pool.wait_ge(banks_free, 4 + 2 * PC.group0)
            pool.wait_ge(da_fetched, 2 * (DA_HEADS + 1))
            pool.wait_ge(rows_copied, 4)
            conv_cols = cols[:, 0:40].rearrange("p (j a h) -> p a h j", a=2, h=ML_HEADS)
            with pool.Fori(0, PC.turns) as i:
                pool.wait_ge(units_done, PC.unit(i, 0))
                for a in range(2):
                    nc.gpsimd.tensor_copy(ml_qk[:, a, :, :], area1[:, :, bass.ds(i * P + a * 512, P)]
                                          ).then_inc(ml_fetched, 1)
                nc.gpsimd.tensor_copy(ml_v[:, :, 0:ML_V], area1[:, :, bass.ds(i * ML_V + WIDTH, ML_V)]
                                      ).then_inc(ml_fetched, 1)
                nc.gpsimd.tensor_copy(conv_h[:, :, :],
                                      conv_cols[:, :, bass.ds(i, 1), :].rearrange("p a h j -> p a (h j)")
                                      ).then_inc(ml_fetched, 1)
                nc.gpsimd.tensor_copy(acol_h, acol[:, :, bass.ds(i, 1)].rearrange("p t h -> p (t h)")
                                      ).then_inc(ml_fetched, 1)
                nc.gpsimd.tensor_copy(guard_h, guard[:, :, bass.ds(i, 1)].rearrange("p t h -> p (t h)")
                                      ).then_inc(ml_fetched, 1)
                pool.wait_ge(ya_ready, TILES * DA_HEADS)
                nc.gpsimd.tensor_copy(ya_blk[:, :, :], area0[:, :, bass.ds(i * 256 + 3 * WIDTH, 256)]
                                      ).then_inc(ya_fetched, 1)
                pool.wait_ge(ml_exp, i + 1)
                diagonals = ml_E.rearrange("p (c n) -> p c n", n=P)[:, 0:3:2, :]
                nc.gpsimd.tensor_tensor(diagonals, diagonals, upper[:, :].unsqueeze(1).broadcast_to([P, 2, P]),
                                        ALU.mult).then_inc(ml_E_ready, 1)
                pool.wait_ge(ml_h_ready, i * 2 + 4)
                nc.gpsimd.tensor_tensor(ml_sq, ml_h, ml_h, ALU.mult).then_inc(ml_pool, 1)
                nc.gpsimd.tensor_copy(area1[:, :, bass.ds(i * ML_V + WIDTH, ML_V)], ml_h).then_inc(ml_pool, 1)

            pool.wait_ge(banks_free, 4 + 2 * PP[0].group0)
            with pool.Fori(0, IDX_TURNS) as i:
                for s in range(4):
                    pool.wait_ge(units_done, PP[0].unit(i, 3 * s))
                    nc.gpsimd.tensor_copy(iq_sb, area0[:, :, bass.ds(i * 512 + (2048 + P * s), P)]
                                          ).then_inc(idx_fetched, 1)
                    pool.wait_ge(idx_added, i * 16 + (4 * s + 1))
                    nc.gpsimd.tensor_copy(iw_pair, small[:, :, bass.ds(i * 8 + (IW0 + 2 * s), 2)]
                                          ).then_inc(iw_fetched, 1)

            with pool.Fori(0, PP[1].turns) as i:
                for s in range(2):
                    h = i * 2 + s
                    pool.wait_ge(units_done, PP[1].unit(i, 6 * s))
                    nc.gpsimd.tensor_copy(dsa_q, area0[:, :, bass.ds(h * DSA_LATENT, DSA_LATENT)]
                                          ).then_inc(dsa_fetched, 1)

            pool.wait_ge(end_landed, 48)
            for n in range(TILES * ROW_OUT):
                t, g = n // ROW_OUT, n % ROW_OUT
                pool.wait_ge(y_scaled, n + 1)
                to = out_sb[:, t, g * GROUP:(g + 1) * GROUP]
                nc.gpsimd.tensor_tensor(to, to, x_again[:, t, g * GROUP:(g + 1) * GROUP], ALU.add).then_inc(y_final, 1)

        @block.scalar
        def _(act):
            def round_unit(part, i, k):
                n = k + AHEAD
                slot = (part.unit0 + n) % RING
                width = SMALL if part is PS and n < FULL_UNITS else GROUP
                act.wait_ge(raw_landed[slot], landed_count(part, i, n))
                if part.unit0 + n >= RING:
                    act.wait_ge(units_done, part.unit(i, n) - RING + 1)
                nc.scalar.activation(whi[:, slot, :, 0:width], raw[:, slot, :, 0:width], ACT.Copy
                                     ).then_inc(whi_ready, 1)

            def take_group(part, i, k_end, bank_pair, to, width=GROUP):
                act.wait_ge(units_done, part.unit(i, k_end))
                for t in range(TILES):
                    nc.scalar.activation(to[t], stream[bank_pair][t][:, 0:width], ACT.Copy, scale=rstdx[:, t:t + 1]
                                         ).then_inc(banks_free, 1)

            act.wait_ge(cols_turned, 1)
            nc.scalar.activation(cols[:, :], M[0][:, 0:56], ACT.Copy).then_inc(cols_ready, 1)
            for b in range(8):
                act.wait_ge(h_ready, 2 * b + 2)
                nc.scalar.activation(xhi[:, 2 * b:2 * b + 2, :], turned[:, 2 * b:2 * b + 2, :], ACT.Copy
                                     ).then_inc(xhi_ready, 1)
                for u in EARLY_UNITS.get(b, ()):
                    round_unit(PS, 0, u - AHEAD)
            for t in range(TILES):
                nc.scalar.activation(area1[:, t, 0:D_MODEL], x_sb[:, t, :], ACT.Square,
                                     accum_out=ssx[:, t:t + 1]).then_inc(ssx_ready, 1)
            act.wait_ge(msx_ready, 1)
            nc.scalar.activation(rstdx, rstdx, ACT.Sqrt).then_inc(stdx_ready, 1)

            for u in range(FULL_UNITS):
                round_unit(PS, 0, u)
            act.wait_ge(rstdx_ready, 2)
            take_group(PS, 0, FULL_UNITS, 0, [small[:, t, :] for t in range(TILES)], SMALL)
            act.wait_ge(lam_sum_ready, 2)
            nc.scalar.activation(lam2, lam2, ACT.Exp).then_inc(lam_exp_ready, 1)
            act.wait_ge(row_ready, 1)
            nc.scalar.activation(forget_t, forget_t, ACT.Exp).then_inc(row_act, 1)
            act.wait_ge(row_act, 1)
            nc.scalar.activation(forget_t, forget_t, ACT.Ln, bias=one).then_inc(row_act, 1)
            act.wait_ge(kv_ms_ready, 1)
            nc.scalar.activation(rstdkv[:, 0:4], rstdkv[:, 0:4], ACT.Sqrt).then_inc(kv_std_ready, 1)

            with act.Fori(0, PA.turns) as i:
                for g in range(2):
                    for u in range(FULL_UNITS):
                        round_unit(PA, i, g * FULL_UNITS + u)
                    take_group(PA, i, (g + 1) * FULL_UNITS, (PA.group0 + g) % 2,
                               [area0[:, t, bass.ds(i * 2 * GROUP + g * GROUP, GROUP)] for t in range(TILES)])

            act.wait_ge(prep_turned, 1)
            nc.scalar.activation(cT, M[0][:, :].rearrange("p (c s) -> p c s", c=2), ACT.Copy).then_inc(prep_copied, 1)
            act.wait_ge(prep_turned, 2)
            nc.scalar.activation(ikT, M[1][:, 0:SEQ], ACT.Copy).then_inc(prep_copied, 1)
            act.wait_ge(row_ready, 2)
            nc.scalar.activation(row_c, row_c, ACT.Exp, scale=-1.0).then_inc(row_act, 1)

            with act.Fori(0, PB.turns) as i:
                for s in range(2):
                    h = i * 2 + s
                    for u in range(FULL_UNITS):
                        round_unit(PB, i, s * FULL_UNITS + u)
                        if u == 1:
                            act.wait_ge(da_qkT_psum, h + 1)
                            nc.scalar.activation(da_qkT, M[0][:, :].rearrange("p (a s) -> p a s", a=2), ACT.Copy
                                                 ).then_inc(da_qkT_ready, 1)
                            nc.scalar.activation(da_sig, area0[:, :, bass.ds(h * P + 3 * WIDTH, P)], ACT.Tanh,
                                                 scale=0.5).then_inc(da_tz, 1)
                        if u == 3:
                            act.wait_ge(da_negmax, h * 2 + 2)
                            for t, a, n in ((0, 0, P), (1, P, 2 * P)):
                                for c in range(2):
                                    nc.scalar.activation(da_s[:, c, a:a + n], da_s[:, c, a:a + n], ACT.Exp,
                                                         bias=da_negmax_c[:, 2 * t + c:2 * t + c + 1],
                                                         accum_out=da_sum_c[:, 2 * t + c:2 * t + c + 1]
                                                         ).then_inc(da_exp, 1)
                        if u == 6:
                            act.wait_ge(da_aT_psum, h + 1)
                            nc.scalar.activation(da_aT, M[3][:, 0:3 * P], ACT.Copy).then_inc(da_aT_ready, 1)
                    take_group(PB, i, (s + 1) * FULL_UNITS, (PB.group0 + s) % 2,
                               [area1[:, t, bass.ds(i * 2 * GROUP + s * GROUP, GROUP)] for t in range(TILES)])

            for n in range(2):
                act.wait_ge(rows_turned, n + 1)
                nc.scalar.activation(ml_negM[:, 2 * n:2 * n + 2, :],
                                     M[n + 1][:, :].rearrange("p (h s) -> p h s", h=2), ACT.Copy
                                     ).then_inc(rows_copied, 1)
            act.wait_ge(rows_turned, 3)
            nc.scalar.activation(acol, M[3][:, 0:8].rearrange("p (t h) -> p t h", t=TILES), ACT.Copy
                                 ).then_inc(rows_copied, 1)
            nc.scalar.activation(guard, M[3][:, 8:16].rearrange("p (t h) -> p t h", t=TILES), ACT.Copy
                                 ).then_inc(rows_copied, 1)
            act.wait_ge(da_ms, 1)
            nc.scalar.activation(da_ss, da_ss, ACT.Sqrt).then_inc(da_std, 1)

            with act.Fori(0, PC.turns) as i:
                for v in range(2 * FULL_UNITS):
                    round_unit(PC, i, v)
                    if v == 1:
                        act.wait_ge(ml_T_psum, i + 1)
                        nc.scalar.activation(ml_xT[:, :, ML_CONV - 1:], M[0][:, :].rearrange("p (a s) -> p a s", a=2),
                                             ACT.Copy).then_inc(ml_xT_ready, 1)
                    if v == 4:
                        act.wait_ge(ml_conv, i + 1)
                        nc.scalar.activation(ml_sT, ml_cT, ACT.Tanh, scale=0.5).then_inc(ml_ts, 1)
                        act.wait_ge(ml_arg, i * 2 + 2)
                        nc.scalar.activation(ml_E, ml_E, ACT.Exp).then_inc(ml_exp, 1)
                    if v == 11:
                        act.wait_ge(ml_gated, i + 1)
                        nc.scalar.activation(ml_to, area1[:, :, bass.ds(i * ML_V + 2 * WIDTH, ML_V)], ACT.Tanh,
                                             scale=0.5).then_inc(ml_toz, 1)
                        nc.scalar.activation(ml_tz, area1[:, :, bass.ds(i * ML_V + 3 * WIDTH, ML_V)], ACT.Tanh,
                                             scale=0.5).then_inc(ml_toz, 1)
                    if v == 2:
                        act.wait_ge(ya_psum, i + 1)
                        nc.scalar.activation(yhi[:, bass.ds(i * 2, 2), :],
                                             M[2][:, :].rearrange("p (k s) -> p k s", k=2), ACT.Copy
                                             ).then_inc(yhi_ready, 1)
                    if v in (FULL_UNITS - 1, 2 * FULL_UNITS - 1):
                        g = v // FULL_UNITS
                        take_group(PC, i, (g + 1) * FULL_UNITS, (PC.group0 + g) % 2,
                                   [area0[:, t, bass.ds(i * 2 * GROUP + g * GROUP, GROUP)] for t in range(TILES)])
            act.wait_ge(ml_ms, 1)
            nc.scalar.activation(ml_ss, ml_ss, ACT.Sqrt).then_inc(ml_std, 1)

            def gates(part, i, n0):
                act.wait_ge(units_done, part.unit(i, FULL_UNITS))
                act.wait_ge(prod_ready, i * 2 + (2 * n0 + 2))
                for t in range(TILES):
                    nc.scalar.activation(sig[:, t, :], stream[part.group0 % 2][t][:, :], ACT.Tanh,
                                         scale=half_rstdx[:, t:t + 1]).then_inc(gate_tanh, 1)

            act.wait_ge(yb_ready, ML_HEADS * TILES)
            with act.Fori(0, IDX_TURNS) as i:
                for v in range(PAIR_UNITS):
                    round_unit(PP[0], i, v)
                    s, u = v // 3, v % 3
                    p = i * 4 + s
                    if u == 0:
                        act.wait_ge(idx_T_psum, p + 1)
                        nc.scalar.activation(iqT, M[0][:, 0:SEQ], ACT.Copy).then_inc(iqT_ready, 1)
                    if u == 2:
                        act.wait_ge(idx_added, p * 4 + 1)
                        act.wait_ge(idx_scores, p + 1)
                        for e in range(2):
                            nc.scalar.activation(idx_relu[:, e, :], M[1 + e][:, 0:3 * P], ACT.Relu
                                                 ).then_inc(idx_relu_ready, 1)
                    if v == FULL_UNITS - 1:
                        gates(PP[0], i, 0)
            with act.Fori(IDX_TURNS, PP[0].turns) as i:
                for v in range(PAIR_UNITS):
                    round_unit(PP[0], i, v)
                    if v == FULL_UNITS - 1:
                        gates(PP[0], i, 0)

            def turn_y(n):
                for b in range(4):
                    act.wait_ge(y_psum, 4 * n + b + 1)
                    nc.scalar.activation(yhi[:, 2 * b:2 * b + 2, :], M[b][:, :].rearrange("p (k s) -> p k s", k=2),
                                         ACT.Copy).then_inc(yhi_ready, 1)

            act.wait_ge(units_done, PP[1].unit0)
            turn_y(0)

            with act.Fori(0, PP[1].turns) as i:
                for v in range(PAIR_UNITS):
                    round_unit(PP[1], i, v)
                    s, u = v // 6, v % 6
                    h = i * 2 + s
                    if u == 0:
                        act.wait_ge(dsa_T_psum, h + 1)
                        nc.scalar.activation(dsa_qT, M[0][:, :].rearrange("p (c s) -> p c s", c=2), ACT.Copy
                                             ).then_inc(dsa_qT_ready, 1)
                    if u == 2:
                        act.wait_ge(dsa_negmax, h * 2 + 2)
                        for t, a, n in ((0, 0, P), (1, P, 2 * P)):
                            nc.scalar.activation(dsa_s[:, a:a + n], dsa_s[:, a:a + n], ACT.Exp,
                                                 bias=dsa_negmax_c[:, t:t + 1], accum_out=dsa_sum_c[:, t:t + 1]
                                                 ).then_inc(dsa_exp, 1)
                        act.wait_ge(dsa_y, h * 2 + 1)
                        nc.scalar.activation(dsa_sig, area0[:, :, bass.ds(h * P + 3 * WIDTH, P)], ACT.Tanh,
                                             scale=0.5).then_inc(dsa_tz, 1)
                    if u == 3:
                        act.wait_ge(dsa_pT_psum, h + 1)
                        nc.scalar.activation(dsa_pT, M[2][:, 0:3 * P], ACT.Copy).then_inc(dsa_pT_ready, 1)
                    if u == 4:
                        act.wait_ge(dsa_ob, h + 1)
                        nc.scalar.activation(dsa_obT, M[3][:, :].rearrange("p (c s) -> p c s", c=2), ACT.Copy
                                             ).then_inc(dsa_ob_ready, 1)
                    if v == FULL_UNITS - 1:
                        gates(PP[1], i, 4)
            act.wait_ge(units_done, PP[2].unit0)
            turn_y(1)

            with act.Fori(0, PP[2].turns) as i:
                for v in range(PAIR_UNITS):
                    round_unit(PP[2], i, v)
                    if v == FULL_UNITS - 1:
                        gates(PP[2], i, 8)

            for b in range(8):
                act.wait_ge(merged_psum, b + 1)
                nc.scalar.activation(xhi[:, 2 * b:2 * b + 2, :], merge_banks[b][:, :].rearrange("p (k s) -> p k s", k=2),
                                     ACT.Copy).then_inc(merged_hi, 1)

            for g in range(ROW_OUT):
                for u in range(FULL_UNITS):
                    if PO.unit0 + g * FULL_UNITS + u + AHEAD < ALL_UNITS:
                        round_unit(PO, 0, g * FULL_UNITS + u)
                act.wait_ge(units_done, PO.unit0 + (g + 1) * FULL_UNITS)
                pair = stream[out_pair(g)]
                for t in range(TILES):
                    nc.scalar.activation(mixed[:, t, 0:GROUP], pair[t][:, :], ACT.Square,
                                         accum_out=sso[:, t, g:g + 1]).then_inc(out_ss, 1)
                    nc.scalar.activation(out_sb[:, t, g * GROUP:(g + 1) * GROUP], pair[t][:, :], ACT.Copy
                                         ).then_inc(out_copied, 1)
            act.wait_ge(out_ms, 1)
            nc.scalar.activation(rstdo, rstdo, ACT.Sqrt).then_inc(out_std, 1)

        @block.vector
        def _(dve):
            steps = Steps(dve, dve_step)

            def split_unit(part, i, k):
                n = k + AHEAD
                slot = (part.unit0 + n) % RING
                width = SMALL if part is PS and n < FULL_UNITS else GROUP
                dve.wait_ge(whi_ready, part.unit(i, n) + 1)
                nc.vector.tensor_tensor(wlo[:, slot, :, 0:width], raw[:, slot, :, 0:width],
                                        whi[:, slot, :, 0:width].bitcast(F32), ALU.subtract).then_inc(wlo_ready, 1)

            nc.vector.memset(spare[0], 0.0).then_inc(banks_free, 4)
            nc.vector.memset(spare[1], 0.0).then_inc(da_o_out, 1)
            nc.vector.memset(spare[2], 0.0).then_inc(ml_h_ready, 2)
            nc.vector.memset(spare[3], 0.0).then_inc(ml_gated, 1)
            nc.vector.memset(spare[4], 0.0).then_inc(ylo_ready, 1)
            nc.vector.memset(spare[6], 0.0).then_inc(dsa_y, 1)
            nc.vector.memset(spare[7], 0.0).then_inc(gate_tanh, 2)
            nc.vector.memset(spare[8], 0.0).then_inc(prod_ready, 2)
            steps.step(nc.vector.memset(one, 1.0))

            dve.wait_ge(cols_ready, 1)
            for b in range(8):
                dve.wait_ge(x_turned, b + 1)
                for k in range(2 * b, 2 * b + 2):
                    nc.vector.tensor_scalar(turned[:, k, :], banks[b][:, (k % 2) * SEQ:(k % 2 + 1) * SEQ],
                                            cols[:, 40 + k:41 + k], None, ALU.mult).then_inc(h_ready, 1)
                for u in EARLY_UNITS.get(b, ()):
                    split_unit(PS, 0, u - AHEAD)
            dve.wait_ge(ssx_ready, 2)
            nc.vector.tensor_scalar(rstdx, ssx, 1.0 / D_MODEL, EPS, ALU.mult, ALU.add).then_inc(msx_ready, 1)
            dve.wait_ge(stdx_ready, 1)
            nc.vector.reciprocal(rstdx, rstdx).then_inc(rstdx_ready, 1)
            dve.wait_ge(rstdx_ready, 1)
            nc.vector.tensor_scalar(half_rstdx, rstdx, 0.5, None, ALU.mult).then_inc(rstdx_ready, 1)

            for u in range(FULL_UNITS):
                split_unit(PS, 0, u)
            dve.wait_ge(consts_landed, 6 * 16)
            dve.wait_ge(banks_free, 4 + 2 * PA.group0)
            for t in range(TILES):
                last = nc.vector.tensor_tensor(gate_in[:, t, :], small[:, t, IF0:IF0 + 2 * ML_HEADS], gate_b[:, :],
                                               ALU.add)
            steps.step(last)
            steps.step(nc.vector.tensor_scalar(forget_t, gate_in[:, :, ML_HEADS:], -1.0, None, ALU.mult))
            nc.vector.tensor_tensor(forget_t, gate_in[:, :, ML_HEADS:], forget_t, ALU.min).then_inc(row_ready, 1)
            steps.step(nc.vector.tensor_tensor(lam_in[:, 0:4:2, :], lam_in[:, 0:4:2, :], lam_in[:, 1:4:2, :],
                                               ALU.mult))
            for n in range(2):
                nc.vector.tensor_reduce(lam2[:, n:n + 1], lam_in[:, 2 * n, :], AX.X, ALU.add).then_inc(lam_sum_ready, 1)
            dve.wait_ge(lam_exp_ready, 1)
            steps.step(nc.vector.tensor_tensor(neglam, lam2[:, 1:2], lam2[:, 0:1], ALU.subtract))
            steps.step(nc.vector.tensor_scalar(neglam, neglam, LAM_INIT, None, ALU.subtract))
            junk = view(scratch, 0, TILES, DSA_LATENT)
            junk2 = view(scratch, 512, TILES, IDX_DIM)
            steps.step(nc.vector.tensor_tensor(junk, small[:, :, KV0:KV0 + DSA_LATENT],
                                               small[:, :, KV0:KV0 + DSA_LATENT], ALU.mult))
            steps.step(nc.vector.tensor_tensor(junk2, small[:, :, IK0:IK0 + IDX_DIM],
                                               small[:, :, IK0:IK0 + IDX_DIM], ALU.mult))
            steps.step(nc.vector.tensor_reduce(sskv[:, 0:2], junk, AX.X, ALU.add))
            steps.step(nc.vector.tensor_reduce(sskv[:, 2:4], junk2, AX.X, ALU.add))
            steps.step(nc.vector.tensor_scalar(rstdkv[:, 0:2], sskv[:, 0:2], 1.0 / DSA_LATENT, EPS, ALU.mult, ALU.add))
            nc.vector.tensor_scalar(rstdkv[:, 2:4], sskv[:, 2:4], 1.0 / IDX_DIM, EPS, ALU.mult, ALU.add
                                    ).then_inc(kv_ms_ready, 1)
            dve.wait_ge(kv_std_ready, 1)
            steps.step(nc.vector.reciprocal(rstdkv, rstdkv))
            for t in range(TILES):
                nc.vector.scalar_tensor_tensor(c_sb[:, t, :], small[:, t, KV0:KV0 + DSA_LATENT], rstdkv[:, t:t + 1],
                                               kv_g[:, :], ALU.mult, ALU.mult).then_inc(kv_normed, 1)
                for n in range(2):
                    nc.vector.scalar_tensor_tensor(ik2[:, t, n * IDX_DIM:(n + 1) * IDX_DIM],
                                                   small[:, t, IK0:IK0 + IDX_DIM], rstdkv[:, 2 + t:3 + t],
                                                   ik_g[:, :], ALU.mult, ALU.mult).then_inc(kv_normed, 1)
            steps.step(nc.vector.tensor_scalar(small[:, :, IW0:IW0 + IDX_HEADS], small[:, :, IW0:IW0 + IDX_HEADS],
                                               IDX_HEADS ** -0.5 * IDX_DIM ** -0.5, None, ALU.mult))
            dve.wait_ge(row_act, 2)
            nc.vector.scalar_tensor_tensor(gate_in[:, :, ML_HEADS:], gate_in[:, :, ML_HEADS:], 0.0, forget_t,
                                           ALU.min, ALU.subtract).then_inc(kv_normed, 1)

            with dve.Fori(0, PA.turns) as i:
                for k in range(2 * FULL_UNITS):
                    split_unit(PA, i, k)

            dve.wait_ge(prep_turned, 3)
            steps.step(nc.vector.memset(row_one, 1.0))
            steps.step(nc.vector.tensor_tensor_scan(row_c, row_one, M[2][0:ML_HEADS, SEQ:2 * SEQ], 0.0, ALU.mult, ALU.add))
            steps.step(nc.vector.tensor_tensor(row_a, M[2][0:ML_HEADS, 0:SEQ], row_c, ALU.subtract))
            steps.step(nc.vector.tensor_tensor_scan(row_b, row_a, row_a, 0.0, ALU.max, ALU.max))
            steps.step(nc.vector.tensor_scalar(row_negM, row_b, -1.0, None, ALU.mult))
            nc.vector.tensor_tensor(row_c, row_c, row_b, ALU.add).then_inc(row_ready, 1)

            dve.wait_ge(masks_ready, 5)
            with dve.Fori(0, PB.turns) as i:
                steps.enter(i, 2 * 8)
                for s in range(2):
                    h = i * 2 + s
                    for u in range(FULL_UNITS):
                        split_unit(PB, i, s * FULL_UNITS + u)
                        if u == 1:
                            dve.wait_ge(da_tz, h + 1)
                            z = area0[:, :, bass.ds(h * P + 3 * WIDTH, P)]
                            steps.step(nc.vector.scalar_tensor_tensor(da_sig, da_sig, 1.0, z, ALU.add, ALU.mult))
                            nc.vector.tensor_tensor(z, da_sig, da_g[:, :].unsqueeze(1).broadcast_to([P, TILES, P]),
                                                    ALU.mult)
                        if u == 2:
                            dve.wait_ge(da_scores, h + 1)
                            for c in range(2):
                                steps.step(nc.vector.scalar_tensor_tensor(da_s[:, c, :], M[1 + c][:, 0:3 * P],
                                                                          DA_DIM ** -0.5, causal[:, :], ALU.mult,
                                                                          ALU.add))
                            for t, a, n in ((0, 0, P), (1, P, 2 * P)):
                                nc.vector.tensor_reduce(da_negmax_c[:, 2 * t:2 * t + 2], da_s[:, :, a:a + n], AX.X,
                                                        ALU.max, negate=True).then_inc(da_negmax, 1)
                        if u == 4:
                            dve.wait_ge(da_exp, h * 4 + 4)
                            steps.step(nc.vector.reciprocal(da_rsum_c, da_sum_c))
                            steps.step(nc.vector.tensor_scalar(da_rsum_c[:, 1:4:2], da_rsum_c[:, 1:4:2], neglam, None,
                                                               ALU.mult))
                            for t, a, n in ((0, 0, P), (1, P, 2 * P)):
                                steps.step(nc.vector.tensor_scalar(da_a[:, a:a + n], da_s[:, 0, a:a + n],
                                                                   da_rsum_c[:, 2 * t:2 * t + 1], None, ALU.mult))
                                nc.vector.scalar_tensor_tensor(da_a[:, a:a + n], da_s[:, 1, a:a + n],
                                                               da_rsum_c[:, 2 * t + 1:2 * t + 2], da_a[:, a:a + n],
                                                               ALU.mult, ALU.add).then_inc(da_attn, 1)
                        if u == 7:
                            dve.wait_ge(da_av, h + 1)
                            nc.vector.tensor_copy(da_o, M[0][:, 0:SEQ].rearrange("p (t v) -> p t v", t=TILES)
                                                  ).then_inc(da_o_out, 1)
                            dve.wait_ge(da_pool, h * 2 + 2)
                            steps.step(nc.vector.tensor_reduce(da_ss[:, bass.ds(h, 1), :].rearrange("p h t -> p (h t)"),
                                                               da_sq, AX.X, ALU.add))
                steps.leave(PB.turns)
            nc.vector.tensor_scalar(da_ss, da_ss, 1.0 / DA_V, EPS, ALU.mult, ALU.add).then_inc(da_ms, 1)
            dve.wait_ge(da_std, 1)
            steps.step(nc.vector.reciprocal(da_ss, da_ss))
            steps.step(nc.vector.tensor_scalar(da_ss, da_ss, 0.25 * (1.0 - LAM_INIT), None, ALU.mult))
            for h in range(DA_HEADS):
                for t in range(TILES):
                    z = area0[:, t, 3 * WIDTH + h * P:3 * WIDTH + (h + 1) * P]
                    nc.vector.scalar_tensor_tensor(z, area0[:, t, h * P:(h + 1) * P], da_ss[:, h, t:t + 1], z,
                                                   ALU.mult, ALU.mult).then_inc(ya_ready, 1)
            dve.wait_ge(ya_ready, TILES * DA_HEADS)
            nc.vector.memset(ml_xT[:, :, 0:ML_CONV - 1], 0.0)
            steps.step(nc.vector.memset(ml_v[:, :, ML_V:ML_V + 1], 1.0))

            dve.wait_ge(rows_copied, 4)
            with dve.Fori(0, PC.turns) as i:
                steps.enter(i, 11)
                for v in range(2 * FULL_UNITS):
                    split_unit(PC, i, v)
                    if v == 2:
                        dve.wait_ge(ml_xT_ready, i + 1)
                        dve.wait_ge(ml_fetched, i * 6 + 6)
                        for j in range(ML_CONV):
                            for a in range(2):
                                x_j = ml_xT[:, a, j:j + SEQ]
                                if j == 0:
                                    last = nc.vector.tensor_scalar(ml_cT[:, a, :], x_j, conv_h[:, a, 0:1],
                                                                   conv_h[:, a, 4:5], ALU.mult, ALU.add)
                                else:
                                    last = nc.vector.scalar_tensor_tensor(ml_cT[:, a, :], x_j, conv_h[:, a, j:j + 1],
                                                                          ml_cT[:, a, :], ALU.mult, ALU.add)
                            if j < ML_CONV - 1:
                                steps.step(last)
                        last.then_inc(ml_conv, 1)
                    if v == 3:
                        nc.vector.tensor_scalar(ml_E[:, 0:SEQ], ml_negM[:, bass.ds(i, 1), :].rearrange("p h s -> p (h s)"),
                                                acol_h[:, 0:1], 0.0, ALU.add, ALU.min).then_inc(ml_arg, 1)
                        nc.vector.tensor_scalar(ml_E[:, SEQ:], ml_negM[:, bass.ds(i, 1), P:].rearrange("p h s -> p (h s)"),
                                                acol_h[:, 1:2], 0.0, ALU.add, ALU.min).then_inc(ml_arg, 1)
                        dve.wait_ge(ya_psum, i + 1)
                        dve.wait_ge(yhi_ready, i + 1)
                        nc.vector.tensor_tensor(ylo[:, bass.ds(i * 2, 2), :],
                                                M[2][:, :].rearrange("p (k s) -> p k s", k=2),
                                                yhi[:, bass.ds(i * 2, 2), :].bitcast(F32), ALU.subtract
                                                ).then_inc(ylo_ready, 1)
                    if v == 5:
                        dve.wait_ge(ml_ts, i + 1)
                        nc.vector.scalar_tensor_tensor(ml_cT, ml_sT, 1.0, ml_cT, ALU.add, ALU.mult
                                                       ).then_inc(ml_cT_ready, 1)
                    if v == 8:
                        dve.wait_ge(ml_scores, i + 1)
                        dve.wait_ge(ml_E_ready, i + 1)
                        nc.vector.scalar_tensor_tensor(ml_w, M[1][:, 0:3 * P], 0.25 * ML_QK ** -0.5, ml_E, ALU.mult, ALU.mult
                                                       ).then_inc(ml_w_ready, 1)
                    if v == 10:
                        dve.wait_ge(ml_num, i + 1)
                        for t in range(TILES):
                            total = M[2 + t][:, ML_V:ML_V + 1]
                            steps.step(nc.vector.tensor_scalar(den[:, t:t + 1], total, -1.0, guard_h[:, t:t + 1],
                                                               ALU.mult, ALU.max))
                            steps.step(nc.vector.tensor_scalar(den[:, t:t + 1], total, den[:, t:t + 1], None,
                                                               ALU.max))
                        steps.step(nc.vector.reciprocal(rden, den))
                        for t in range(TILES):
                            nc.vector.tensor_scalar(ml_h[:, t, :], M[2 + t][:, 0:ML_V], rden[:, t:t + 1], None,
                                                    ALU.mult).then_inc(ml_h_ready, 1)
                    if v == 12:
                        dve.wait_ge(ml_toz, i * 2 + 2)
                        z = area1[:, :, bass.ds(i * ML_V + 3 * WIDTH, ML_V)]
                        steps.step(nc.vector.scalar_tensor_tensor(ml_to, ml_to, 1.0, z, ALU.add, ALU.mult))
                        steps.step(nc.vector.scalar_tensor_tensor(ml_tz, ml_tz, 1.0, ml_to, ALU.add, ALU.mult))
                        nc.vector.tensor_tensor(z, ml_tz, ml_g[:, :].unsqueeze(1).broadcast_to([P, TILES, ML_V]),
                                                ALU.mult).then_inc(ml_gated, 1)
                    if v == 15:
                        dve.wait_ge(ml_pool, i * 2 + 2)
                        steps.step(nc.vector.tensor_reduce(ml_ss[:, bass.ds(i, 1), :].rearrange("p h t -> p (h t)"),
                                                           ml_sq, AX.X, ALU.add))
                steps.leave(PC.turns)
            nc.vector.tensor_scalar(ml_ss, ml_ss, 1.0 / ML_V, EPS, ALU.mult, ALU.add).then_inc(ml_ms, 1)
            dve.wait_ge(ml_std, 1)
            steps.step(nc.vector.reciprocal(ml_ss, ml_ss))
            steps.step(nc.vector.tensor_scalar(ml_ss, ml_ss, 0.125, None, ALU.mult))
            for h in range(ML_HEADS):
                for t in range(TILES):
                    z = area1[:, t, 3 * WIDTH + h * ML_V:3 * WIDTH + (h + 1) * ML_V]
                    nc.vector.scalar_tensor_tensor(z, area1[:, t, WIDTH + h * ML_V:WIDTH + (h + 1) * ML_V],
                                                   ml_ss[:, h, t:t + 1], z, ALU.mult, ALU.mult).then_inc(yb_ready, 1)
            dve.wait_ge(yb_ready, ML_HEADS * TILES)

            def gate_branch(part, i, n0):
                dve.wait_ge(units_done, part.unit(i, PAIR_UNITS))
                dve.wait_ge(gate_tanh, i * 2 + (2 * n0 + 4))
                for t in range(TILES):
                    columns = mixed[:, t, bass.ds(i * GROUP, GROUP)]
                    nc.vector.scalar_tensor_tensor(prod[:, t, :] if n0 else columns, sig[:, t, :], 1.0,
                                                   stream[(part.group0 + 1) % 2][t][:, :], ALU.add, ALU.mult
                                                   ).then_inc(prod_ready, 1)
                if n0:
                    for t in range(TILES):
                        dve.wait_ge(prod_ready, i * 2 + (2 * n0 + t + 3))
                        columns = mixed[:, t, bass.ds(i * GROUP, GROUP)]
                        nc.vector.tensor_tensor(columns, columns, prod[:, t, :], ALU.add).then_inc(mixed_added, 1)

            nc.vector.tensor_copy(idx_acc, causal[:, :]).then_inc(idx_added, 1)
            with dve.Fori(0, IDX_TURNS) as i:
                for v in range(PAIR_UNITS):
                    split_unit(PP[0], i, v)
                    s, u = v // 3, v % 3
                    p = i * 4 + s
                    if u == 2:
                        dve.wait_ge(idx_relu_ready, p * 2 + 2)
                        dve.wait_ge(iw_fetched, p + 1)
                        for e in range(2):
                            dve.wait_ge(idx_added, p * 4 + (2 * e + 1))
                            for t, a, n in ((0, 0, P), (1, P, 2 * P)):
                                nc.vector.scalar_tensor_tensor(idx_acc[:, a:a + n], idx_relu[:, e, a:a + n],
                                                               iw_pair[:, t, e:e + 1], idx_acc[:, a:a + n],
                                                               ALU.mult, ALU.add).then_inc(idx_added, 1)
                gate_branch(PP[0], i, 0)
            dve.wait_ge(idx_added, 1 + 4 * IDX_HEADS // 2)
            rounds = TOPK // 8 // (PP[0].turns - IDX_TURNS)

            def carry_wait():
                nc.vector.tensor_copy(wait_carrier, causal[:, 0:1])

            with dve.Fori(IDX_TURNS, PP[0].turns) as i:
                steps.enter(i - IDX_TURNS, 2 * rounds)
                for v in range(PAIR_UNITS):
                    split_unit(PP[0], i, v)
                    if v % 2 == 1 and v // 2 < rounds:
                        carry_wait()
                        for t, a, n in ((0, 0, P), (1, P, 2 * P)):
                            last = nc.vector.max(top8[:, t, :], idx_acc[:, a:a + n])
                        steps.step(last)
                        carry_wait()
                        for t, a, n in ((0, 0, P), (1, P, 2 * P)):
                            last = nc.vector.match_replace(idx_acc[:, a:a + n], top8[:, t, :], idx_acc[:, a:a + n],
                                                           TAKEN)
                        steps.step(last)
                gate_branch(PP[0], i, 0)
                steps.leave(PP[0].turns - IDX_TURNS)
            dve.wait_ge(prod_ready, 2 + 2 * PP[0].turns)

            def turn_y(n):
                for b in range(4):
                    dve.wait_ge(yhi_ready, 4 + 4 * n + b + 1)
                    nc.vector.tensor_tensor(ylo[:, 2 * b:2 * b + 2, :], M[b][:, :].rearrange("p (k s) -> p k s", k=2),
                                            yhi[:, 2 * b:2 * b + 2, :].bitcast(F32), ALU.subtract
                                            ).then_inc(ylo_ready, 1)

            turn_y(0)
            steps.step(nc.vector.tensor_scalar(select, idx_acc, 0.5 * (MASKED + TAKEN), MASKED, ALU.is_gt, ALU.mult))
            steps.step(nc.vector.tensor_tensor(select, select, causal[:, :], ALU.min))

            with dve.Fori(0, PP[1].turns) as i:
                steps.enter(i, 2 * 4)
                for v in range(PAIR_UNITS):
                    split_unit(PP[1], i, v)
                    s, u = v // 6, v % 6
                    h = i * 2 + s
                    if u == 1:
                        dve.wait_ge(dsa_logits, h + 1)
                        steps.step(nc.vector.scalar_tensor_tensor(dsa_s, M[1][:, 0:3 * P], DSA_LATENT ** -0.5, select,
                                                                  ALU.mult, ALU.add))
                        for t, a, n in ((0, 0, P), (1, P, 2 * P)):
                            nc.vector.tensor_reduce(dsa_negmax_c[:, t:t + 1], dsa_s[:, a:a + n], AX.X, ALU.max,
                                                    negate=True).then_inc(dsa_negmax, 1)
                    if u == 2:
                        dve.wait_ge(dsa_exp, h * 2 + 2)
                        steps.step(nc.vector.reciprocal(dsa_rsum_c, dsa_sum_c))
                        steps.step(nc.vector.tensor_scalar(dsa_rsum_c, dsa_rsum_c, 0.25, None, ALU.mult))
                        dve.wait_ge(dsa_tz, h + 1)
                        steps.step(nc.vector.scalar_tensor_tensor(dsa_sig, dsa_sig, 1.0,
                                                                  area0[:, :, bass.ds(h * P + 3 * WIDTH, P)],
                                                                  ALU.add, ALU.mult))
                    if u == 5:
                        dve.wait_ge(dsa_out, h + 1)
                        for t in range(TILES):
                            nc.vector.scalar_tensor_tensor(area0[:, t, bass.ds(h * P + 3 * WIDTH, P)],
                                                           M[2][:, t * P:(t + 1) * P], dsa_rsum_c[:, t:t + 1],
                                                           dsa_sig[:, t, :], ALU.mult, ALU.mult).then_inc(dsa_y, 1)
                gate_branch(PP[1], i, 4)
                steps.leave(PP[1].turns)
            turn_y(1)

            dve.wait_ge(mixed_added, 2 * PP[1].turns)
            with dve.Fori(0, PP[2].turns) as i:
                for v in range(PAIR_UNITS):
                    split_unit(PP[2], i, v)
                gate_branch(PP[2], i, 8)

            for b in range(8):
                dve.wait_ge(merged_hi, b + 1)
                nc.vector.tensor_tensor(xlo[:, 2 * b:2 * b + 2, :],
                                        merge_banks[b][:, :].rearrange("p (k s) -> p k s", k=2),
                                        xhi[:, 2 * b:2 * b + 2, :].bitcast(F32), ALU.subtract).then_inc(merged_lo, 1)
            for k in range(PO.units - AHEAD):
                split_unit(PO, 0, k)
            dve.wait_ge(out_ss, TILES * ROW_OUT)
            steps.step(nc.vector.tensor_reduce(rstdo, sso, AX.X, ALU.add))
            nc.vector.tensor_scalar(rstdo, rstdo, 1.0 / D_MODEL, EPS, ALU.mult, ALU.add).then_inc(out_ms, 1)
            dve.wait_ge(out_std, 1)
            dve.wait_ge(end_landed, 48)
            dve.wait_ge(out_copied, TILES * ROW_OUT)
            steps.step(nc.vector.reciprocal(rstdo, rstdo))
            for n in range(TILES * ROW_OUT):
                t, g = n // ROW_OUT, n % ROW_OUT
                to = out_sb[:, t, g * GROUP:(g + 1) * GROUP]
                nc.vector.scalar_tensor_tensor(to, to, rstdo[:, t:t + 1], post_g[:, g * GROUP:(g + 1) * GROUP],
                                               ALU.mult, ALU.mult).then_inc(y_scaled, 1)

        @block.tensor
        def _(pe):
            def multiply(part, i, k, u, units, bank_pair, left_hi, left_lo, width=GROUP):
                slot = (part.unit0 + k) % RING
                pe.wait_ge(wlo_ready, part.unit(i, k) + 1)
                for j in range(UNIT_KT):
                    kt = UNIT_KT * u + j
                    first, final = kt == 0, kt == UNIT_KT * units - 1
                    for t in range(TILES):
                        to = stream[bank_pair][t][:, 0:width]
                        tokens = slice(t * P, (t + 1) * P)
                        high, low = whi[:, slot, j, 0:width], wlo[:, slot, j, 0:width]
                        nc.tensor.matmul(to, left_hi[:, kt, tokens], high, start=first, stop=False)
                        nc.tensor.matmul(to, left_hi[:, kt, tokens], low, start=False, stop=False)
                        last = nc.tensor.matmul(to, left_lo[:, kt, tokens], high, start=False, stop=final)
                last.then_inc(units_done, 1)

            def open_banks(part, i, k):
                pe.wait_ge(banks_free, i * (2 * part.groups) + (2 * (part.group0 + k) + 2))

            pe.wait_ge(masks_ready, 1)
            pe.wait_ge(rows_landed, 3 * 16)
            nc.tensor.transpose(M[0][:, 0:56], rows[:, :], ident[0:56, 0:56]).then_inc(cols_turned, 1)

            def turn_x(b):
                if b % 2 == 0:
                    pe.wait_ge(x_landed[b // 2], 16)
                if b == 4:
                    pe.wait_ge(cols_ready, 1)
                for j in range(2):
                    for t in range(TILES):
                        kt = 2 * b + j
                        last = nc.tensor.transpose(banks[b][:, j * SEQ + t * P:j * SEQ + (t + 1) * P],
                                                   x_sb[:, t, kt * P:(kt + 1) * P], ident[:, :])
                last.then_inc(x_turned, 1)

            for b in range(8):
                turn_x(b)
            pe.wait_ge(h_ready, 4)
            for u in range(FULL_UNITS):
                pe.wait_ge(xlo_ready, u + 1)
                multiply(PS, 0, u, u, FULL_UNITS, 0, xhi, xlo, SMALL)
            with pe.Fori(0, PA.turns) as i:
                for g in range(2):
                    open_banks(PA, i, g)
                    for u in range(FULL_UNITS):
                        multiply(PA, i, g * FULL_UNITS + u, u, FULL_UNITS, (PA.group0 + g) % 2, xhi, xlo)

            pe.wait_ge(kv_normed, 7)
            for c in range(2):
                for t in range(TILES):
                    last = nc.tensor.transpose(M[0][:, c * SEQ + t * P:c * SEQ + (t + 1) * P],
                                               c_sb[:, t, c * P:(c + 1) * P], ident[:, :])
            last.then_inc(prep_turned, 1)
            for t in range(TILES):
                last = nc.tensor.transpose(M[1][:, t * P:(t + 1) * P], ik2[:, t, :], ident[:, :])
            last.then_inc(prep_turned, 1)
            for e in range(2):
                for t in range(TILES):
                    last = nc.tensor.transpose(M[2][0:ML_HEADS, e * SEQ + t * P:e * SEQ + (t + 1) * P],
                                               gate_in[:, t, e * ML_HEADS:(e + 1) * ML_HEADS], ident[:, :])
            last.then_inc(prep_turned, 1)

            pe.wait_ge(prep_copied, 2)
            with pe.Fori(0, PB.turns) as i:
                for s in range(2):
                    h = i * 2 + s
                    open_banks(PB, i, s)
                    for u in range(FULL_UNITS):
                        multiply(PB, i, s * FULL_UNITS + u, u, FULL_UNITS, (PB.group0 + s) % 2, xhi, xlo)
                        if u == 1:
                            pe.wait_ge(da_fetched, h * 2 + 2)
                            pe.wait_ge(da_o_out, h + 1)
                            for n, of in enumerate((da_q, da_k)):
                                for t in range(TILES):
                                    last = nc.tensor.transpose(M[0][:, n * SEQ + t * P:n * SEQ + (t + 1) * P],
                                                               of[:, t, :], ident[:, :])
                            last.then_inc(da_qkT_psum, 1)
                        if u == 2:
                            pe.wait_ge(da_qkT_ready, h + 1)
                            pe.wait_ge(row_act, 3)
                            for c in range(2):
                                d = slice(c * DA_DIM, (c + 1) * DA_DIM)
                                nc.tensor.matmul(M[1 + c][:, 0:P], da_qkT[d, 0, 0:P], da_qkT[d, 1, 0:P],
                                                 start=True, stop=True)
                                last = nc.tensor.matmul(M[1 + c][:, P:3 * P], da_qkT[d, 0, P:], da_qkT[d, 1, :],
                                                        start=True, stop=True)
                            last.then_inc(da_scores, 1)
                        if u == 6:
                            pe.wait_ge(da_attn, h * 2 + 2)
                            for b in range(3):
                                last = nc.tensor.transpose(M[3][:, b * P:(b + 1) * P], da_a[:, b * P:(b + 1) * P],
                                                           ident[:, :])
                            last.then_inc(da_aT_psum, 1)
                        if u == 7:
                            pe.wait_ge(da_v_fetched, h + 1)
                            pe.wait_ge(da_aT_ready, h + 1)
                            nc.tensor.matmul(M[0][:, 0:P], da_aT[:, 0:P], da_v[:, 0, :], start=True, stop=True)
                            for t in range(TILES):
                                last = nc.tensor.matmul(M[0][:, P:2 * P], da_aT[:, (1 + t) * P:(2 + t) * P],
                                                        da_v[:, t, :], start=(t == 0), stop=(t == 1))
                            last.then_inc(da_av, 1)

            for n in range(2):
                for e in range(2):
                    last = nc.tensor.matmul(M[n + 1][:, e * SEQ:(e + 1) * SEQ], selrow[:, 2 * n + e, :], row_negM,
                                            start=True, stop=True)
                last.then_inc(rows_turned, 1)
            for n, row in enumerate((row_a, row_c)):
                for t in range(TILES):
                    last = nc.tensor.transpose(M[3][:, 8 * n + ML_HEADS * t:8 * n + ML_HEADS * (t + 1)],
                                               row[:, t * P:(t + 1) * P], ident[0:ML_HEADS, 0:ML_HEADS])
            last.then_inc(rows_turned, 1)

            with pe.Fori(0, PC.turns) as i:
                for v in range(2 * FULL_UNITS):
                    g, u = v // FULL_UNITS, v % FULL_UNITS
                    if u == 0:
                        open_banks(PC, i, g)
                    multiply(PC, i, v, u, FULL_UNITS, (PC.group0 + g) % 2, xhi, xlo)
                    if v == 1:
                        pe.wait_ge(ml_fetched, i * 6 + 6)
                        for a in range(2):
                            for t in range(TILES):
                                last = nc.tensor.transpose(M[0][:, a * SEQ + t * P:a * SEQ + (t + 1) * P],
                                                           ml_qk[:, a, t, :], ident[:, :])
                        last.then_inc(ml_T_psum, 1)
                    if v == 2:
                        pe.wait_ge(ya_fetched, i + 1)
                        pe.wait_ge(rows_copied, 4)
                        pe.wait_ge(ml_h_ready, i * 2 + 2)
                        for j in range(2):
                            for t in range(TILES):
                                last = nc.tensor.transpose(M[2][:, j * SEQ + t * P:j * SEQ + (t + 1) * P],
                                                           ya_blk[:, t, j * P:(j + 1) * P], ident[:, :])
                        last.then_inc(ya_psum, 1)
                    if v == 7:
                        pe.wait_ge(ml_cT_ready, i + 1)
                        nc.tensor.matmul(M[1][:, 0:SEQ], ml_cT[:, 1, 0:P], ml_cT[:, 0, :], start=True, stop=True)
                        nc.tensor.matmul(M[1][:, SEQ:3 * P], ml_cT[:, 1, P:], ml_cT[:, 0, P:], start=True, stop=True
                                         ).then_inc(ml_scores, 1)
                    if v == 9:
                        pe.wait_ge(ml_w_ready, i + 1)
                        pe.wait_ge(ylo_ready, i + 2)
                        n = ML_V + 1
                        nc.tensor.matmul(M[2][:, 0:n], ml_w[:, 0:P], ml_v[:, 0, :], start=True, stop=True)
                        nc.tensor.matmul(M[3][:, 0:n], ml_w[:, P:2 * P], ml_v[:, 0, :], start=True, stop=False)
                        nc.tensor.matmul(M[3][:, 0:n], ml_w[:, 2 * P:], ml_v[:, 1, :], start=False, stop=True
                                         ).then_inc(ml_num, 1)

            def gate_units(part, i, v, n0):
                if v == 0:
                    pe.wait_ge(gate_tanh, i * 2 + (2 * n0 + 2))
                multiply(part, i, v, v, FULL_UNITS, part.group0 % 2, xhi, xlo)

            def branch_units(part, i, v, n0, ylo_count):
                if v == FULL_UNITS:
                    pe.wait_ge(prod_ready, i * 2 + (2 * n0 + 2))
                    pe.wait_ge(banks_free, 4 + 2 * PP[0].group0)
                    pe.wait_ge(ylo_ready, ylo_count)
                multiply(part, i, v, v - FULL_UNITS, HALF_UNITS, (part.group0 + 1) % 2, yhi, ylo)

            def turn_y(area):
                for b in range(4):
                    for j in range(2):
                        for t in range(TILES):
                            kt = 2 * b + j
                            last = nc.tensor.transpose(M[b][:, j * SEQ + t * P:j * SEQ + (t + 1) * P],
                                                       area[:, t, 3 * WIDTH + kt * P:3 * WIDTH + (kt + 1) * P],
                                                       ident[:, :])
                    last.then_inc(y_psum, 1)

            pe.wait_ge(banks_free, 4 + 2 * (PP[0].group0 - 1))
            with pe.Fori(0, IDX_TURNS) as i:
                for v in range(PAIR_UNITS):
                    s, u = v // 3, v % 3
                    p = i * 4 + s
                    if v < FULL_UNITS:
                        gate_units(PP[0], i, v, 0)
                    else:
                        branch_units(PP[0], i, v, 0, 5)
                    if u == 0:
                        pe.wait_ge(idx_fetched, p + 1)
                        for t in range(TILES):
                            last = nc.tensor.transpose(M[0][:, t * P:(t + 1) * P], iq_sb[:, t, :], ident[:, :])
                        last.then_inc(idx_T_psum, 1)
                    if u == 1:
                        pe.wait_ge(iqT_ready, p + 1)
                        for e in range(2):
                            d = slice(e * IDX_DIM, (e + 1) * IDX_DIM)
                            nc.tensor.matmul(M[1 + e][:, 0:P], iqT[d, 0:P], ikT[d, 0:P], start=True, stop=True)
                            last = nc.tensor.matmul(M[1 + e][:, P:3 * P], iqT[d, P:], ikT[d, :], start=True, stop=True)
                        last.then_inc(idx_scores, 1)
            with pe.Fori(IDX_TURNS, PP[0].turns) as i:
                for v in range(PAIR_UNITS):
                    if v < FULL_UNITS:
                        gate_units(PP[0], i, v, 0)
                    else:
                        branch_units(PP[0], i, v, 0, 5)
            pe.wait_ge(idx_relu_ready, IDX_HEADS)
            turn_y(area1)

            with pe.Fori(0, PP[1].turns) as i:
                for v in range(PAIR_UNITS):
                    s, u = v // 6, v % 6
                    h = i * 2 + s
                    if v < FULL_UNITS:
                        gate_units(PP[1], i, v, 4)
                    else:
                        branch_units(PP[1], i, v, 4, 9)
                    if u == 0:
                        pe.wait_ge(dsa_fetched, h + 1)
                        pe.wait_ge(ylo_ready, 9)
                        for c in range(2):
                            for t in range(TILES):
                                last = nc.tensor.transpose(M[0][:, c * SEQ + t * P:c * SEQ + (t + 1) * P],
                                                           dsa_q[:, t, c * P:(c + 1) * P], ident[:, :])
                        last.then_inc(dsa_T_psum, 1)
                    if u == 1:
                        pe.wait_ge(dsa_qT_ready, h + 1)
                        for t, a, n in ((0, 0, P), (1, P, 2 * P)):
                            for c in range(2):
                                last = nc.tensor.matmul(M[1][:, a:a + n], dsa_qT[:, c, t * P:(t + 1) * P],
                                                        cT[:, c, 0:n], start=(c == 0), stop=(c == 1))
                        last.then_inc(dsa_logits, 1)
                    if u == 3:
                        pe.wait_ge(dsa_exp, h * 2 + 2)
                        pe.wait_ge(dsa_y, h * 2 + 1)
                        for b in range(3):
                            last = nc.tensor.transpose(M[2][:, b * P:(b + 1) * P], dsa_s[:, b * P:(b + 1) * P],
                                                       ident[:, :])
                        last.then_inc(dsa_pT_psum, 1)
                    if u == 4:
                        pe.wait_ge(dsa_pT_ready, h + 1)
                        for c in range(2):
                            latent = slice(c * P, (c + 1) * P)
                            nc.tensor.matmul(M[3][:, c * SEQ:c * SEQ + P], c_sb[:, 0, latent], dsa_pT[:, 0:P],
                                             start=True, stop=True)
                            for t in range(TILES):
                                last = nc.tensor.matmul(M[3][:, c * SEQ + P:(c + 1) * SEQ], c_sb[:, t, latent],
                                                        dsa_pT[:, (1 + t) * P:(2 + t) * P],
                                                        start=(t == 0), stop=(t == 1))
                        last.then_inc(dsa_ob, 1)
                    if u == 5:
                        pe.wait_ge(dsa_ob_ready, h + 1)
                        pe.wait_ge(uv_landed, 16)
                        for t in range(TILES):
                            for c in range(2):
                                last = nc.tensor.matmul(M[2][:, t * P:(t + 1) * P], dsa_obT[:, c, t * P:(t + 1) * P],
                                                        w_uv[:, bass.ds(h, 1), c, :].rearrange("p h v -> p (h v)"),
                                                        start=(c == 0), stop=(c == 1))
                        last.then_inc(dsa_out, 1)
            pe.wait_ge(dsa_y, 1 + TILES * DSA_HEADS)
            turn_y(area0)

            with pe.Fori(0, PP[2].turns) as i:
                for v in range(PAIR_UNITS):
                    if v < FULL_UNITS:
                        gate_units(PP[2], i, v, 8)
                    else:
                        branch_units(PP[2], i, v, 8, 13)

            def turn_merged(b):
                for j in range(2):
                    for t in range(TILES):
                        kt = 2 * b + j
                        last = nc.tensor.transpose(merge_banks[b][:, j * SEQ + t * P:j * SEQ + (t + 1) * P],
                                                   mixed[:, t, kt * P:(kt + 1) * P], ident[:, :])
                last.then_inc(merged_psum, 1)

            pe.wait_ge(gate_tanh, 2 + 2 * 4 * BRANCHES)
            pe.wait_ge(mixed_added, 2 * (4 * (BRANCHES - 1) - 1))
            for b in range(6):
                turn_merged(b)

            for g in range(ROW_OUT):
                if g == 0:
                    pe.wait_ge(prod_ready, 2 + 2 * 4 * BRANCHES)
                elif g == 1:
                    pe.wait_ge(merged_lo, 6)
                else:
                    pe.wait_ge(out_copied, TILES * (g - 1))
                for u in range(FULL_UNITS):
                    if g == 0:
                        pe.wait_ge(merged_lo, u + 1)
                    multiply(PO, 0, g * FULL_UNITS + u, u, FULL_UNITS, out_pair(g), xhi, xlo)
                    if g == 0 and u == 1:
                        pe.wait_ge(mixed_added, 2 * 4 * (BRANCHES - 1))
                        turn_merged(6)
                        turn_merged(7)


_INS = ["x", "pre_norm_g", "w_in", "da_lambda", "da_norm_g", "ml_conv_w", "ml_conv_b", "ml_gate_b", "ml_norm_g",
        "dsa_kv_norm_g", "dsa_ik_norm_g", "dsa_w_uv", "w_branch", "w_out", "post_norm_g"]


def kernel(**inputs):
    import numpy as np
    import concourse.bacc as bacc
    from concourse.bass_utils import run_bass_kernel_spmd

    nc = bacc.Bacc("TRN2", target_bir_lowering=False, num_devices=1)
    arrays, args = {}, []
    for name in _INS:
        a = np.ascontiguousarray(inputs[name])
        arrays[f"in_{name}"] = a
        args.append(nc.dram_tensor(f"in_{name}", a.shape, mybir.dt.from_np(a.dtype), kind="ExternalInput").ap())
    out = nc.dram_tensor("out_0", (1, SEQ, D_MODEL), F32, kind="ExternalOutput").ap()
    build(nc, *args, out)
    result = run_bass_kernel_spmd(nc, [arrays], core_ids=[0])
    return result.results[0]["out_0"]
```

```python
import math
from contextlib import ExitStack

import concourse.bass as bass
from concourse import mybir

F32 = mybir.dt.float32
F32R = mybir.dt.float32r
ALU = mybir.AluOpType
ACT = mybir.ActivationFunctionType
AX = mybir.AxisListType

P = 128
D_MODEL = 2048
SEQ = 256
TILES = SEQ // P
KT = D_MODEL // P
WIDTH = 1024
YT = WIDTH // P
BRANCHES = 3
EPS = 1e-6
LAM_INIT = 0.8 - 0.6 * math.exp(0.0)

DA_HEADS, DA_DIM, DA_V = 8, 64, 128
ML_HEADS, ML_QK, ML_V, ML_CONV = 4, 128, 256, 4
DSA_HEADS, DSA_LATENT, DSA_V = 8, 256, 128
IDX_HEADS, IDX_DIM, TOPK = 16, 64, SEQ // 4

COL_A = 0
COL_ML_QKV = 4096
COL_ML_IF = 6144
COL_ML_OZ = 6152
COL_DSA_Q = 8200
COL_DSA_KV = 10248
COL_IQ = 10504
COL_IK = 11528
COL_DSA_Z = 11608
COL_GATES = 12632

KV0, IK0, IW0, IF0, SMALL = 0, 256, 320, 336, 344

X_LOADS = 4
GROUP = 512
UNIT_KT = 2
RING = 4
AHEAD = 4
FULL_UNITS = KT // UNIT_KT
HALF_UNITS = YT // UNIT_KT
IDX_TURNS = 2

MASKED = -1e38
TAKEN = -3e38


class Part:

    def __init__(self, unit0, group0, turns, units, groups):
        self.unit0, self.group0, self.turns, self.units, self.groups = unit0, group0, turns, units, groups

    def unit(self, i, k):
        return i * self.units + (self.unit0 + k)

    def group(self, i, k):
        return i * self.groups + (self.group0 + k)

    def next(self, turns, units, groups):
        return Part(self.unit0 + self.turns * self.units, self.group0 + self.turns * self.groups,
                    turns, units, groups)


EARLY_UNITS = {5: (0,), 7: (1, 2, 3)}
PS = Part(0, 0, 1, FULL_UNITS, 1)
PA = PS.next(4, 2 * FULL_UNITS, 2)
PB = PA.next(4, 2 * FULL_UNITS, 2)
PC = PB.next(4, 2 * FULL_UNITS, 2)
PAIR_UNITS = FULL_UNITS + HALF_UNITS
PP = [PC.next(4, PAIR_UNITS, 2)]
PV = PP[0].next(1, 2, 2)
PP.append(PV.next(4, PAIR_UNITS, 2))
PP.append(PP[1].next(4, PAIR_UNITS, 2))
PO = PP[2].next(1, 4 * FULL_UNITS, 4)
ALL_UNITS = PO.unit0 + PO.units


FINAL_DVE = tuple((t, slice(g * GROUP, (g + 1) * GROUP)) for t, g in ((0, 0), (0, 1), (0, 2), (0, 3), (1, 0)))
FINAL_POOL = ((1, slice(3 * GROUP, 4 * GROUP)), (1, slice(2 * GROUP, 3 * GROUP)), (1, slice(GROUP, 2 * GROUP)))


def landed_count(part, i, k):
    use = (part.unit0 + k) // RING
    if part is PS and use < 2:
        return 48 * (use + 1)
    return i * (16 * part.units // RING) + (16 * (use - 2) + 96 + 16)


class Steps:

    def __init__(self, engine, sem):
        self.engine, self.sem, self.base, self.k, self.per, self.i = engine, sem, 0, 0, 0, 0

    def enter(self, i, per):
        self.base, self.i, self.per, self.k = self.base + self.k, i, per, 0

    def leave(self, turns):
        assert self.k == self.per, (self.k, self.per)
        self.base, self.k, self.per, self.i = self.base + turns * self.per, 0, 0, 0

    def step(self, instruction):
        self.k += 1
        instruction.then_inc(self.sem, 1)
        self.engine.wait_ge(self.sem, self.i * self.per + (self.base + self.k))


def build(nc, x, pre_norm_g, w_in, da_lambda, da_norm_g, ml_conv_w, ml_conv_b, ml_gate_b, ml_norm_g,
          dsa_kv_norm_g, dsa_ik_norm_g, dsa_w_uv, w_branch, w_out, post_norm_g, out):
    with ExitStack() as ctx:
        def sb(name, shape, dt=F32):
            return ctx.enter_context(nc.sbuf_tensor(name, shape, dt))

        def sem(name):
            return ctx.enter_context(nc.semaphore(name))

        xhi = sb("xhi", [P, KT, SEQ], F32R)
        xlo = sb("xlo", [P, KT, SEQ], F32R)
        raw = sb("raw", [P, RING, UNIT_KT, GROUP])
        whi = sb("whi", [P, RING, UNIT_KT, GROUP], F32R)
        wlo = sb("wlo", [P, RING, UNIT_KT, GROUP], F32R)
        area0 = sb("area0", [P, TILES, 4096])
        area1 = sb("area1", [P, TILES, 4096])
        yhi = sb("yhi", [P, YT, SEQ], F32R)
        ylo = sb("ylo", [P, YT, SEQ], F32R)
        chi = sb("chi", [P, 2, SEQ], F32R)
        clo = sb("clo", [P, 2, SEQ], F32R)
        mixed = sb("mixed", [P, TILES, D_MODEL])
        scratch = sb("scratch", [P, 3330])
        small = sb("small", [P, TILES, SMALL])
        ident = sb("ident", [P, P])
        causal = sb("causal", [P, 3 * P])
        upper = sb("upper", [P, P])
        selrow = sb("selrow", [ML_HEADS, ML_HEADS, P])
        rows = sb("rows", [56, P])
        cols = sb("cols", [P, 56])
        lam_in = sb("lam_in", [P, 4, DA_DIM])
        da_g = sb("da_g", [P, DA_V])
        ml_g = sb("ml_g", [P, ML_V])
        kv_g = sb("kv_g", [P, DSA_LATENT])
        ik_g = sb("ik_g", [P, IDX_DIM])
        gate_b = sb("gate_b", [P, 2 * ML_HEADS])
        tiny = sb("tiny", [P, 168])

        ssx, rstdx, half_rstdx = tiny[:, 0:2], tiny[:, 2:4], tiny[:, 154:156]
        sskv, rstdkv = tiny[:, 4:8], tiny[:, 8:12]
        neglam, lam2 = tiny[:, 12:13], tiny[:, 14:16]
        da_negmax_c = tiny[:, 16:20]
        da_sum_c = tiny[:, 20:24]
        da_rsum_c = tiny[:, 24:28]
        acol_h, guard_h = tiny[:, 28:30], tiny[:, 30:32]
        den, rden = tiny[:, 32:34], tiny[:, 34:36]
        dsa_negmax_c, dsa_sum_c, dsa_rsum_c = tiny[:, 36:38], tiny[:, 38:40], tiny[:, 40:42]
        da_ss = tiny[:, 44:60].rearrange("p (h t) -> p h t", t=TILES)
        ml_ss = tiny[:, 60:68].rearrange("p (h t) -> p h t", t=TILES)
        sso, rstdo = tiny[:, 68:76].rearrange("p (t g) -> p t g", t=TILES), tiny[:, 76:78]
        acol = tiny[:, 80:88].rearrange("p (t h) -> p t h", t=TILES)
        guard = tiny[:, 88:96].rearrange("p (t h) -> p t h", t=TILES)
        iw_pair = tiny[:, 96:100].rearrange("p (t e) -> p t e", t=TILES)
        top8 = tiny[:, 100:116].rearrange("p (t e) -> p t e", t=TILES)
        gate_in = tiny[:, 116:132].rearrange("p (t e) -> p t e", t=TILES)
        forget_t = tiny[:, 156:164].rearrange("p (t h) -> p t h", t=TILES)
        conv_h = tiny[:, 132:142].rearrange("p (a j) -> p a j", a=2)
        wait_carrier = tiny[:, 166:167]
        sqrt_first = tiny[:, 167:168]
        one = tiny[:, 142:143]
        spare = [tiny[:, 143 + n:144 + n] for n in range(10)]

        def view(base, at, *shape):
            n = 1
            for s in shape:
                n *= s
            flat = base[:, at:at + n]
            if len(shape) == 2:
                return flat.rearrange("p (a b) -> p a b", a=shape[0])
            if len(shape) == 3:
                return flat.rearrange("p (a b c) -> p a b c", a=shape[0], b=shape[1])
            return flat

        early = mixed[:, :, :].rearrange("p t n -> p (t n)")
        x_sb = mixed
        da_q, da_k, da_v = (view(early, 256 * n, TILES, P) for n in range(3))
        da_qkT = view(early, 768, 2, SEQ)
        da_s = view(early, 1280, 2, 3 * P)
        da_a = view(early, 2048, 3 * P)
        da_aT = view(early, 2432, 3 * P)
        da_sig = view(early, 2816, TILES, P)
        da_o = view(early, 3072, TILES, P)
        da_sq = view(early, 3328, TILES, P)
        ml_qk = view(early, 0, 2, TILES, P)
        ml_xT = view(early, 512, 2, ML_CONV - 1 + SEQ)
        ml_cT = view(early, 1030, 2, SEQ)
        ml_sT = view(early, 1542, 2, SEQ)
        ml_E = view(early, 2054, 3 * P)
        ml_w = view(early, 2438, 3 * P)
        ml_h = view(early, 2822, TILES, ML_V)
        ml_sq = view(early, 3334, TILES, ML_V)
        c_sb = view(area1[:, 0, :], 0, TILES, DSA_LATENT)
        cT = view(scratch, 0, 2, SEQ)
        ikT = view(scratch, 512, SEQ)
        ml_v = view(scratch, 768, TILES, ML_V + 1)
        ml_to = view(scratch, 1282, TILES, ML_V)
        ml_tz = view(scratch, 1794, TILES, ML_V)
        ml_negM = view(scratch, 2306, ML_HEADS, SEQ)
        row_a, row_b, row_c, row_negM = (scratch[0:ML_HEADS, 1282 + SEQ * n:1282 + SEQ * (n + 1)] for n in range(4))
        row_one = scratch[0:ML_HEADS, 768:768 + SEQ]
        kv_sq = view(area1[:, 1, :], 0, TILES, DSA_LATENT)
        ik_sq = view(area1[:, 1, :], 512, TILES, IDX_DIM)
        ik2 = view(area1[:, 0, :], 512, TILES, 2 * IDX_DIM)
        ya_blk = sb("ya_blk", [P, TILES, 256])
        dsa_v = view(area1[:, 0, :], 0, TILES, WIDTH)
        sig = view(area1[:, 1, :], 0, TILES, GROUP)
        prod = view(area1[:, 1, :], 1024, TILES, GROUP)
        room0, room1 = area1[:, 0, 2048:3072], area1[:, 1, 2048:3072]
        iq_sb = ya_blk[:, :, 0:P]
        iqT = view(room0, 256, SEQ)
        idx_acc = view(scratch, 2048, 3 * P)
        select = view(scratch, 768, 3 * P)
        idx_relu = view(room1, 0, 2, 3 * P)
        dsa_q = ya_blk[:, :, :]
        dsa_qT = view(room0, 512, 2, SEQ)
        dsa_pT = view(room1, 512, 3 * P)
        dsa_s = view(scratch, 1152, 3 * P)
        dsa_sig = view(scratch, 1536, TILES, P)
        out_sb = area0[:, :, 0:D_MODEL]
        x_again = area0[:, :, D_MODEL:2 * D_MODEL]
        post_g = area1[:, 0, D_MODEL:2 * D_MODEL]

        stream = [[ctx.enter_context(nc.psum_tensor(f"stream{g}{t}", [P, GROUP], F32)) for t in range(TILES)]
                  for g in range(2)]
        M = [ctx.enter_context(nc.psum_tensor(f"mixer{n}", [P, GROUP], F32)) for n in range(4)]
        banks = [stream[0][0], stream[0][1], stream[1][0], stream[1][1], *M]

        def out_pair(g):
            return (PP[2].group0 + g) % 2

        x_landed = [sem(f"x_landed{n}") for n in range(X_LOADS)]
        rows_landed = sem("rows_landed")
        consts_landed = sem("consts_landed")
        raw_landed = [sem(f"raw_landed{n}") for n in range(RING)]
        uv_landed = sem("uv_landed")
        end_landed = sem("end_landed")
        stored = sem("stored")
        whi_ready = sem("whi_ready")
        wlo_ready = sem("wlo_ready")
        units_done = sem("units_done")
        banks_free = sem("banks_free")
        masks_ready = sem("masks_ready")
        dve_step, pool_step = sem("dve_step"), sem("pool_step")
        ssx_ready, msx_ready, stdx_ready = sem("ssx_ready"), sem("msx_ready"), sem("stdx_ready")
        cols_turned, cols_ready = sem("cols_turned"), sem("cols_ready")
        rstdx_ready, x_turned = sem("rstdx_ready"), sem("x_turned")
        xhi_ready, xlo_ready = sem("xhi_ready"), sem("xlo_ready")
        lam_sum_ready, lam_exp_ready = sem("lam_sum_ready"), sem("lam_exp_ready")
        kv_squared = sem("kv_squared")
        kv_ms_ready, kv_std_ready, kv_normed = sem("kv_ms_ready"), sem("kv_std_ready"), sem("kv_normed")
        prep_turned, prep_copied = sem("prep_turned"), sem("prep_copied")
        row_ready, row_act = sem("row_ready"), sem("row_act")
        da_v_fetched = sem("da_v_fetched")
        da_fetched, da_qkT_psum, da_qkT_ready = sem("da_fetched"), sem("da_qkT_psum"), sem("da_qkT_ready")
        da_scores, da_negmax, da_exp, da_attn = sem("da_scores"), sem("da_negmax"), sem("da_exp"), sem("da_attn")
        da_aT_psum, da_aT_ready, da_av, da_o_out = sem("da_aT_psum"), sem("da_aT_ready"), sem("da_av"), sem("da_o_out")
        da_tz, da_pool = sem("da_tz"), sem("da_pool")
        da_ms, da_std, ya_ready = sem("da_ms"), sem("da_std"), sem("ya_ready")
        rows_turned, rows_copied = sem("rows_turned"), sem("rows_copied")
        ml_fetched, ml_T_psum, ml_xT_ready = sem("ml_fetched"), sem("ml_T_psum"), sem("ml_xT_ready")
        ml_conv, ml_ts, ml_cT_ready = sem("ml_conv"), sem("ml_ts"), sem("ml_cT_ready")
        ml_arg, ml_exp, ml_E_ready, ml_scores = sem("ml_arg"), sem("ml_exp"), sem("ml_E_ready"), sem("ml_scores")
        ml_w_ready, ml_num, ml_h_ready, ml_pool = sem("ml_w_ready"), sem("ml_num"), sem("ml_h_ready"), sem("ml_pool")
        ml_toz, ml_gated = sem("ml_toz"), sem("ml_gated")
        ml_ms, ml_std, yb_ready = sem("ml_ms"), sem("ml_std"), sem("yb_ready")
        ya_fetched, ya_psum = sem("ya_fetched"), sem("ya_psum")
        y_psum, yhi_ready, ylo_ready = sem("y_psum"), sem("yhi_ready"), sem("ylo_ready")
        gate_tanh, prod_ready, mixed_added, iw_fetched = (sem("gate_tanh"), sem("prod_ready"), sem("mixed_added"),
                                                          sem("iw_fetched"))
        idx_fetched, idx_T_psum, iqT_ready = sem("idx_fetched"), sem("idx_T_psum"), sem("iqT_ready")
        idx_scores, idx_relu_ready, idx_added = sem("idx_scores"), sem("idx_relu_ready"), sem("idx_added")
        dsa_fetched, dsa_T_psum, dsa_qT_ready = sem("dsa_fetched"), sem("dsa_T_psum"), sem("dsa_qT_ready")
        dsa_logits, dsa_negmax, dsa_exp = sem("dsa_logits"), sem("dsa_negmax"), sem("dsa_exp")
        dsa_pT_psum, dsa_pT_ready = sem("dsa_pT_psum"), sem("dsa_pT_ready")
        chi_ready, clo_ready, v_taken = sem("chi_ready"), sem("clo_ready"), sem("v_taken")
        dsa_out, dsa_y, dsa_tz = sem("dsa_out"), sem("dsa_y"), sem("dsa_tz")
        merged_psum, merged_hi, merged_lo = sem("merged_psum"), sem("merged_hi"), sem("merged_lo")
        out_taken, out_ss, out_ms, out_std = sem("out_taken"), sem("out_ss"), sem("out_ms"), sem("out_std")
        rstdo_ready, y_scaled, y_dve, y_pool = sem("rstdo_ready"), sem("y_scaled"), sem("y_dve"), sem("y_pool")
        ROW_OUT = D_MODEL // GROUP

        x_d = x[0].rearrange("(t p) d -> p t d", p=P)
        out_d = out[0].rearrange("(t p) d -> p t d", p=P)
        w_in_d = w_in[0].rearrange("(k p) n -> p k n", p=P)
        w_branch_d = [w_branch[0, b].rearrange("(k p) n -> p k n", p=P) for b in range(BRANCHES)]
        w_out_d = w_out[0].rearrange("(k p) n -> p k n", p=P)

        block = ctx.enter_context(nc.Block())

        @block.sync
        def _(sp):
            def load_group(units, part, i, k0, source, col, ahead=False, waited=False):
                for u in range(units):
                    k = k0 + u
                    slot = (part.unit0 + k) % RING
                    if not (waited and u == 0):
                        sp.wait_ge(wlo_ready, part.unit(i, k) - RING + 1 + (ahead and u == units - 1))
                    sp.dma_start(raw[:, slot, :, :],
                                 source[:, UNIT_KT * u:UNIT_KT * (u + 1), bass.ds(col, GROUP)]
                                 ).then_inc(raw_landed[slot], 16)

            def load_small(u):
                slot = u % RING
                if u >= RING:
                    sp.wait_ge(wlo_ready, u - RING + 1)
                for at, col, n in ((KV0, COL_DSA_KV, DSA_LATENT), (IK0, COL_IK, IDX_DIM + IDX_HEADS),
                                   (IF0, COL_ML_IF, 2 * ML_HEADS)):
                    sp.dma_start(raw[:, slot, :, at:at + n],
                                 w_in_d[:, UNIT_KT * u:UNIT_KT * (u + 1), col:col + n]
                                 ).then_inc(raw_landed[slot], 16)

            for n in range(X_LOADS):
                part_of_x = slice(n * D_MODEL // X_LOADS, (n + 1) * D_MODEL // X_LOADS)
                sp.dma_start(x_sb[:, :, part_of_x], x_d[:, :, part_of_x]).then_inc(x_landed[n], 16)
                if n == 0:
                    sp.dma_start(rows[40:56, :], pre_norm_g[0].rearrange("(b d) -> b d", d=P)).then_inc(rows_landed, 16)
                    sp.dma_start(rows[0:32, :], ml_conv_w[0].rearrange("j (b d) -> (j b) d", d=P)
                                 ).then_inc(rows_landed, 16)
                    sp.dma_start(rows[32:40, :], ml_conv_b[0].rearrange("(b d) -> b d", d=P)).then_inc(rows_landed, 16)
                if n >= 2:
                    load_small(n - 2)
            load_small(2)
            load_small(3)
            for to, of in ((lam_in[:, :, :].rearrange("p a b -> p (a b)"), da_lambda[0].rearrange("a b -> (a b)")),
                           (da_g[:, :], da_norm_g[0]), (ml_g[:, :], ml_norm_g[0]), (kv_g[:, :], dsa_kv_norm_g[0]),
                           (ik_g[:, :], dsa_ik_norm_g[0]), (gate_b[:, :], ml_gate_b[0].rearrange("a b -> (a b)"))):
                sp.dma_start(to, of.partition_broadcast(P)).then_inc(consts_landed, 16)
            for u in range(RING, FULL_UNITS):
                load_small(u)

            with sp.Fori(0, PA.turns) as i:
                for g in range(2):
                    load_group(FULL_UNITS, PA, i, g * FULL_UNITS, w_in_d, i * 2 * GROUP + (COL_A + g * GROUP))
            for turn0, col in ((0, COL_ML_QKV), (2, COL_ML_OZ)):
                with sp.Fori(0, 2) as i:
                    for g in range(2):
                        load_group(FULL_UNITS, PB, i, (2 * turn0 + g) * FULL_UNITS, w_in_d,
                                   i * 2 * GROUP + (col + g * GROUP))
            with sp.Fori(0, 2) as i:
                for g in range(2):
                    load_group(FULL_UNITS, PC, i, g * FULL_UNITS, w_in_d, i * 2 * GROUP + (COL_DSA_Q + g * GROUP))
            for turn, col in ((2, COL_IQ), (3, COL_DSA_Z)):
                for g in range(2):
                    load_group(FULL_UNITS, PC, 0, (2 * turn + g) * FULL_UNITS, w_in_d, col + g * GROUP)
            for b in range(BRANCHES):
                if b == 1:
                    for g in range(2):
                        slot = (PV.unit0 + g) % RING
                        sp.wait_ge(wlo_ready, PV.unit0 + g - RING + 1)
                        for c in range(2):
                            if c == 1:
                                sp.wait_ge(uv_landed, 16 * (g + 1))
                            sp.dma_start(raw[:, slot, c, :].rearrange("p (h v) -> p h v", v=P),
                                         dsa_w_uv[0, 4 * g:4 * g + 4, c * P:(c + 1) * P].rearrange("h p v -> p h v")
                                         ).then_inc(raw_landed[slot] if c else uv_landed, 16)
                with sp.Fori(0, PP[b].turns) as i:
                    load_group(FULL_UNITS, PP[b], i, 0, w_in_d, i * GROUP + (COL_GATES + b * D_MODEL), ahead=True)
                    load_group(HALF_UNITS, PP[b], i, FULL_UNITS, w_branch_d[b], i * GROUP, waited=True)
            sp.wait_ge(y_psum, 8)
            for t in range(TILES):
                sp.dma_start(x_again[:, t, :], x_d[:, t, :]).then_inc(end_landed, 16)
            sp.dma_start(post_g, post_norm_g[0].partition_broadcast(P)).then_inc(end_landed, 16)
            for g in range(ROW_OUT):
                load_group(FULL_UNITS, PO, 0, g * FULL_UNITS, w_out_d, g * GROUP)
            for ended, parts, n in ((y_dve, FINAL_DVE, 0), (y_dve, FINAL_DVE, 1), (y_pool, FINAL_POOL, 0),
                                    (y_dve, FINAL_DVE, 2), (y_dve, FINAL_DVE, 3), (y_pool, FINAL_POOL, 1),
                                    (y_dve, FINAL_DVE, 4), (y_pool, FINAL_POOL, 2)):
                t, columns = parts[n]
                sp.wait_ge(ended, n + 1)
                sp.dma_start(out_d[:, t, columns], out_sb[:, t, columns]).then_inc(stored, 16)
            sp.wait_ge(stored, 16 * (len(FINAL_DVE) + len(FINAL_POOL)))

        @block.gpsimd
        def _(pool):
            steps = Steps(pool, pool_step)
            steps.step(nc.gpsimd.memset(ident[:, :], 0.0))
            nc.gpsimd.affine_select(out=ident[:, :], in_=ident[:, :], compare_op=ALU.not_equal, fill=1.0, base=0,
                                    pattern=[[-1, P]], channel_multiplier=1).then_inc(masks_ready, 1)
            steps.step(nc.gpsimd.memset(upper[:, :], 1.0))
            nc.gpsimd.affine_select(out=upper[:, :], in_=upper[:, :], compare_op=ALU.is_ge, fill=0.0, base=0,
                                    pattern=[[1, P]], channel_multiplier=-1).then_inc(masks_ready, 1)
            steps.step(nc.gpsimd.memset(causal[:, :], 0.0))
            for at, n, base in ((0, P, 0), (P, 2 * P, P)):
                nc.gpsimd.affine_select(out=causal[:, at:at + n], in_=causal[:, at:at + n], compare_op=ALU.is_ge,
                                        fill=MASKED, base=base, pattern=[[-1, n]], channel_multiplier=1
                                        ).then_inc(masks_ready, 1)
            steps.step(nc.gpsimd.memset(selrow[:, :, :], 0.0))
            nc.gpsimd.affine_select(out=selrow[:, :, :], in_=selrow[:, :, :], compare_op=ALU.not_equal, fill=1.0,
                                    base=0, pattern=[[-1, ML_HEADS], [0, P]], channel_multiplier=1
                                    ).then_inc(masks_ready, 1)

            pool.wait_ge(banks_free, 4 + 2 * PA.group0)
            for to, at, n in ((kv_sq, KV0, DSA_LATENT), (ik_sq, IK0, IDX_DIM)):
                nc.gpsimd.tensor_tensor(to, small[:, :, at:at + n], small[:, :, at:at + n], ALU.mult
                                        ).then_inc(kv_squared, 1)

            pool.wait_ge(banks_free, 4 + 2 * PB.group0)
            pool.wait_ge(consts_landed, 6 * 16)

            def fetch_da(at, n):
                nc.gpsimd.tensor_copy((da_q, da_k, da_v)[n], area0[:, :, bass.ds(at + n * WIDTH, P)]
                                      ).then_inc(da_v_fetched if n == 2 else da_fetched, 1)

            def put_da(at):
                nc.gpsimd.tensor_tensor(da_sq, da_o, da_o, ALU.mult).then_inc(da_pool, 1)
                nc.gpsimd.tensor_copy(area0[:, :, bass.ds(at, P)], da_o).then_inc(da_pool, 1)

            for n in range(3):
                fetch_da(0, n)
            with pool.Fori(0, DA_HEADS - 1) as h:
                pool.wait_ge(da_qkT_psum, h + 1)
                fetch_da(h * P + P, 0)
                fetch_da(h * P + P, 1)
                pool.wait_ge(da_o_out, h + 2)
                put_da(h * P)
                fetch_da(h * P + P, 2)
            pool.wait_ge(da_o_out, DA_HEADS + 1)
            put_da((DA_HEADS - 1) * P)

            pool.wait_ge(banks_free, 4 + 2 * PC.group0)
            pool.wait_ge(rows_copied, 4)
            conv_cols = cols[:, 0:40].rearrange("p (j a h) -> p a h j", a=2, h=ML_HEADS)
            with pool.Fori(0, PC.turns) as i:
                pool.wait_ge(units_done, PC.unit(i, 0))
                for a in range(2):
                    nc.gpsimd.tensor_copy(ml_qk[:, a, :, :], area1[:, :, bass.ds(i * P + a * 512, P)]
                                          ).then_inc(ml_fetched, 1)
                nc.gpsimd.tensor_copy(ml_v[:, :, 0:ML_V], area1[:, :, bass.ds(i * ML_V + WIDTH, ML_V)]
                                      ).then_inc(ml_fetched, 1)
                nc.gpsimd.tensor_copy(conv_h[:, :, :],
                                      conv_cols[:, :, bass.ds(i, 1), :].rearrange("p a h j -> p a (h j)")
                                      ).then_inc(ml_fetched, 1)
                nc.gpsimd.tensor_copy(acol_h, acol[:, :, bass.ds(i, 1)].rearrange("p t h -> p (t h)")
                                      ).then_inc(ml_fetched, 1)
                nc.gpsimd.tensor_copy(guard_h, guard[:, :, bass.ds(i, 1)].rearrange("p t h -> p (t h)")
                                      ).then_inc(ml_fetched, 1)
                pool.wait_ge(ya_ready, TILES * DA_HEADS)
                nc.gpsimd.tensor_copy(ya_blk[:, :, :], area0[:, :, bass.ds(i * 256 + 3 * WIDTH, 256)]
                                      ).then_inc(ya_fetched, 1)
                pool.wait_ge(ml_exp, i + 1)
                diagonals = ml_E.rearrange("p (c n) -> p c n", n=P)[:, 0:3:2, :]
                nc.gpsimd.tensor_tensor(diagonals, diagonals, upper[:, :].unsqueeze(1).broadcast_to([P, 2, P]),
                                        ALU.mult).then_inc(ml_E_ready, 1)
                pool.wait_ge(ml_h_ready, i * 2 + 4)
                nc.gpsimd.tensor_tensor(ml_sq, ml_h, ml_h, ALU.mult).then_inc(ml_pool, 1)
                nc.gpsimd.tensor_copy(area1[:, :, bass.ds(i * ML_V + WIDTH, ML_V)], ml_h).then_inc(ml_pool, 1)

            def fetch_iq(at):
                nc.gpsimd.tensor_copy(iq_sb, area0[:, :, bass.ds(at, P)]).then_inc(idx_fetched, 1)

            def fetch_iw(at):
                nc.gpsimd.tensor_copy(iw_pair, small[:, :, bass.ds(at, 2)]).then_inc(iw_fetched, 1)

            pool.wait_ge(banks_free, 4 + 2 * (PC.group0 + 6))
            pool.wait_ge(ya_psum, PC.turns)
            fetch_iq(2048)
            fetch_iw(IW0)
            with pool.Fori(0, IDX_HEADS // 2 - 1) as p:
                pool.wait_ge(idx_T_psum, p + 1)
                fetch_iq(p * P + (2048 + P))
                pool.wait_ge(idx_added, p * 4 + 5)
                fetch_iw(p * 2 + (IW0 + 2))

            pool.wait_ge(idx_T_psum, IDX_HEADS // 2)
            nc.gpsimd.tensor_copy(dsa_q, area0[:, :, 0:DSA_LATENT]).then_inc(dsa_fetched, 1)
            with pool.Fori(0, DSA_HEADS - 1) as h:
                pool.wait_ge(dsa_T_psum, h + 1)
                nc.gpsimd.tensor_copy(dsa_q, area0[:, :, bass.ds(h * DSA_LATENT + DSA_LATENT, DSA_LATENT)]
                                      ).then_inc(dsa_fetched, 1)

            pool.wait_ge(end_landed, 48)
            for n, (t, columns) in enumerate(FINAL_POOL):
                pool.wait_ge(y_scaled, n + 1)
                to = out_sb[:, t, columns]
                nc.gpsimd.tensor_tensor(to, to, x_again[:, t, columns], ALU.add).then_inc(y_pool, 1)

        @block.scalar
        def _(act):
            def round_unit(part, i, k):
                n = k + AHEAD
                slot = (part.unit0 + n) % RING
                width = SMALL if part is PS and n < FULL_UNITS else GROUP
                act.wait_ge(raw_landed[slot], landed_count(part, i, n))
                if part.unit0 + n >= RING:
                    act.wait_ge(units_done, part.unit(i, n) - RING + 1)
                nc.scalar.activation(whi[:, slot, :, 0:width], raw[:, slot, :, 0:width], ACT.Copy
                                     ).then_inc(whi_ready, 1)

            def take_group(part, i, k_end, bank_pair, to, width=GROUP):
                act.wait_ge(units_done, part.unit(i, k_end))
                for t in range(TILES):
                    nc.scalar.activation(to[t], stream[bank_pair][t][:, 0:width], ACT.Copy, scale=rstdx[:, t:t + 1]
                                         ).then_inc(banks_free, 1)

            act.wait_ge(cols_turned, 1)
            nc.scalar.activation(cols[:, :], M[0][:, 0:56], ACT.Copy).then_inc(cols_ready, 1)
            act.wait_ge(cols_ready, 1)
            for b in range(8):
                act.wait_ge(x_turned, b + 1)
                for k in range(2 * b, 2 * b + 2):
                    nc.scalar.activation(xhi[:, k, :], banks[b][:, (k % 2) * SEQ:(k % 2 + 1) * SEQ], ACT.Copy,
                                         scale=cols[:, 40 + k:41 + k]).then_inc(xhi_ready, 1)
                for u in EARLY_UNITS.get(b, ()):
                    round_unit(PS, 0, u - AHEAD)
            def square_x(t):
                nc.scalar.activation(area1[:, t, 0:D_MODEL], x_sb[:, t, :], ACT.Square,
                                     accum_out=ssx[:, t:t + 1]).then_inc(ssx_ready, 1)

            square_x(0)
            for u in range(FULL_UNITS // 2):
                round_unit(PS, 0, u)
            square_x(1)
            act.wait_ge(msx_ready, 1)
            nc.scalar.activation(rstdx, rstdx, ACT.Sqrt).then_inc(stdx_ready, 1)

            for u in range(FULL_UNITS // 2, FULL_UNITS):
                round_unit(PS, 0, u)
            act.wait_ge(rstdx_ready, 2)
            take_group(PS, 0, FULL_UNITS, 0, [small[:, t, :] for t in range(TILES)], SMALL)
            act.wait_ge(lam_sum_ready, 2)
            nc.scalar.activation(lam2, lam2, ACT.Exp).then_inc(lam_exp_ready, 1)
            act.wait_ge(row_ready, 1)
            nc.scalar.activation(forget_t, forget_t, ACT.Exp).then_inc(row_act, 1)
            act.wait_ge(row_act, 1)
            nc.scalar.activation(forget_t, forget_t, ACT.Ln, bias=one).then_inc(row_act, 1)
            act.wait_ge(kv_ms_ready, 1)
            nc.scalar.activation(rstdkv[:, 0:4], rstdkv[:, 0:4], ACT.Sqrt).then_inc(kv_std_ready, 1)

            with act.Fori(0, PA.turns) as i:
                for g in range(2):
                    for u in range(FULL_UNITS):
                        round_unit(PA, i, g * FULL_UNITS + u)
                    take_group(PA, i, (g + 1) * FULL_UNITS, (PA.group0 + g) % 2,
                               [area0[:, t, bass.ds(i * 2 * GROUP + g * GROUP, GROUP)] for t in range(TILES)])

            act.wait_ge(prep_turned, 1)
            nc.scalar.activation(cT, M[0][:, :].rearrange("p (c s) -> p c s", c=2), ACT.Copy).then_inc(prep_copied, 1)
            act.wait_ge(prep_turned, 2)
            nc.scalar.activation(ikT, M[1][:, 0:SEQ], ACT.Copy).then_inc(prep_copied, 1)
            act.wait_ge(row_ready, 2)
            nc.scalar.activation(row_c, row_c, ACT.Exp, scale=-1.0).then_inc(row_act, 1)

            with act.Fori(0, PB.turns) as i:
                for s in range(2):
                    h = i * 2 + s
                    for u in range(FULL_UNITS):
                        round_unit(PB, i, s * FULL_UNITS + u)
                        if u == 1:
                            act.wait_ge(da_qkT_psum, h + 1)
                            nc.scalar.activation(da_qkT, M[0][:, :].rearrange("p (a s) -> p a s", a=2), ACT.Copy
                                                 ).then_inc(da_qkT_ready, 1)
                            nc.scalar.activation(da_sig, area0[:, :, bass.ds(h * P + 3 * WIDTH, P)], ACT.Tanh,
                                                 scale=0.5).then_inc(da_tz, 1)
                        if u == 3:
                            act.wait_ge(da_negmax, h * 2 + 2)
                            for t, a, n in ((0, 0, P), (1, P, 2 * P)):
                                for c in range(2):
                                    nc.scalar.activation(da_s[:, c, a:a + n], da_s[:, c, a:a + n], ACT.Exp,
                                                         bias=da_negmax_c[:, 2 * t + c:2 * t + c + 1],
                                                         accum_out=da_sum_c[:, 2 * t + c:2 * t + c + 1]
                                                         ).then_inc(da_exp, 1)
                        if u == 6:
                            act.wait_ge(da_aT_psum, h + 1)
                            nc.scalar.activation(da_aT, M[3][:, 0:3 * P], ACT.Copy).then_inc(da_aT_ready, 1)
                    take_group(PB, i, (s + 1) * FULL_UNITS, (PB.group0 + s) % 2,
                               [area1[:, t, bass.ds(i * 2 * GROUP + s * GROUP, GROUP)] for t in range(TILES)])

            for n in range(2):
                act.wait_ge(rows_turned, n + 1)
                nc.scalar.activation(ml_negM[:, 2 * n:2 * n + 2, :],
                                     M[n + 1][:, :].rearrange("p (h s) -> p h s", h=2), ACT.Copy
                                     ).then_inc(rows_copied, 1)
            act.wait_ge(rows_turned, 3)
            nc.scalar.activation(acol, M[3][:, 0:8].rearrange("p (t h) -> p t h", t=TILES), ACT.Copy
                                 ).then_inc(rows_copied, 1)
            nc.scalar.activation(guard, M[3][:, 8:16].rearrange("p (t h) -> p t h", t=TILES), ACT.Copy
                                 ).then_inc(rows_copied, 1)
            act.wait_ge(da_ms, 1)
            nc.scalar.activation(da_ss, da_ss, ACT.Sqrt).then_inc(da_std, 1)

            with act.Fori(0, PC.turns) as i:
                for v in range(2 * FULL_UNITS):
                    round_unit(PC, i, v)
                    if v == 1:
                        act.wait_ge(ml_T_psum, i + 1)
                        nc.scalar.activation(ml_xT[:, :, ML_CONV - 1:], M[0][:, :].rearrange("p (a s) -> p a s", a=2),
                                             ACT.Copy).then_inc(ml_xT_ready, 1)
                    if v == 4:
                        act.wait_ge(ml_conv, i + 1)
                        nc.scalar.activation(ml_sT, ml_cT, ACT.Tanh, scale=0.5).then_inc(ml_ts, 1)
                        act.wait_ge(ml_arg, i * 2 + 2)
                        nc.scalar.activation(ml_E, ml_E, ACT.Exp).then_inc(ml_exp, 1)
                    if v == 11:
                        act.wait_ge(ml_gated, i + 1)
                        nc.scalar.activation(ml_to, area1[:, :, bass.ds(i * ML_V + 2 * WIDTH, ML_V)], ACT.Tanh,
                                             scale=0.5).then_inc(ml_toz, 1)
                        nc.scalar.activation(ml_tz, area1[:, :, bass.ds(i * ML_V + 3 * WIDTH, ML_V)], ACT.Tanh,
                                             scale=0.5).then_inc(ml_toz, 1)
                    if v == 3:
                        act.wait_ge(ya_psum, i + 1)
                        nc.scalar.activation(yhi[:, bass.ds(i * 2, 2), :],
                                             M[2][:, :].rearrange("p (k s) -> p k s", k=2), ACT.Copy
                                             ).then_inc(yhi_ready, 1)
                    if v in (FULL_UNITS - 1, 2 * FULL_UNITS - 1):
                        g = v // FULL_UNITS
                        take_group(PC, i, (g + 1) * FULL_UNITS, (PC.group0 + g) % 2,
                                   [area0[:, t, bass.ds(i * 2 * GROUP + g * GROUP, GROUP)] for t in range(TILES)])
            act.wait_ge(ml_ms, 1)
            nc.scalar.activation(ml_ss, ml_ss, ACT.Sqrt).then_inc(ml_std, 1)

            def gates(part, i, n0):
                act.wait_ge(units_done, part.unit(i, FULL_UNITS))
                act.wait_ge(prod_ready, i * 2 + (2 * n0 + 2))
                for t in range(TILES):
                    nc.scalar.activation(sig[:, t, :], stream[part.group0 % 2][t][:, :], ACT.Tanh,
                                         scale=half_rstdx[:, t:t + 1]).then_inc(gate_tanh, 1)

            with act.Fori(0, IDX_TURNS) as i:
                for v in range(PAIR_UNITS):
                    round_unit(PP[0], i, v)
                    s, u = v // 3, v % 3
                    p = i * 4 + s
                    if u == 1:
                        act.wait_ge(idx_T_psum, p + 1)
                        nc.scalar.activation(iqT, M[0][:, 0:SEQ], ACT.Copy).then_inc(iqT_ready, 1)
                    if u == 2:
                        act.wait_ge(yb_ready, ML_HEADS * TILES)
                        act.wait_ge(idx_added, p * 4 + 1)
                        act.wait_ge(idx_scores, p + 1)
                        for e in range(2):
                            nc.scalar.activation(idx_relu[:, e, :], M[1 + e][:, 0:3 * P], ACT.Relu
                                                 ).then_inc(idx_relu_ready, 1)
                    if v == FULL_UNITS - 1:
                        gates(PP[0], i, 0)
            nc.scalar.activation(chi[:, :, :], cT, ACT.Copy).then_inc(chi_ready, 1)
            with act.Fori(IDX_TURNS, PP[0].turns) as i:
                for v in range(PAIR_UNITS):
                    round_unit(PP[0], i, v)
                    if v == FULL_UNITS - 1:
                        gates(PP[0], i, 0)

            def turn_y(n):
                for b in range(4):
                    act.wait_ge(y_psum, 4 * n + b + 1)
                    nc.scalar.activation(yhi[:, 2 * b:2 * b + 2, :], M[b][:, :].rearrange("p (k s) -> p k s", k=2),
                                         ACT.Copy).then_inc(yhi_ready, 1)

            act.wait_ge(units_done, PV.unit0)
            turn_y(0)
            for g in range(2):
                round_unit(PV, 0, g)
                act.wait_ge(units_done, PV.unit0 + g + 1)
                for t in range(TILES):
                    nc.scalar.activation(dsa_v[:, t, g * GROUP:(g + 1) * GROUP], stream[(PV.group0 + g) % 2][t][:, :],
                                         ACT.Copy).then_inc(v_taken, 1)

            with act.Fori(0, PP[1].turns) as i:
                for v in range(PAIR_UNITS):
                    round_unit(PP[1], i, v)
                    s, u = v // 6, v % 6
                    h = i * 2 + s
                    if u == 0:
                        act.wait_ge(dsa_T_psum, h + 1)
                        nc.scalar.activation(dsa_qT, M[0][:, :].rearrange("p (c s) -> p c s", c=2), ACT.Copy
                                             ).then_inc(dsa_qT_ready, 1)
                    if u == 2:
                        act.wait_ge(dsa_negmax, h * 2 + 2)
                        for t, a, n in ((0, 0, P), (1, P, 2 * P)):
                            nc.scalar.activation(dsa_s[:, a:a + n], dsa_s[:, a:a + n], ACT.Exp,
                                                 bias=dsa_negmax_c[:, t:t + 1], accum_out=dsa_sum_c[:, t:t + 1]
                                                 ).then_inc(dsa_exp, 1)
                        act.wait_ge(dsa_y, h * 2 + 1)
                        nc.scalar.activation(dsa_sig, area0[:, :, bass.ds(h * P + 3 * WIDTH, P)], ACT.Tanh,
                                             scale=0.5).then_inc(dsa_tz, 1)
                    if u == 3:
                        act.wait_ge(dsa_pT_psum, h + 1)
                        nc.scalar.activation(dsa_pT, M[2][:, 0:3 * P], ACT.Copy).then_inc(dsa_pT_ready, 1)
                    if v == FULL_UNITS - 1:
                        gates(PP[1], i, 4)
            act.wait_ge(units_done, PP[2].unit0)
            turn_y(1)

            def merged_high(b):
                act.wait_ge(merged_psum, b + 1)
                nc.scalar.activation(xhi[:, 2 * b:2 * b + 2, :], M[b % 4][:, :].rearrange("p (k s) -> p k s", k=2),
                                     ACT.Copy).then_inc(merged_hi, 1)

            with act.Fori(0, PP[2].turns - 1) as i:
                for v in range(PAIR_UNITS):
                    round_unit(PP[2], i, v)
                    if v == FULL_UNITS - 1:
                        gates(PP[2], i, 8)
            for v in range(PAIR_UNITS):
                round_unit(PP[2], PP[2].turns - 1, v)
                if v == FULL_UNITS - 1:
                    gates(PP[2], PP[2].turns - 1, 8)
                if v >= PAIR_UNITS - 2:
                    merged_high(2 * v - 20)
                    merged_high(2 * v - 19)
            act.wait_ge(lam_sum_ready, 2)
            nc.scalar.activation(sqrt_first, one, ACT.Sqrt)

            for g in range(ROW_OUT):
                for u in range(FULL_UNITS):
                    if g == 0 and u == 2:
                        for b in range(4, 8):
                            merged_high(b)
                    if PO.unit0 + g * FULL_UNITS + u + AHEAD < ALL_UNITS:
                        round_unit(PO, 0, g * FULL_UNITS + u)
                act.wait_ge(units_done, PO.unit0 + (g + 1) * FULL_UNITS)
                for t in range(TILES):
                    nc.scalar.activation(mixed[:, t, 0:GROUP], stream[out_pair(g)][t][:, :], ACT.Square,
                                         accum_out=sso[:, t, g:g + 1]).then_inc(out_ss, 1)
            act.wait_ge(out_ms, 1)
            nc.scalar.activation(rstdo, rstdo, ACT.Sqrt).then_inc(out_std, 1)
            act.wait_ge(rstdo_ready, 1)
            act.wait_ge(out_taken, TILES * ROW_OUT)
            for t, columns in FINAL_POOL:
                nc.scalar.activation(out_sb[:, t, columns], out_sb[:, t, columns], ACT.Copy, scale=rstdo[:, t:t + 1]
                                     ).then_inc(y_scaled, 1)

        @block.vector
        def _(dve):
            steps = Steps(dve, dve_step)

            def split_unit(part, i, k):
                n = k + AHEAD
                slot = (part.unit0 + n) % RING
                width = SMALL if part is PS and n < FULL_UNITS else GROUP
                dve.wait_ge(whi_ready, part.unit(i, n) + 1)
                nc.vector.tensor_tensor(wlo[:, slot, :, 0:width], raw[:, slot, :, 0:width],
                                        whi[:, slot, :, 0:width].bitcast(F32), ALU.subtract).then_inc(wlo_ready, 1)

            nc.vector.memset(spare[0], 0.0).then_inc(banks_free, 4)
            nc.vector.memset(spare[1], 0.0).then_inc(da_o_out, 1)
            nc.vector.memset(spare[2], 0.0).then_inc(ml_h_ready, 2)
            nc.vector.memset(spare[3], 0.0).then_inc(ml_gated, 1)
            nc.vector.memset(spare[4], 0.0).then_inc(ylo_ready, 1)
            nc.vector.memset(spare[6], 0.0).then_inc(dsa_y, 1)
            nc.vector.memset(spare[7], 0.0).then_inc(gate_tanh, 2)
            nc.vector.memset(spare[8], 0.0).then_inc(prod_ready, 2)
            steps.step(nc.vector.memset(one, 1.0))

            dve.wait_ge(cols_ready, 1)
            for b in range(8):
                dve.wait_ge(xhi_ready, 2 * b + 2)
                for k in range(2 * b, 2 * b + 2):
                    nc.vector.scalar_tensor_tensor(xlo[:, k, :], banks[b][:, (k % 2) * SEQ:(k % 2 + 1) * SEQ],
                                                   cols[:, 40 + k:41 + k], xhi[:, k, :].bitcast(F32),
                                                   ALU.mult, ALU.subtract).then_inc(xlo_ready, 1)
                for u in EARLY_UNITS.get(b, ()):
                    split_unit(PS, 0, u - AHEAD)
            for u in range(FULL_UNITS // 2):
                split_unit(PS, 0, u)
            dve.wait_ge(ssx_ready, 2)
            nc.vector.tensor_scalar(rstdx, ssx, 1.0 / D_MODEL, EPS, ALU.mult, ALU.add).then_inc(msx_ready, 1)
            dve.wait_ge(stdx_ready, 1)
            nc.vector.reciprocal(rstdx, rstdx).then_inc(rstdx_ready, 1)
            dve.wait_ge(rstdx_ready, 1)
            nc.vector.tensor_scalar(half_rstdx, rstdx, 0.5, None, ALU.mult).then_inc(rstdx_ready, 1)

            for u in range(FULL_UNITS // 2, FULL_UNITS):
                split_unit(PS, 0, u)
            dve.wait_ge(consts_landed, 6 * 16)
            dve.wait_ge(banks_free, 4 + 2 * PA.group0)
            for t in range(TILES):
                last = nc.vector.tensor_tensor(gate_in[:, t, :], small[:, t, IF0:IF0 + 2 * ML_HEADS], gate_b[:, :],
                                               ALU.add)
            steps.step(last)
            steps.step(nc.vector.tensor_scalar(forget_t, gate_in[:, :, ML_HEADS:], -1.0, None, ALU.mult))
            nc.vector.tensor_tensor(forget_t, gate_in[:, :, ML_HEADS:], forget_t, ALU.min).then_inc(row_ready, 1)
            steps.step(nc.vector.tensor_tensor(lam_in[:, 0:4:2, :], lam_in[:, 0:4:2, :], lam_in[:, 1:4:2, :],
                                               ALU.mult))
            for n in range(2):
                nc.vector.tensor_reduce(lam2[:, n:n + 1], lam_in[:, 2 * n, :], AX.X, ALU.add).then_inc(lam_sum_ready, 1)
            dve.wait_ge(lam_exp_ready, 1)
            steps.step(nc.vector.tensor_tensor(neglam, lam2[:, 1:2], lam2[:, 0:1], ALU.subtract))
            steps.step(nc.vector.tensor_scalar(neglam, neglam, LAM_INIT, None, ALU.subtract))
            dve.wait_ge(kv_squared, 2)
            steps.step(nc.vector.tensor_reduce(sskv[:, 0:2], kv_sq, AX.X, ALU.add))
            steps.step(nc.vector.tensor_reduce(sskv[:, 2:4], ik_sq, AX.X, ALU.add))
            steps.step(nc.vector.tensor_scalar(rstdkv[:, 0:2], sskv[:, 0:2], 1.0 / DSA_LATENT, EPS, ALU.mult, ALU.add))
            nc.vector.tensor_scalar(rstdkv[:, 2:4], sskv[:, 2:4], 1.0 / IDX_DIM, EPS, ALU.mult, ALU.add
                                    ).then_inc(kv_ms_ready, 1)
            dve.wait_ge(kv_std_ready, 1)
            steps.step(nc.vector.reciprocal(rstdkv, rstdkv))
            for t in range(TILES):
                nc.vector.scalar_tensor_tensor(c_sb[:, t, :], small[:, t, KV0:KV0 + DSA_LATENT], rstdkv[:, t:t + 1],
                                               kv_g[:, :], ALU.mult, ALU.mult).then_inc(kv_normed, 1)
                for n in range(2):
                    nc.vector.scalar_tensor_tensor(ik2[:, t, n * IDX_DIM:(n + 1) * IDX_DIM],
                                                   small[:, t, IK0:IK0 + IDX_DIM], rstdkv[:, 2 + t:3 + t],
                                                   ik_g[:, :], ALU.mult, ALU.mult).then_inc(kv_normed, 1)
            steps.step(nc.vector.tensor_scalar(small[:, :, IW0:IW0 + IDX_HEADS], small[:, :, IW0:IW0 + IDX_HEADS],
                                               IDX_HEADS ** -0.5 * IDX_DIM ** -0.5, None, ALU.mult))
            dve.wait_ge(row_act, 2)
            nc.vector.scalar_tensor_tensor(gate_in[:, :, ML_HEADS:], gate_in[:, :, ML_HEADS:], 0.0, forget_t,
                                           ALU.min, ALU.subtract).then_inc(kv_normed, 1)

            with dve.Fori(0, PA.turns) as i:
                for k in range(2 * FULL_UNITS):
                    split_unit(PA, i, k)

            dve.wait_ge(prep_turned, 3)
            steps.step(nc.vector.memset(row_one, 1.0))
            steps.step(nc.vector.tensor_tensor_scan(row_c, row_one, M[2][0:ML_HEADS, SEQ:2 * SEQ], 0.0, ALU.mult,
                                                    ALU.add))
            steps.step(nc.vector.tensor_tensor(row_a, M[2][0:ML_HEADS, 0:SEQ], row_c, ALU.subtract))
            steps.step(nc.vector.tensor_tensor_scan(row_b, row_a, row_a, 0.0, ALU.max, ALU.max))
            steps.step(nc.vector.tensor_scalar(row_negM, row_b, -1.0, None, ALU.mult))
            nc.vector.tensor_tensor(row_c, row_c, row_b, ALU.add).then_inc(row_ready, 1)

            dve.wait_ge(masks_ready, 5)
            with dve.Fori(0, PB.turns) as i:
                steps.enter(i, 2 * 8)
                for s in range(2):
                    h = i * 2 + s
                    for u in range(FULL_UNITS):
                        split_unit(PB, i, s * FULL_UNITS + u)
                        if u == 1:
                            dve.wait_ge(da_tz, h + 1)
                            z = area0[:, :, bass.ds(h * P + 3 * WIDTH, P)]
                            steps.step(nc.vector.scalar_tensor_tensor(da_sig, da_sig, 1.0, z, ALU.add, ALU.mult))
                            nc.vector.tensor_tensor(z, da_sig, da_g[:, :].unsqueeze(1).broadcast_to([P, TILES, P]),
                                                    ALU.mult)
                        if u == 2:
                            dve.wait_ge(da_scores, h + 1)
                            for c in range(2):
                                steps.step(nc.vector.scalar_tensor_tensor(da_s[:, c, :], M[1 + c][:, 0:3 * P],
                                                                          DA_DIM ** -0.5, causal[:, :], ALU.mult,
                                                                          ALU.add))
                            for t, a, n in ((0, 0, P), (1, P, 2 * P)):
                                nc.vector.tensor_reduce(da_negmax_c[:, 2 * t:2 * t + 2], da_s[:, :, a:a + n], AX.X,
                                                        ALU.max, negate=True).then_inc(da_negmax, 1)
                        if u == 4:
                            dve.wait_ge(da_exp, h * 4 + 4)
                            steps.step(nc.vector.reciprocal(da_rsum_c, da_sum_c))
                            steps.step(nc.vector.tensor_scalar(da_rsum_c[:, 1:4:2], da_rsum_c[:, 1:4:2], neglam, None,
                                                               ALU.mult))
                            for t, a, n in ((0, 0, P), (1, P, 2 * P)):
                                steps.step(nc.vector.tensor_scalar(da_a[:, a:a + n], da_s[:, 0, a:a + n],
                                                                   da_rsum_c[:, 2 * t:2 * t + 1], None, ALU.mult))
                                nc.vector.scalar_tensor_tensor(da_a[:, a:a + n], da_s[:, 1, a:a + n],
                                                               da_rsum_c[:, 2 * t + 1:2 * t + 2], da_a[:, a:a + n],
                                                               ALU.mult, ALU.add).then_inc(da_attn, 1)
                        if u == 7:
                            dve.wait_ge(da_av, h + 1)
                            nc.vector.tensor_copy(da_o, M[0][:, 0:SEQ].rearrange("p (t v) -> p t v", t=TILES)
                                                  ).then_inc(da_o_out, 1)
                            dve.wait_ge(da_pool, h * 2 + 2)
                            steps.step(nc.vector.tensor_reduce(da_ss[:, bass.ds(h, 1), :].rearrange("p h t -> p (h t)"),
                                                               da_sq, AX.X, ALU.add))
                steps.leave(PB.turns)
            nc.vector.tensor_scalar(da_ss, da_ss, 1.0 / DA_V, EPS, ALU.mult, ALU.add).then_inc(da_ms, 1)
            dve.wait_ge(da_std, 1)
            steps.step(nc.vector.reciprocal(da_ss, da_ss))
            steps.step(nc.vector.tensor_scalar(da_ss, da_ss, 0.25 * (1.0 - LAM_INIT), None, ALU.mult))
            for h in range(DA_HEADS):
                for t in range(TILES):
                    z = area0[:, t, 3 * WIDTH + h * P:3 * WIDTH + (h + 1) * P]
                    nc.vector.scalar_tensor_tensor(z, area0[:, t, h * P:(h + 1) * P], da_ss[:, h, t:t + 1], z,
                                                   ALU.mult, ALU.mult).then_inc(ya_ready, 1)
            dve.wait_ge(ya_ready, TILES * DA_HEADS)
            nc.vector.memset(ml_xT[:, :, 0:ML_CONV - 1], 0.0)
            steps.step(nc.vector.memset(ml_v[:, :, ML_V:ML_V + 1], 1.0))

            dve.wait_ge(rows_copied, 4)
            with dve.Fori(0, PC.turns) as i:
                steps.enter(i, 11)
                for v in range(2 * FULL_UNITS):
                    split_unit(PC, i, v)
                    if v == 2:
                        dve.wait_ge(ml_xT_ready, i + 1)
                        dve.wait_ge(ml_fetched, i * 6 + 6)
                        for j in range(ML_CONV):
                            for a in range(2):
                                x_j = ml_xT[:, a, j:j + SEQ]
                                if j == 0:
                                    last = nc.vector.tensor_scalar(ml_cT[:, a, :], x_j, conv_h[:, a, 0:1],
                                                                   conv_h[:, a, 4:5], ALU.mult, ALU.add)
                                else:
                                    last = nc.vector.scalar_tensor_tensor(ml_cT[:, a, :], x_j, conv_h[:, a, j:j + 1],
                                                                          ml_cT[:, a, :], ALU.mult, ALU.add)
                            if j < ML_CONV - 1:
                                steps.step(last)
                        last.then_inc(ml_conv, 1)
                    if v == 3:
                        nc.vector.tensor_scalar(ml_E[:, 0:SEQ], ml_negM[:, bass.ds(i, 1), :].rearrange("p h s -> p (h s)"),
                                                acol_h[:, 0:1], 0.0, ALU.add, ALU.min).then_inc(ml_arg, 1)
                        nc.vector.tensor_scalar(ml_E[:, SEQ:], ml_negM[:, bass.ds(i, 1), P:].rearrange("p h s -> p (h s)"),
                                                acol_h[:, 1:2], 0.0, ALU.add, ALU.min).then_inc(ml_arg, 1)
                        dve.wait_ge(ya_psum, i + 1)
                        dve.wait_ge(yhi_ready, i + 1)
                        nc.vector.tensor_tensor(ylo[:, bass.ds(i * 2, 2), :],
                                                M[2][:, :].rearrange("p (k s) -> p k s", k=2),
                                                yhi[:, bass.ds(i * 2, 2), :].bitcast(F32), ALU.subtract
                                                ).then_inc(ylo_ready, 1)
                    if v == 5:
                        dve.wait_ge(ml_ts, i + 1)
                        nc.vector.scalar_tensor_tensor(ml_cT, ml_sT, 1.0, ml_cT, ALU.add, ALU.mult
                                                       ).then_inc(ml_cT_ready, 1)
                    if v == 8:
                        dve.wait_ge(ml_scores, i + 1)
                        dve.wait_ge(ml_E_ready, i + 1)
                        nc.vector.scalar_tensor_tensor(ml_w, M[1][:, 0:3 * P], 0.25 * ML_QK ** -0.5, ml_E,
                                                       ALU.mult, ALU.mult
                                                       ).then_inc(ml_w_ready, 1)
                    if v == 11:
                        dve.wait_ge(ml_num, i + 1)
                        for t in range(TILES):
                            total = M[2 + t][:, ML_V:ML_V + 1]
                            steps.step(nc.vector.tensor_scalar(den[:, t:t + 1], total, -1.0, guard_h[:, t:t + 1],
                                                               ALU.mult, ALU.max))
                            steps.step(nc.vector.tensor_scalar(den[:, t:t + 1], total, den[:, t:t + 1], None,
                                                               ALU.max))
                        steps.step(nc.vector.reciprocal(rden, den))
                        for t in range(TILES):
                            nc.vector.tensor_scalar(ml_h[:, t, :], M[2 + t][:, 0:ML_V], rden[:, t:t + 1], None,
                                                    ALU.mult).then_inc(ml_h_ready, 1)
                    if v == 12:
                        dve.wait_ge(ml_toz, i * 2 + 2)
                        z = area1[:, :, bass.ds(i * ML_V + 3 * WIDTH, ML_V)]
                        steps.step(nc.vector.scalar_tensor_tensor(ml_to, ml_to, 1.0, z, ALU.add, ALU.mult))
                        steps.step(nc.vector.scalar_tensor_tensor(ml_tz, ml_tz, 1.0, ml_to, ALU.add, ALU.mult))
                        nc.vector.tensor_tensor(z, ml_tz, ml_g[:, :].unsqueeze(1).broadcast_to([P, TILES, ML_V]),
                                                ALU.mult).then_inc(ml_gated, 1)
                    if v == 13:
                        dve.wait_ge(ml_pool, i * 2 + 2)
                        steps.step(nc.vector.tensor_reduce(ml_ss[:, bass.ds(i, 1), :].rearrange("p h t -> p (h t)"),
                                                           ml_sq, AX.X, ALU.add))
                steps.leave(PC.turns)
            nc.vector.tensor_scalar(ml_ss, ml_ss, 1.0 / ML_V, EPS, ALU.mult, ALU.add).then_inc(ml_ms, 1)
            dve.wait_ge(ml_std, 1)
            steps.step(nc.vector.reciprocal(ml_ss, ml_ss))
            steps.step(nc.vector.tensor_scalar(ml_ss, ml_ss, 0.125, None, ALU.mult))
            for h in range(ML_HEADS):
                for t in range(TILES):
                    z = area1[:, t, 3 * WIDTH + h * ML_V:3 * WIDTH + (h + 1) * ML_V]
                    nc.vector.scalar_tensor_tensor(z, area1[:, t, WIDTH + h * ML_V:WIDTH + (h + 1) * ML_V],
                                                   ml_ss[:, h, t:t + 1], z, ALU.mult, ALU.mult).then_inc(yb_ready, 1)
            dve.wait_ge(yb_ready, ML_HEADS * TILES)

            def gate_branch(part, i, n0):
                dve.wait_ge(units_done, part.unit(i, PAIR_UNITS))
                dve.wait_ge(gate_tanh, i * 2 + (2 * n0 + 4))
                for t in range(TILES):
                    columns = mixed[:, t, bass.ds(i * GROUP, GROUP)]
                    nc.vector.scalar_tensor_tensor(prod[:, t, :] if n0 else columns, sig[:, t, :], 1.0,
                                                   stream[(part.group0 + 1) % 2][t][:, :], ALU.add, ALU.mult
                                                   ).then_inc(prod_ready, 1)
                if n0:
                    for t in range(TILES):
                        dve.wait_ge(prod_ready, i * 2 + (2 * n0 + t + 3))
                        columns = mixed[:, t, bass.ds(i * GROUP, GROUP)]
                        nc.vector.tensor_tensor(columns, columns, prod[:, t, :], ALU.add).then_inc(mixed_added, 1)

            nc.vector.tensor_copy(idx_acc, causal[:, :]).then_inc(idx_added, 1)
            with dve.Fori(0, IDX_TURNS) as i:
                for v in range(PAIR_UNITS):
                    split_unit(PP[0], i, v)
                    s, u = v // 3, v % 3
                    p = i * 4 + s
                    if u == 2:
                        dve.wait_ge(idx_relu_ready, p * 2 + 2)
                        dve.wait_ge(iw_fetched, p + 1)
                        for e in range(2):
                            dve.wait_ge(idx_added, p * 4 + (2 * e + 1))
                            for t, a, n in ((0, 0, P), (1, P, 2 * P)):
                                nc.vector.scalar_tensor_tensor(idx_acc[:, a:a + n], idx_relu[:, e, a:a + n],
                                                               iw_pair[:, t, e:e + 1], idx_acc[:, a:a + n],
                                                               ALU.mult, ALU.add).then_inc(idx_added, 1)
                gate_branch(PP[0], i, 0)
            dve.wait_ge(idx_added, 1 + 4 * IDX_HEADS // 2)
            dve.wait_ge(chi_ready, 1)
            nc.vector.tensor_tensor(clo[:, :, :], cT, chi[:, :, :].bitcast(F32), ALU.subtract).then_inc(clo_ready, 1)
            rounds = TOPK // 8 // (PP[0].turns - IDX_TURNS)

            def carry_wait():
                nc.vector.tensor_copy(wait_carrier, causal[:, 0:1])

            with dve.Fori(IDX_TURNS, PP[0].turns) as i:
                steps.enter(i - IDX_TURNS, 2 * rounds)
                for v in range(PAIR_UNITS):
                    split_unit(PP[0], i, v)
                    if v % 2 == 1 and v // 2 < rounds:
                        carry_wait()
                        for t, a, n in ((0, 0, P), (1, P, 2 * P)):
                            last = nc.vector.max(top8[:, t, :], idx_acc[:, a:a + n])
                        steps.step(last)
                        carry_wait()
                        for t, a, n in ((0, 0, P), (1, P, 2 * P)):
                            last = nc.vector.match_replace(idx_acc[:, a:a + n], top8[:, t, :], idx_acc[:, a:a + n],
                                                           TAKEN)
                        steps.step(last)
                gate_branch(PP[0], i, 0)
                steps.leave(PP[0].turns - IDX_TURNS)
            dve.wait_ge(prod_ready, 2 + 2 * PP[0].turns)

            def turn_y(n):
                for b in range(4):
                    dve.wait_ge(yhi_ready, 4 + 4 * n + b + 1)
                    nc.vector.tensor_tensor(ylo[:, 2 * b:2 * b + 2, :], M[b][:, :].rearrange("p (k s) -> p k s", k=2),
                                            yhi[:, 2 * b:2 * b + 2, :].bitcast(F32), ALU.subtract
                                            ).then_inc(ylo_ready, 1)

            turn_y(0)
            for g in range(2):
                split_unit(PV, 0, g)
            steps.step(nc.vector.tensor_scalar(select, idx_acc, 0.5 * (MASKED + TAKEN), MASKED, ALU.is_gt, ALU.mult))
            steps.step(nc.vector.tensor_tensor(select, select, causal[:, :], ALU.min))

            with dve.Fori(0, PP[1].turns) as i:
                steps.enter(i, 2 * 4)
                for v in range(PAIR_UNITS):
                    split_unit(PP[1], i, v)
                    s, u = v // 6, v % 6
                    h = i * 2 + s
                    if u == 1:
                        dve.wait_ge(dsa_logits, h + 1)
                        steps.step(nc.vector.scalar_tensor_tensor(dsa_s, M[1][:, 0:3 * P], DSA_LATENT ** -0.5, select,
                                                                  ALU.mult, ALU.add))
                        for t, a, n in ((0, 0, P), (1, P, 2 * P)):
                            nc.vector.tensor_reduce(dsa_negmax_c[:, t:t + 1], dsa_s[:, a:a + n], AX.X, ALU.max,
                                                    negate=True).then_inc(dsa_negmax, 1)
                    if u == 2:
                        dve.wait_ge(dsa_exp, h * 2 + 2)
                        steps.step(nc.vector.reciprocal(dsa_rsum_c, dsa_sum_c))
                        steps.step(nc.vector.tensor_scalar(dsa_rsum_c, dsa_rsum_c, 0.25, None, ALU.mult))
                        dve.wait_ge(dsa_tz, h + 1)
                        steps.step(nc.vector.scalar_tensor_tensor(dsa_sig, dsa_sig, 1.0,
                                                                  area0[:, :, bass.ds(h * P + 3 * WIDTH, P)],
                                                                  ALU.add, ALU.mult))
                    if u == 4:
                        dve.wait_ge(dsa_out, h + 1)
                        for t in range(TILES):
                            nc.vector.scalar_tensor_tensor(area0[:, t, bass.ds(h * P + 3 * WIDTH, P)],
                                                           M[3][:, t * P:(t + 1) * P], dsa_rsum_c[:, t:t + 1],
                                                           dsa_sig[:, t, :], ALU.mult, ALU.mult).then_inc(dsa_y, 1)
                gate_branch(PP[1], i, 4)
                steps.leave(PP[1].turns)
            turn_y(1)

            dve.wait_ge(mixed_added, 2 * PP[1].turns)
            with dve.Fori(0, PP[2].turns - 1) as i:
                for v in range(PAIR_UNITS):
                    split_unit(PP[2], i, v)
                gate_branch(PP[2], i, 8)
            def merged_low(b):
                dve.wait_ge(merged_hi, b + 1)
                nc.vector.tensor_tensor(xlo[:, 2 * b:2 * b + 2, :], M[b % 4][:, :].rearrange("p (k s) -> p k s", k=2),
                                        xhi[:, 2 * b:2 * b + 2, :].bitcast(F32), ALU.subtract).then_inc(merged_lo, 1)

            for v in range(PAIR_UNITS):
                split_unit(PP[2], PP[2].turns - 1, v)
                if v >= PAIR_UNITS - 2:
                    merged_low(2 * v - 20)
                    merged_low(2 * v - 19)
            gate_branch(PP[2], PP[2].turns - 1, 8)

            def take_out(g, t):
                columns = slice(g * GROUP, (g + 1) * GROUP)
                dve.wait_ge(out_ss, TILES * g + t + 1)
                nc.vector.tensor_tensor(out_sb[:, t, columns], stream[out_pair(g)][t][:, :], post_g[:, columns],
                                        ALU.mult).then_inc(out_taken, 1)

            dve.wait_ge(end_landed, 48)
            for g in range(ROW_OUT):
                for u in range(FULL_UNITS):
                    if g == 0 and u == 2:
                        for b in range(4, 8):
                            merged_low(b)
                    if PO.unit0 + g * FULL_UNITS + u + AHEAD < ALL_UNITS:
                        split_unit(PO, 0, g * FULL_UNITS + u)
                if g < ROW_OUT - 1:
                    for t in range(TILES):
                        take_out(g, t)
            take_out(ROW_OUT - 1, 0)
            dve.wait_ge(out_ss, TILES * ROW_OUT)
            steps.step(nc.vector.tensor_reduce(rstdo, sso, AX.X, ALU.add))
            nc.vector.tensor_scalar(rstdo, rstdo, 1.0 / D_MODEL, EPS, ALU.mult, ALU.add).then_inc(out_ms, 1)
            take_out(ROW_OUT - 1, 1)
            dve.wait_ge(out_std, 1)
            nc.vector.reciprocal(rstdo, rstdo).then_inc(rstdo_ready, 1)
            dve.wait_ge(rstdo_ready, 1)
            dve.wait_ge(out_taken, TILES * ROW_OUT)
            for t, columns in FINAL_DVE:
                to = out_sb[:, t, columns]
                nc.vector.scalar_tensor_tensor(to, to, rstdo[:, t:t + 1], x_again[:, t, columns],
                                               ALU.mult, ALU.add).then_inc(y_dve, 1)

        @block.tensor
        def _(pe):
            def multiply(part, i, k, u, units, bank_pair, left_hi, left_lo, width=GROUP):
                slot = (part.unit0 + k) % RING
                pe.wait_ge(wlo_ready, part.unit(i, k) + 1)
                for j in range(UNIT_KT):
                    kt = UNIT_KT * u + j
                    first, final = kt == 0, kt == UNIT_KT * units - 1
                    for t in range(TILES):
                        to = stream[bank_pair][t][:, 0:width]
                        tokens = slice(t * P, (t + 1) * P)
                        high, low = whi[:, slot, j, 0:width], wlo[:, slot, j, 0:width]
                        nc.tensor.matmul(to, left_hi[:, kt, tokens], high, start=first, stop=False)
                        nc.tensor.matmul(to, left_hi[:, kt, tokens], low, start=False, stop=False)
                        last = nc.tensor.matmul(to, left_lo[:, kt, tokens], high, start=False, stop=final)
                last.then_inc(units_done, 1)

            def open_banks(part, i, k):
                pe.wait_ge(banks_free, i * (2 * part.groups) + (2 * (part.group0 + k) + 2))

            pe.wait_ge(masks_ready, 1)
            pe.wait_ge(rows_landed, 3 * 16)
            nc.tensor.transpose(M[0][:, 0:56], rows[:, :], ident[0:56, 0:56]).then_inc(cols_turned, 1)

            def turn_x(b):
                if b % 2 == 0:
                    pe.wait_ge(x_landed[b // 2], 16)
                if b == 4:
                    pe.wait_ge(cols_ready, 1)
                for j in range(2):
                    for t in range(TILES):
                        kt = 2 * b + j
                        last = nc.tensor.transpose(banks[b][:, j * SEQ + t * P:j * SEQ + (t + 1) * P],
                                                   x_sb[:, t, kt * P:(kt + 1) * P], ident[:, :])
                last.then_inc(x_turned, 1)

            for b in range(8):
                turn_x(b)
            pe.wait_ge(xlo_ready, 4)
            for u in range(FULL_UNITS):
                pe.wait_ge(xlo_ready, UNIT_KT * (u + 1))
                multiply(PS, 0, u, u, FULL_UNITS, 0, xhi, xlo, SMALL)
            with pe.Fori(0, PA.turns) as i:
                for g in range(2):
                    open_banks(PA, i, g)
                    for u in range(FULL_UNITS):
                        multiply(PA, i, g * FULL_UNITS + u, u, FULL_UNITS, (PA.group0 + g) % 2, xhi, xlo)

            pe.wait_ge(kv_normed, 7)
            for c in range(2):
                for t in range(TILES):
                    last = nc.tensor.transpose(M[0][:, c * SEQ + t * P:c * SEQ + (t + 1) * P],
                                               c_sb[:, t, c * P:(c + 1) * P], ident[:, :])
            last.then_inc(prep_turned, 1)
            for t in range(TILES):
                last = nc.tensor.transpose(M[1][:, t * P:(t + 1) * P], ik2[:, t, :], ident[:, :])
            last.then_inc(prep_turned, 1)
            for e in range(2):
                for t in range(TILES):
                    last = nc.tensor.transpose(M[2][0:ML_HEADS, e * SEQ + t * P:e * SEQ + (t + 1) * P],
                                               gate_in[:, t, e * ML_HEADS:(e + 1) * ML_HEADS], ident[:, :])
            last.then_inc(prep_turned, 1)

            with pe.Fori(0, PB.turns) as i:
                for s in range(2):
                    h = i * 2 + s
                    open_banks(PB, i, s)
                    for u in range(FULL_UNITS):
                        multiply(PB, i, s * FULL_UNITS + u, u, FULL_UNITS, (PB.group0 + s) % 2, xhi, xlo)
                        if u == 1:
                            pe.wait_ge(prep_copied, 2)
                            pe.wait_ge(da_fetched, h * 2 + 2)
                            pe.wait_ge(da_o_out, h + 1)
                            for n, of in enumerate((da_q, da_k)):
                                for t in range(TILES):
                                    last = nc.tensor.transpose(M[0][:, n * SEQ + t * P:n * SEQ + (t + 1) * P],
                                                               of[:, t, :], ident[:, :])
                            last.then_inc(da_qkT_psum, 1)
                        if u == 2:
                            pe.wait_ge(da_qkT_ready, h + 1)
                            pe.wait_ge(row_act, 3)
                            for c in range(2):
                                d = slice(c * DA_DIM, (c + 1) * DA_DIM)
                                nc.tensor.matmul(M[1 + c][:, 0:P], da_qkT[d, 0, 0:P], da_qkT[d, 1, 0:P],
                                                 start=True, stop=True)
                                last = nc.tensor.matmul(M[1 + c][:, P:3 * P], da_qkT[d, 0, P:], da_qkT[d, 1, :],
                                                        start=True, stop=True)
                            last.then_inc(da_scores, 1)
                        if u == 6:
                            pe.wait_ge(da_attn, h * 2 + 2)
                            for b in range(3):
                                last = nc.tensor.transpose(M[3][:, b * P:(b + 1) * P], da_a[:, b * P:(b + 1) * P],
                                                           ident[:, :])
                            last.then_inc(da_aT_psum, 1)
                        if u == 7:
                            pe.wait_ge(da_v_fetched, h + 1)
                            pe.wait_ge(da_aT_ready, h + 1)
                            nc.tensor.matmul(M[0][:, 0:P], da_aT[:, 0:P], da_v[:, 0, :], start=True, stop=True)
                            for t in range(TILES):
                                last = nc.tensor.matmul(M[0][:, P:2 * P], da_aT[:, (1 + t) * P:(2 + t) * P],
                                                        da_v[:, t, :], start=(t == 0), stop=(t == 1))
                            last.then_inc(da_av, 1)

            for n in range(2):
                for e in range(2):
                    last = nc.tensor.matmul(M[n + 1][:, e * SEQ:(e + 1) * SEQ], selrow[:, 2 * n + e, :], row_negM,
                                            start=True, stop=True)
                last.then_inc(rows_turned, 1)
            for n, row in enumerate((row_a, row_c)):
                for t in range(TILES):
                    last = nc.tensor.transpose(M[3][:, 8 * n + ML_HEADS * t:8 * n + ML_HEADS * (t + 1)],
                                               row[:, t * P:(t + 1) * P], ident[0:ML_HEADS, 0:ML_HEADS])
            last.then_inc(rows_turned, 1)

            with pe.Fori(0, PC.turns) as i:
                for v in range(2 * FULL_UNITS):
                    g, u = v // FULL_UNITS, v % FULL_UNITS
                    if u == 0:
                        open_banks(PC, i, g)
                    multiply(PC, i, v, u, FULL_UNITS, (PC.group0 + g) % 2, xhi, xlo)
                    if v == 1:
                        pe.wait_ge(ml_fetched, i * 6 + 2)
                        for a in range(2):
                            for t in range(TILES):
                                last = nc.tensor.transpose(M[0][:, a * SEQ + t * P:a * SEQ + (t + 1) * P],
                                                           ml_qk[:, a, t, :], ident[:, :])
                        last.then_inc(ml_T_psum, 1)
                    if v == 3:
                        pe.wait_ge(ya_fetched, i + 1)
                        pe.wait_ge(rows_copied, 4)
                        pe.wait_ge(ml_h_ready, i * 2 + 2)
                        for j in range(2):
                            for t in range(TILES):
                                last = nc.tensor.transpose(M[2][:, j * SEQ + t * P:j * SEQ + (t + 1) * P],
                                                           ya_blk[:, t, j * P:(j + 1) * P], ident[:, :])
                        last.then_inc(ya_psum, 1)
                    if v == 7:
                        pe.wait_ge(ml_cT_ready, i + 1)
                        nc.tensor.matmul(M[1][:, 0:SEQ], ml_cT[:, 1, 0:P], ml_cT[:, 0, :], start=True, stop=True)
                        nc.tensor.matmul(M[1][:, SEQ:3 * P], ml_cT[:, 1, P:], ml_cT[:, 0, P:], start=True, stop=True
                                         ).then_inc(ml_scores, 1)
                    if v == 10:
                        pe.wait_ge(ml_w_ready, i + 1)
                        pe.wait_ge(ml_fetched, i * 6 + 3)
                        pe.wait_ge(ylo_ready, i + 2)
                        n = ML_V + 1
                        nc.tensor.matmul(M[2][:, 0:n], ml_w[:, 0:P], ml_v[:, 0, :], start=True, stop=True)
                        nc.tensor.matmul(M[3][:, 0:n], ml_w[:, P:2 * P], ml_v[:, 0, :], start=True, stop=False)
                        nc.tensor.matmul(M[3][:, 0:n], ml_w[:, 2 * P:], ml_v[:, 1, :], start=False, stop=True
                                         ).then_inc(ml_num, 1)

            def gate_units(part, i, v, n0):
                if v == 0:
                    pe.wait_ge(gate_tanh, i * 2 + (2 * n0 + 2))
                multiply(part, i, v, v, FULL_UNITS, part.group0 % 2, xhi, xlo)

            def branch_units(part, i, v, n0, ylo_count):
                if v == FULL_UNITS:
                    pe.wait_ge(prod_ready, i * 2 + (2 * n0 + 2))
                    pe.wait_ge(banks_free, 4 + 2 * PP[0].group0)
                    pe.wait_ge(ylo_ready, ylo_count)
                multiply(part, i, v, v - FULL_UNITS, HALF_UNITS, (part.group0 + 1) % 2, yhi, ylo)

            def turn_y(area):
                for b in range(4):
                    for j in range(2):
                        for t in range(TILES):
                            kt = 2 * b + j
                            last = nc.tensor.transpose(M[b][:, j * SEQ + t * P:j * SEQ + (t + 1) * P],
                                                       area[:, t, 3 * WIDTH + kt * P:3 * WIDTH + (kt + 1) * P],
                                                       ident[:, :])
                    last.then_inc(y_psum, 1)

            pe.wait_ge(banks_free, 4 + 2 * (PP[0].group0 - 1))
            with pe.Fori(0, IDX_TURNS) as i:
                for v in range(PAIR_UNITS):
                    s, u = v // 3, v % 3
                    p = i * 4 + s
                    if v < FULL_UNITS:
                        gate_units(PP[0], i, v, 0)
                    else:
                        branch_units(PP[0], i, v, 0, 5)
                    if u == 1:
                        pe.wait_ge(idx_fetched, p + 1)
                        for t in range(TILES):
                            last = nc.tensor.transpose(M[0][:, t * P:(t + 1) * P], iq_sb[:, t, :], ident[:, :])
                        last.then_inc(idx_T_psum, 1)
                    if u == 2:
                        pe.wait_ge(iqT_ready, p + 1)
                        for e in range(2):
                            d = slice(e * IDX_DIM, (e + 1) * IDX_DIM)
                            nc.tensor.matmul(M[1 + e][:, 0:P], iqT[d, 0:P], ikT[d, 0:P], start=True, stop=True)
                            last = nc.tensor.matmul(M[1 + e][:, P:3 * P], iqT[d, P:], ikT[d, :], start=True, stop=True)
                        last.then_inc(idx_scores, 1)
            with pe.Fori(IDX_TURNS, PP[0].turns) as i:
                for v in range(PAIR_UNITS):
                    if v < FULL_UNITS:
                        gate_units(PP[0], i, v, 0)
                    else:
                        branch_units(PP[0], i, v, 0, 5)
            pe.wait_ge(idx_relu_ready, IDX_HEADS)
            turn_y(area1)

            pe.wait_ge(clo_ready, 1)
            pe.wait_ge(gate_tanh, 2 + 2 * PP[0].turns)
            multiply(PV, 0, 0, 0, 1, PV.group0 % 2, chi, clo)
            pe.wait_ge(prod_ready, 2 + 2 * PP[0].turns)
            multiply(PV, 0, 1, 0, 1, (PV.group0 + 1) % 2, chi, clo)
            pe.wait_ge(v_taken, 2)

            with pe.Fori(0, PP[1].turns) as i:
                for v in range(PAIR_UNITS):
                    s, u = v // 6, v % 6
                    h = i * 2 + s
                    if v < FULL_UNITS:
                        gate_units(PP[1], i, v, 4)
                    else:
                        branch_units(PP[1], i, v, 4, 9)
                    if u == 0:
                        pe.wait_ge(dsa_fetched, h + 1)
                        pe.wait_ge(ylo_ready, 9)
                        for c in range(2):
                            for t in range(TILES):
                                last = nc.tensor.transpose(M[0][:, c * SEQ + t * P:c * SEQ + (t + 1) * P],
                                                           dsa_q[:, t, c * P:(c + 1) * P], ident[:, :])
                        last.then_inc(dsa_T_psum, 1)
                    if u == 1:
                        pe.wait_ge(dsa_qT_ready, h + 1)
                        for t, a, n in ((0, 0, P), (1, P, 2 * P)):
                            for c in range(2):
                                last = nc.tensor.matmul(M[1][:, a:a + n], dsa_qT[:, c, t * P:(t + 1) * P],
                                                        cT[:, c, 0:n], start=(c == 0), stop=(c == 1))
                        last.then_inc(dsa_logits, 1)
                    if u == 3:
                        pe.wait_ge(dsa_exp, h * 2 + 2)
                        for b in range(3):
                            last = nc.tensor.transpose(M[2][:, b * P:(b + 1) * P], dsa_s[:, b * P:(b + 1) * P],
                                                       ident[:, :])
                        last.then_inc(dsa_pT_psum, 1)
                    if u == 4:
                        pe.wait_ge(v_taken, 4)
                        pe.wait_ge(dsa_pT_ready, h + 1)
                        pe.wait_ge(dsa_y, h * 2 + 1)
                        of_head = bass.ds(h * P, P)
                        nc.tensor.matmul(M[3][:, 0:P], dsa_pT[:, 0:P], dsa_v[:, 0, of_head], start=True, stop=True)
                        for t in range(TILES):
                            last = nc.tensor.matmul(M[3][:, P:2 * P], dsa_pT[:, (1 + t) * P:(2 + t) * P],
                                                    dsa_v[:, t, of_head], start=(t == 0), stop=(t == 1))
                        last.then_inc(dsa_out, 1)
            pe.wait_ge(dsa_y, 1 + TILES * DSA_HEADS)
            turn_y(area0)

            def turn_merged(b):
                for j in range(2):
                    for t in range(TILES):
                        kt = 2 * b + j
                        last = nc.tensor.transpose(M[b % 4][:, j * SEQ + t * P:j * SEQ + (t + 1) * P],
                                                   mixed[:, t, kt * P:(kt + 1) * P], ident[:, :])
                last.then_inc(merged_psum, 1)

            with pe.Fori(0, PP[2].turns - 1) as i:
                for v in range(PAIR_UNITS):
                    if v < FULL_UNITS:
                        gate_units(PP[2], i, v, 8)
                    else:
                        branch_units(PP[2], i, v, 8, 13)
            for v in range(PAIR_UNITS):
                if v < FULL_UNITS:
                    gate_units(PP[2], PP[2].turns - 1, v, 8)
                else:
                    branch_units(PP[2], PP[2].turns - 1, v, 8, 13)
                if v == PAIR_UNITS - 3:
                    pe.wait_ge(mixed_added, 2 * (4 + 2))
                    for b in range(4):
                        turn_merged(b)

            for g in range(ROW_OUT):
                if g == 0:
                    pe.wait_ge(gate_tanh, 2 + 2 * 4 * BRANCHES)
                elif g == 1:
                    pe.wait_ge(prod_ready, 2 + 2 * 4 * BRANCHES)
                else:
                    pe.wait_ge(out_taken, TILES * (g - 1))
                    pe.wait_ge(out_ss, TILES * (g - 1))
                for u in range(FULL_UNITS):
                    if g == 0:
                        pe.wait_ge(merged_lo, u + 1)
                    multiply(PO, 0, g * FULL_UNITS + u, u, FULL_UNITS, out_pair(g), xhi, xlo)
                    if g == 0 and u == 1:
                        pe.wait_ge(mixed_added, 2 * 4 * (BRANCHES - 1))
                        pe.wait_ge(merged_lo, 4)
                        for b in range(4, 8):
                            turn_merged(b)


_INS = ["x", "pre_norm_g", "w_in", "da_lambda", "da_norm_g", "ml_conv_w", "ml_conv_b", "ml_gate_b", "ml_norm_g",
        "dsa_kv_norm_g", "dsa_ik_norm_g", "dsa_w_uv", "w_branch", "w_out", "post_norm_g"]


def kernel(**inputs):
    import numpy as np
    import concourse.bacc as bacc
    from concourse.bass_utils import run_bass_kernel_spmd

    nc = bacc.Bacc("TRN2", target_bir_lowering=False, num_devices=1)
    arrays, args = {}, []
    for name in _INS:
        a = np.ascontiguousarray(inputs[name])
        arrays[f"in_{name}"] = a
        args.append(nc.dram_tensor(f"in_{name}", a.shape, mybir.dt.from_np(a.dtype), kind="ExternalInput").ap())
    out = nc.dram_tensor("out_0", (1, SEQ, D_MODEL), F32, kind="ExternalOutput").ap()
    build(nc, *args, out)
    result = run_bass_kernel_spmd(nc, [arrays], core_ids=[0])
    return result.results[0]["out_0"]
```
